# Optimizing a Trainium2 kernel written in Bass

```python
import math
import jax, jax.numpy as jnp
from jax import lax
import numpy as np

D_MODEL = 1024
BATCH = 1
SEQ = 256
DEPTH = 2

GRID_W = 64
CTX_LEN = 256
N_HEADS = 8
Q_LORA = 256
KV_LORA = 128
QK_NOPE = 64
QK_ROPE = 32
V_HEAD = 64
ATT_WIDTH = N_HEADS * V_HEAD
ATT_SCALE = (QK_NOPE + QK_ROPE) ** -0.5
ROPE_BASE = 10000.0
Q_BLOCK = 128
FOURIER_WIDTH = 256
POOL_WINDOWS = (2, 4, 8, 16)
POOL_GROUP = 64
POOL_WIDTH = POOL_GROUP * len(POOL_WINDOWS)
N_BRANCH = 3
IN_WIDTH = Q_LORA + KV_LORA + QK_ROPE + FOURIER_WIDTH + POOL_WIDTH + N_BRANCH * D_MODEL
SPLITS = (Q_LORA, Q_LORA + KV_LORA, Q_LORA + KV_LORA + QK_ROPE,
          Q_LORA + KV_LORA + QK_ROPE + FOURIER_WIDTH,
          Q_LORA + KV_LORA + QK_ROPE + FOURIER_WIDTH + POOL_WIDTH)
PEER_HEADS = 8
N_KEYS = 128
N_EXPERTS = N_KEYS * N_KEYS
PEER_QDIM = 256
PEER_TOPK = 16
TOKEN_BLOCK = 128
EPS = 1e-6


def _rmsnorm(x, g):
    xf = x.astype(jnp.float32)
    y = xf * lax.rsqrt(jnp.mean(xf * xf, axis=-1, keepdims=True) + EPS)
    return (y * g.astype(jnp.float32)).astype(x.dtype)

def _modulation(cvec, w_mod, b_mod):
    m = jax.nn.silu(cvec) @ w_mod + b_mod
    return jnp.split(m[:, None, :], 6, axis=-1)

def _modulate(x, g, shift, scale):
    return _rmsnorm(x, g) * (1 + scale) + shift

def _axial_angles(L):
    rows = L // GRID_W
    r, cl = jnp.meshgrid(jnp.arange(rows, dtype=jnp.float32),
                         jnp.arange(GRID_W, dtype=jnp.float32), indexing="ij")
    half = QK_ROPE // 2
    inv_freq = ROPE_BASE ** (-jnp.arange(0, half, 2, dtype=jnp.float32) / half)
    ang_r = r.reshape(L, 1, 1) * inv_freq
    ang_c = cl.reshape(L, 1, 1) * inv_freq
    return ang_r, ang_c

def _rotate_half(x, ang):
    x1, x2 = jnp.split(x.astype(jnp.float32), 2, axis=-1)
    cos, sin = jnp.cos(ang), jnp.sin(ang)
    return jnp.concatenate([x1 * cos - x2 * sin, x1 * sin + x2 * cos], axis=-1)

def _rope_2d(x, ang):
    ang_r, ang_c = ang
    xr, xc = jnp.split(x, 2, axis=-1)
    return jnp.concatenate([_rotate_half(xr, ang_r), _rotate_half(xc, ang_c)], axis=-1).astype(x.dtype)

def _mla_q(cq, lp, ang):
    B, L, _ = cq.shape
    q = (_rmsnorm(cq, lp["q_norm_g"]) @ lp["w_uq"]).reshape(B, L, N_HEADS, QK_NOPE + QK_ROPE)
    q_nope, q_rope = q[..., :QK_NOPE], q[..., QK_NOPE:]
    if ang is not None:
        q_rope = _rope_2d(q_rope, ang)
    return jnp.concatenate([q_nope, q_rope], axis=-1)

def _mla_kv(ckv, kr, lp, ang):
    B, L, _ = ckv.shape
    kv = (_rmsnorm(ckv, lp["kv_norm_g"]) @ lp["w_ukv"]).reshape(B, L, N_HEADS, QK_NOPE + V_HEAD)
    k_nope, v = kv[..., :QK_NOPE], kv[..., QK_NOPE:]
    k_rope = kr[:, :, None, :]
    if ang is not None:
        k_rope = _rope_2d(k_rope, ang)
    k = jnp.concatenate([k_nope, jnp.broadcast_to(k_rope, (B, L, N_HEADS, QK_ROPE))], axis=-1)
    return k, v

def _attend(q, k, v):
    s = jnp.einsum("bqhd,bkhd->bhqk", q, k, preferred_element_type=jnp.float32) * ATT_SCALE
    p = jax.nn.softmax(s, axis=-1).astype(v.dtype)
    return jnp.einsum("bhqk,bkhd->bqhd", p, v)

def _latent_attention(q, k, v, kv_ctx):
    k_ctx, v_ctx = kv_ctx
    k_all = jnp.concatenate([k_ctx, k], axis=1)
    v_all = jnp.concatenate([v_ctx, v], axis=1)
    B, L, H, Dq = q.shape
    nb = L // Q_BLOCK
    qb = jnp.moveaxis(q.reshape(B, nb, Q_BLOCK, H, Dq), 1, 0)
    o = lax.map(lambda qq: _attend(qq, k_all, v_all), qb)
    return jnp.moveaxis(o, 0, 1).reshape(B, L, ATT_WIDTH)

def _fourier_mix(z):
    zf = z.astype(jnp.float32)
    return jnp.real(jnp.fft.fft2(zf, axes=(1, 2), norm="ortho")).astype(z.dtype)

def _pool_mix(z, w_grp, pool_scale):
    B, L, _ = z.shape
    zf = z.astype(jnp.float32)
    cs = jnp.concatenate([jnp.zeros((B, 1, POOL_WIDTH), jnp.float32), jnp.cumsum(zf, axis=1)], axis=1)
    t = jnp.arange(L)
    outs = []
    for gi, w in enumerate(POOL_WINDOWS):
        lo = jnp.clip(t - w // 2, 0, L)
        hi = jnp.clip(t - w // 2 + w, 0, L)
        seg = cs[:, :, gi * POOL_GROUP:(gi + 1) * POOL_GROUP]
        cnt = (hi - lo).astype(jnp.float32)[None, :, None]
        outs.append((seg[:, hi] - seg[:, lo]) / cnt - zf[:, :, gi * POOL_GROUP:(gi + 1) * POOL_GROUP])
    pooled = jnp.concatenate(outs, axis=-1).astype(z.dtype).reshape(B, L, len(POOL_WINDOWS), POOL_GROUP)
    y = jnp.einsum("blgc,gcd->blgd", pooled, w_grp).reshape(B, L, POOL_WIDTH)
    return y * pool_scale

def _token_mix(h, lp, ang, kv_ctx):
    B, L, _ = h.shape
    z = h @ lp["w_in"]
    cq, ckv, kr, zf, zp, zg = jnp.split(z, SPLITS, axis=-1)
    q = _mla_q(cq, lp, ang)
    k, v = _mla_kv(ckv, kr, lp, ang)
    if kv_ctx is None:
        att = _attend(q, k, v).reshape(B, L, ATT_WIDTH)
    else:
        att = _latent_attention(q, k, v, kv_ctx)
    y_a = att @ lp["w_oa"]
    y_b = _fourier_mix(zf) @ lp["w_ob"]
    y_c = _pool_mix(zp, lp["w_grp"], lp["pool_scale"]) @ lp["w_oc"]
    g = jax.nn.sigmoid((zg + lp["b_gate"]).astype(jnp.float32)).astype(h.dtype)
    g_a, g_b, g_c = jnp.split(g, N_BRANCH, axis=-1)
    return (g_a * y_a + g_b * y_b + g_c * y_c) @ lp["w_out"], (k, v)

def _ctx_keys_values(hc, lp):
    z = hc @ lp["w_in"][:, Q_LORA:Q_LORA + KV_LORA + QK_ROPE]
    ckv, kr = z[..., :KV_LORA], z[..., KV_LORA:]
    return _mla_kv(ckv, kr, lp, None)

def _peer(h, w_pq, peer_keys, peer_down, peer_up):
    B, L, D = h.shape
    q = (h @ w_pq).reshape(B, L, PEER_HEADS, 2, PEER_QDIM // 2)
    s = jnp.einsum("blhpd,hpkd->blhpk", q, peer_keys, preferred_element_type=jnp.float32)
    sv, si = lax.top_k(s, PEER_TOPK)
    cand = (sv[..., 0, :, None] + sv[..., 1, None, :]).reshape(B, L, PEER_HEADS, PEER_TOPK * PEER_TOPK)
    cidx = (si[..., 0, :, None] * N_KEYS + si[..., 1, None, :]).reshape(B, L, PEER_HEADS, PEER_TOPK * PEER_TOPK)
    top_s, pos = lax.top_k(cand, PEER_TOPK)
    eidx = jnp.take_along_axis(cidx, pos, axis=-1)
    gate = jax.nn.softmax(top_s, axis=-1)
    T = B * L
    nb = T // TOKEN_BLOCK
    hb = h.reshape(nb, TOKEN_BLOCK, D)
    eb = eidx.reshape(nb, TOKEN_BLOCK, PEER_HEADS * PEER_TOPK)
    gb = gate.reshape(nb, TOKEN_BLOCK, PEER_HEADS * PEER_TOPK)

    def one(args):
        hh, ee, gg = args
        a = jnp.einsum("tkd,td->tk", peer_down[ee], hh, preferred_element_type=jnp.float32)
        act = (gg * jax.nn.gelu(a)).astype(hh.dtype)
        return jnp.einsum("tk,tkd->td", act, peer_up[ee])

    return lax.map(one, (hb, eb, gb)).reshape(B, L, D)

def first_inputs(seed: int = 0) -> dict:
    key = jax.random.key(seed)
    ks = jax.random.split(key, 25)
    D = D_MODEL

    def n(k, shape, s):
        return jax.random.normal(k, shape, jnp.float32) * s

    return {
        "x": n(ks[0], (BATCH, SEQ, D), 1.0),
        "c": n(ks[1], (BATCH, D), 1.0),
        "ctx": n(ks[2], (BATCH, CTX_LEN, D), 1.0),
        "c_ctx": n(ks[3], (D,), 1.0),
        "w_mod": n(ks[4], (DEPTH, D, 6 * D), 0.5 * D ** -0.5),
        "b_mod": n(ks[5], (DEPTH, 6 * D), 0.01),
        "norm1_g": 1.0 + n(ks[6], (DEPTH, D), 0.02),
        "norm2_g": 1.0 + n(ks[7], (DEPTH, D), 0.02),
        "w_in": n(ks[8], (DEPTH, D, IN_WIDTH), D ** -0.5),
        "b_gate": n(ks[9], (DEPTH, N_BRANCH * D), 0.01),
        "q_norm_g": 1.0 + n(ks[10], (DEPTH, Q_LORA), 0.02),
        "w_uq": n(ks[11], (DEPTH, Q_LORA, N_HEADS * (QK_NOPE + QK_ROPE)), Q_LORA ** -0.5),
        "kv_norm_g": 1.0 + n(ks[12], (DEPTH, KV_LORA), 0.02),
        "w_ukv": n(ks[13], (DEPTH, KV_LORA, N_HEADS * (QK_NOPE + V_HEAD)), KV_LORA ** -0.5),
        "w_oa": n(ks[14], (DEPTH, ATT_WIDTH, D), ATT_WIDTH ** -0.5),
        "w_ob": n(ks[15], (DEPTH, FOURIER_WIDTH, D), FOURIER_WIDTH ** -0.5),
        "w_grp": n(ks[16], (DEPTH, len(POOL_WINDOWS), POOL_GROUP, POOL_GROUP), POOL_GROUP ** -0.5),
        "pool_scale": 1.0 + n(ks[17], (DEPTH, POOL_WIDTH), 0.02),
        "w_oc": n(ks[18], (DEPTH, POOL_WIDTH, D), POOL_WIDTH ** -0.5),
        "w_out": n(ks[19], (DEPTH, D, D), D ** -0.5),
        "w_pq": n(ks[20], (DEPTH, D, PEER_HEADS * PEER_QDIM), D ** -0.5),
        "peer_keys": n(ks[21], (DEPTH, PEER_HEADS, 2, N_KEYS, PEER_QDIM // 2), (PEER_QDIM // 2) ** -0.5),
        "peer_down": n(ks[22], (DEPTH, N_EXPERTS, D), D ** -0.5),
        "peer_up": n(ks[23], (DEPTH, N_EXPERTS, D), PEER_HEADS ** -0.5),
        "final_g": 1.0 + n(ks[24], (D,), 0.02),
    }

def first_block(x, c, ctx, c_ctx, w_mod, b_mod, norm1_g, norm2_g, w_in, b_gate, q_norm_g, w_uq,
              kv_norm_g, w_ukv, w_oa, w_ob, w_grp, pool_scale, w_oc, w_out, w_pq, peer_keys,
              peer_down, peer_up, final_g):
    L = x.shape[1]
    ang = _axial_angles(L)
    for l in range(DEPTH):
        last = l == DEPTH - 1
        lp = {"w_in": w_in[l], "b_gate": b_gate[l], "q_norm_g": q_norm_g[l], "w_uq": w_uq[l],
              "kv_norm_g": kv_norm_g[l], "w_ukv": w_ukv[l], "w_oa": w_oa[l], "w_ob": w_ob[l],
              "w_grp": w_grp[l], "pool_scale": pool_scale[l], "w_oc": w_oc[l], "w_out": w_out[l]}
        m_x = _modulation(c, w_mod[l], b_mod[l])
        m_c = _modulation(c_ctx[None, :], w_mod[l], b_mod[l])
        h = _modulate(x, norm1_g[l], m_x[0], m_x[1])
        hc = _modulate(ctx, norm1_g[l], m_c[0], m_c[1])
        if last:
            kv_c = _ctx_keys_values(hc, lp)
        else:
            mix_c, kv_c = _token_mix(hc, lp, None, None)
        mix_x, _ = _token_mix(h, lp, ang, kv_c)
        x = x + m_x[2] * mix_x
        h2 = _modulate(x, norm2_g[l], m_x[3], m_x[4])
        x = x + m_x[5] * _peer(h2, w_pq[l], peer_keys[l], peer_down[l], peer_up[l])
        if not last:
            ctx = ctx + m_c[2] * mix_c
            hc2 = _modulate(ctx, norm2_g[l], m_c[3], m_c[4])
            ctx = ctx + m_c[5] * _peer(hc2, w_pq[l], peer_keys[l], peer_down[l], peer_up[l])
    return _rmsnorm(x, final_g)


N_A_LAYERS = DEPTH // 2
N_B_LAYERS = DEPTH - N_A_LAYERS
D_FF = ((8 * D_MODEL // 3) + 127) // 128 * 128
CONV_WIDTH = 31
HEAD_DIM = 128
N_HEADS_2 = D_MODEL // HEAD_DIM
MOBA_BLOCK = 256
MOBA_TOPK = 3
Q_CHUNK = 32
RMS_EPS = 1e-6
LN_EPS = 1e-5
MACARON_WEIGHT = 0.5
NEG_INF = -1e30


def rms_norm(x, g):
    x32 = x.astype(jnp.float32)
    y = x32 * lax.rsqrt(jnp.mean(x32 * x32, axis=-1, keepdims=True) + RMS_EPS)
    return (y * g.astype(jnp.float32)).astype(x.dtype)

def swiglu_ffn(h, w_gate_up, w_down):
    gate, up = jnp.split(h @ w_gate_up, 2, axis=-1)
    return (jax.nn.silu(gate) * up) @ w_down

def conformer_conv(h, w_in, b_in, w_dw, b_dw, ln_g, ln_b, w_out, b_out):
    a, g = jnp.split(h @ w_in + b_in, 2, axis=-1)
    u = a * jax.nn.sigmoid(g)
    u = lax.conv_general_dilated(
        u, w_dw[:, None, :].astype(u.dtype), window_strides=(1,),
        padding=[(CONV_WIDTH - 1, 0)],
        dimension_numbers=('NWC', 'WIO', 'NWC'),
        feature_group_count=D_MODEL) + b_dw
    u32 = u.astype(jnp.float32)
    mu = jnp.mean(u32, axis=-1, keepdims=True)
    var = jnp.mean(jnp.square(u32 - mu), axis=-1, keepdims=True)
    u = ((u32 - mu) * lax.rsqrt(var + LN_EPS) * ln_g.astype(jnp.float32)
         + ln_b.astype(jnp.float32)).astype(h.dtype)
    return jax.nn.silu(u) @ w_out + b_out

def alibi_slopes():
    return jnp.asarray(2.0 ** (-8.0 * (np.arange(N_HEADS_2) + 1) / N_HEADS_2), dtype=jnp.float32)

def shared_kv(x, g_kv, w_kv):
    B, T, _ = x.shape
    k, v = jnp.split(rms_norm(x, g_kv) @ w_kv, 2, axis=-1)
    nb = -(-T // MOBA_BLOCK)
    pad = nb * MOBA_BLOCK - T

    def to_blocks(z):
        z = jnp.pad(z, ((0, 0), (0, pad), (0, 0)))
        return z.reshape(B, nb, MOBA_BLOCK, N_HEADS_2, HEAD_DIM).transpose(0, 3, 1, 2, 4)

    kb = to_blocks(k)
    vb = to_blocks(v)
    k_means = jnp.mean(kb.astype(jnp.float32), axis=3).astype(kb.dtype)
    return kb, vb, k_means

def moba_attention(q, kb, vb, k_means, slopes):
    B, T = q.shape[0], q.shape[1]
    nb = kb.shape[2]
    ksel = min(MOBA_TOPK, nb)
    q = (q * (HEAD_DIM ** -0.5)).transpose(0, 2, 1, 3)
    qblk = jnp.arange(T) // MOBA_BLOCK
    gate = jnp.einsum('bhtd,bhnd->bhtn', q, k_means, preferred_element_type=jnp.float32)
    past = jnp.arange(nb)[None, :] < qblk[:, None]
    gate = jnp.where(past, gate, NEG_INF)
    _, sel = lax.top_k(gate, ksel)

    nc = T // Q_CHUNK
    q_c = q.reshape(B, N_HEADS_2, nc, Q_CHUNK, HEAD_DIM).transpose(2, 0, 1, 3, 4)
    sel_c = sel.reshape(B, N_HEADS_2, nc, Q_CHUNK, ksel).transpose(2, 0, 1, 3, 4)
    b_ix = jnp.arange(B)[:, None, None, None]
    h_ix = jnp.arange(N_HEADS_2)[None, :, None, None]
    slopes5 = slopes[:, None, None, None]
    slopes4 = slopes[:, None, None]

    def chunk(args):
        c, qq, ss = args
        t = c * Q_CHUNK + jnp.arange(Q_CHUNK)
        own = (c * Q_CHUNK) // MOBA_BLOCK
        valid = jnp.arange(ksel)[None, :] < (t // MOBA_BLOCK)[:, None]
        kg = kb[b_ix, h_ix, ss]
        vg = vb[b_ix, h_ix, ss]
        s_sel = jnp.einsum('bhqd,bhqkpd->bhqkp', qq, kg, preferred_element_type=jnp.float32)
        key_pos = ss[..., None] * MOBA_BLOCK + jnp.arange(MOBA_BLOCK)
        dist = (t[:, None, None] - key_pos).astype(jnp.float32)
        s_sel = jnp.where(valid[:, :, None], s_sel - slopes5 * dist, NEG_INF)
        s_sel = s_sel.reshape(B, N_HEADS_2, Q_CHUNK, ksel * MOBA_BLOCK)
        k_own = lax.dynamic_index_in_dim(kb, own, axis=2, keepdims=False)
        v_own = lax.dynamic_index_in_dim(vb, own, axis=2, keepdims=False)
        s_own = jnp.einsum('bhqd,bhpd->bhqp', qq, k_own, preferred_element_type=jnp.float32)
        d_own = t[:, None] - (own * MOBA_BLOCK + jnp.arange(MOBA_BLOCK))[None, :]
        s_own = jnp.where(d_own >= 0, s_own - slopes4 * d_own.astype(jnp.float32), NEG_INF)
        p = jax.nn.softmax(jnp.concatenate([s_sel, s_own], axis=-1), axis=-1)
        p_sel = p[..., :ksel * MOBA_BLOCK].reshape(B, N_HEADS_2, Q_CHUNK, ksel, MOBA_BLOCK).astype(vb.dtype)
        p_own = p[..., ksel * MOBA_BLOCK:].astype(vb.dtype)
        return (jnp.einsum('bhqkp,bhqkpd->bhqd', p_sel, vg)
                + jnp.einsum('bhqp,bhpd->bhqd', p_own, v_own))

    out = lax.map(chunk, (jnp.arange(nc), q_c, sel_c))
    return out.transpose(1, 0, 3, 2, 4).reshape(B, T, N_HEADS_2 * HEAD_DIM)

def second_inputs(seed: int = 0) -> dict:
    key = jax.random.key(seed)
    ks = jax.random.split(key, 20)
    f32 = jnp.float32

    def nrm(k, shape, scale):
        return jax.random.normal(k, shape, f32) * scale

    def gain(k, shape):
        return 1.0 + 0.02 * jax.random.normal(k, shape, f32)

    D = D_MODEL
    return {
        "x": jax.random.normal(ks[0], (BATCH, SEQ, D), f32),
        "ffn_norm_pre": gain(ks[1], (DEPTH, 2, D)),
        "ffn_norm_post": gain(ks[2], (DEPTH, 2, D)),
        "ffn_w_gate_up": nrm(ks[3], (DEPTH, 2, D, 2 * D_FF), D ** -0.5),
        "ffn_w_down": nrm(ks[4], (DEPTH, 2, D_FF, D), D_FF ** -0.5),
        "mix_norm_pre": gain(ks[5], (DEPTH, D)),
        "mix_norm_post": gain(ks[6], (DEPTH, D)),
        "conv_w_in": nrm(ks[7], (N_A_LAYERS, D, 2 * D), D ** -0.5),
        "conv_b_in": nrm(ks[8], (N_A_LAYERS, 2 * D), 0.02),
        "conv_w_dw": nrm(ks[9], (N_A_LAYERS, CONV_WIDTH, D), CONV_WIDTH ** -0.5),
        "conv_b_dw": nrm(ks[10], (N_A_LAYERS, D), 0.02),
        "conv_ln_g": gain(ks[11], (N_A_LAYERS, D)),
        "conv_ln_b": nrm(ks[12], (N_A_LAYERS, D), 0.02),
        "conv_w_out": nrm(ks[13], (N_A_LAYERS, D, D), D ** -0.5),
        "conv_b_out": nrm(ks[14], (N_A_LAYERS, D), 0.02),
        "kv_norm": gain(ks[15], (D,)),
        "w_kv": nrm(ks[16], (D, 2 * D), D ** -0.5),
        "attn_w_q": nrm(ks[17], (N_B_LAYERS, D, D), D ** -0.5),
        "attn_w_o": nrm(ks[18], (N_B_LAYERS, D, D), D ** -0.5),
    }

def second_block(x, ffn_norm_pre, ffn_norm_post, ffn_w_gate_up, ffn_w_down, mix_norm_pre,
              mix_norm_post, conv_w_in, conv_b_in, conv_w_dw, conv_b_dw, conv_ln_g, conv_ln_b,
              conv_w_out, conv_b_out, kv_norm, w_kv, attn_w_q, attn_w_o):
    B, T, _ = x.shape
    slopes = alibi_slopes()
    kv = None
    for layer in range(DEPTH):
        f = swiglu_ffn(rms_norm(x, ffn_norm_pre[layer, 0]), ffn_w_gate_up[layer, 0], ffn_w_down[layer, 0])
        x = x + MACARON_WEIGHT * rms_norm(f, ffn_norm_post[layer, 0])
        h = rms_norm(x, mix_norm_pre[layer])
        if layer < N_A_LAYERS:
            a = layer
            y = conformer_conv(h, conv_w_in[a], conv_b_in[a], conv_w_dw[a], conv_b_dw[a],
                               conv_ln_g[a], conv_ln_b[a], conv_w_out[a], conv_b_out[a])
        else:
            if kv is None:
                kv = shared_kv(x, kv_norm, w_kv)
            j = layer - N_A_LAYERS
            q = (h @ attn_w_q[j]).reshape(B, T, N_HEADS_2, HEAD_DIM)
            y = moba_attention(q, kv[0], kv[1], kv[2], slopes) @ attn_w_o[j]
        x = x + rms_norm(y, mix_norm_post[layer])
        f = swiglu_ffn(rms_norm(x, ffn_norm_pre[layer, 1]), ffn_w_gate_up[layer, 1], ffn_w_down[layer, 1])
        x = x + MACARON_WEIGHT * rms_norm(f, ffn_norm_post[layer, 1])
    return x


def setup_inputs(seed=0):
    out = dict(first_inputs(seed))
    for name, value in second_inputs(seed + 1).items():
        if name != "x":
            out[name + "_2"] = value
    return out


def reference(
    x, c, ctx, c_ctx, w_mod, b_mod, norm1_g, norm2_g, w_in, b_gate, q_norm_g, w_uq, kv_norm_g,
    w_ukv, w_oa, w_ob, w_grp, pool_scale, w_oc, w_out, w_pq, peer_keys, peer_down, peer_up,
    final_g, ffn_norm_pre_2, ffn_norm_post_2, ffn_w_gate_up_2, ffn_w_down_2, mix_norm_pre_2,
    mix_norm_post_2, conv_w_in_2, conv_b_in_2, conv_w_dw_2, conv_b_dw_2, conv_ln_g_2,
    conv_ln_b_2, conv_w_out_2, conv_b_out_2, kv_norm_2, w_kv_2, attn_w_q_2, attn_w_o_2,
):
    x = first_block(
        x, c, ctx, c_ctx, w_mod, b_mod, norm1_g, norm2_g, w_in, b_gate, q_norm_g, w_uq,
        kv_norm_g, w_ukv, w_oa, w_ob, w_grp, pool_scale, w_oc, w_out, w_pq, peer_keys,
        peer_down, peer_up, final_g,
    )
    return second_block(
        x, ffn_norm_pre_2, ffn_norm_post_2, ffn_w_gate_up_2, ffn_w_down_2, mix_norm_pre_2,
        mix_norm_post_2, conv_w_in_2, conv_b_in_2, conv_w_dw_2, conv_b_dw_2, conv_ln_g_2,
        conv_ln_b_2, conv_w_out_2, conv_b_out_2, kv_norm_2, w_kv_2, attn_w_q_2, attn_w_o_2,
    )


_drawn_inputs = setup_inputs


def setup_inputs(seed=0):
    import zlib

    import numpy as np

    out = dict(_drawn_inputs(seed))
    spreads = {}
    factors = {'norm1_g': 4.396,
     'norm2_g': 3.109,
     'b_gate': 8.0,
     'q_norm_g': 8.0,
     'kv_norm_g': 8.0,
     'pool_scale': 5.797,
     'ffn_norm_post_2': 3.587,
     'mix_norm_pre_2': 2.995,
     'mix_norm_post_2': 2.841,
     'kv_norm_2': 4.578}
    for name, (base, spread) in spreads.items():
        noise = np.random.default_rng([zlib.crc32(name.encode()), seed]).standard_normal(out[name].shape)
        drawn = base * np.exp(spread * noise) if base else spread * noise
        out[name] = __import__('jax').numpy.asarray(drawn.astype(out[name].dtype))
    for name, factor in factors.items():
        out[name] = (out[name] * factor).astype(out[name].dtype)
    return out
```

```python
from contextlib import ExitStack

import numpy as np

import concourse.bass as bass
from concourse import mybir

P = 128
D = 1024
KT = D // P
TOK = 256
TT = TOK // P
EPS = 1e-6
H = 8
NOPE, ROPE, VH = 64, 32, 64
QK = NOPE + ROPE
QLORA, KVLORA = 256, 128
ATT_SCALE = QK ** -0.5
WA = QLORA + KVLORA + ROPE
WZ = 512
HP = 16
KEYS = 128
TOP = 16
NEG = -3.0e38
GROUP = 8
GROUPS = P // GROUP
SLOTS = 3
SLOT_W = 2048
DIAGS = 4
GELU_C = 0.7978845608028654
GELU_A = 0.044715

RUNS = {"c0": (1, 0), "x0": (0, 0), "x1": (0, 1), "c1": (1, 1)}
GATHERS = [(r, t) for r in ("x0", "c0", "x1") for t in range(TT)]
GATHER_NO = {g: n for n, g in enumerate(GATHERS)}


def keys_stages(r):
    return [("norm", r, 0), ("hT", r, 0), ("zA", r), ("kv", r)]


def mix_stages(r):
    return [("hT", r, 2), ("zF", r), ("four", r), ("q", r), ("att", r), ("gate", r), ("out", r), ("norm", r, 1), ("hT", r, 1), ("pq", r)]


def expert_stages(r):
    return [st for t in range(TT) for st in (("route", r, t), ("gather", r, t), ("fin", r, t))]


ORDER = (
    [("start",), ("mod", 0)] + keys_stages("c0") + keys_stages("x0") + mix_stages("x0") + expert_stages("x0")
    + mix_stages("c0") + expert_stages("c0")
    + [("mod", 1)] + keys_stages("x1") + keys_stages("c1") + mix_stages("x1") + expert_stages("x1") + [("final",)]
)

FF = 2816
FT = FF // P
FP_ = FT // 2
TAPS = 31
PAD = TAPS - 1
H2, DH = 8, 128
LN_EPS = 1e-5
BLOCKS = ["f0", "cv", "f1", "f2", "at", "f3"]


def block_stages(tag):
    inner = {"f": [("gu", tag), ("dn", tag)], "c": [("cin",), ("dw",), ("ln",), ("cout",)], "a": [("qkv",), ("moba",), ("ao",)]}[tag[0]]
    return [("pre", tag), ("hT2", tag)] + inner + [("post", tag)]


ORDER2 = [st for tag in BLOCKS for st in block_stages(tag)] + [("store",)]
SS2_AT, X2_AT, H2_AT = {}, {"start": 2}, {}
_s, _x, _h = 0, 2, 0
for _st in ORDER2:
    if _st[0] == "pre":
        _s += 2
        SS2_AT["pre", _st[1]] = _s
        _h += 4 if _st[1] == "at" else 2
        H2_AT[_st[1]] = _h
    elif _st[0] == "post":
        _s += 4
        SS2_AT["post", _st[1]] = _s
        _x += 2
        X2_AT[_st[1]] = _x


def x2_before(tag):
    n = BLOCKS.index(tag)
    return X2_AT[BLOCKS[n - 1]] if n else X2_AT["start"]


def plan2():
    plan = []
    for name, *args in ORDER2:
        if name in ("gu", "dn"):
            n = int(args[0][1])
            plan += [("wgu" if name == "gu" else "wdn", (n, c)) for c in range(2 * FP_ if name == "gu" else FT // 2)]
        elif name == "cin":
            plan += [("cwin", (c,)) for c in range(8)]
        elif name == "cout":
            plan += [("cwout", (c,)) for c in range(4)]
        elif name == "qkv":
            plan += [("w2k", (c,)) for c in range(4)] + [("w2v", (c,)) for c in range(4)] + [("w2q", (c,)) for c in range(4)]
        elif name == "ao":
            plan += [("w2o", (c,)) for c in range(4)]
    return plan


SLOTS2 = 4

MARKS = {
    "h": (2, ["c0", "x0", "x1", "c1"]),
    "ckn": (2, ["c0", "x0", "x1", "c1"]),
    "krr": (2, ["c0", "x0", "x1", "c1"]),
    "cqn": (2, ["x0", "c0", "x1"]),
    "qr": (2, ["x0", "x1"]),
    "nmax": (16, ["x0", "c0", "x1"]),
    "pn": (16, ["x0", "c0", "x1"]),
    "mixT": (4, ["x0", "c0", "x1"]),
    "resid": (4, ["x0", "c0", "x1"]),
    "topd": (2, ["x0", "c0", "x1"]),
    "route": (2, ["x0", "c0", "x1"]),
    "fin": (2, ["x0", "c0", "x1"]),
    "ss": (4, ["c0", "x0", "x1", "c1"]),
    "kvss": (2, ["c0", "x0", "x1", "c1"]),
    "qss": (2, ["x0", "c0", "x1"]),
    "tope": (2, ["x0", "c0", "x1"]),
}


def mark_base(name, run):
    per, runs = MARKS[name]
    return per * runs.index(run)


def chunk_plan():
    plan = []
    for st in ORDER:
        name = st[0]
        if name == "mod":
            plan += [("wmod", (st[1], n), SLOT_W) for n in range(24)]
            continue
        if name in ("start", "final"):
            continue
        l = RUNS[st[1]][1]
        if name == "zA":
            plan += [("wA", (l, n), 4 * WA) for n in range(2)]
        elif name == "kv":
            plan += [("wukv", (l,), D)]
        elif name == "zF":
            plan += [("wZ", (l, n), SLOT_W) for n in range(2)]
        elif name == "four":
            plan += [("dft", (), 2 * 768), ("poolm", (), SLOT_W), ("wgrp", (l,), 256)]
        elif name == "q":
            plan += [("wuq", (l,), 2 * H * QK)]
        elif name == "gate":
            for dp in range(4):
                plan += [("wG", (l, dp, j), SLOT_W) for j in range(3)] + [("wO", (l, dp), SLOT_W)]
        elif name == "out":
            plan += [("wout", (l, n), SLOT_W) for n in range(4)]
        elif name == "pq":
            plan += [("wpq", (l, n), SLOT_W) for n in range(8)]
    return plan


def build(nc, A, out):
    f32, i32, u32 = mybir.dt.float32, mybir.dt.int32, mybir.dt.uint32
    ALU, ACT, AX = mybir.AluOpType, mybir.ActivationFunctionType, mybir.AxisListType
    ctx = ExitStack()

    def sb(name, shape, dt=f32):
        return ctx.enter_context(nc.sbuf_tensor(name, shape, dt))

    def sem(name):
        return ctx.enter_context(nc.semaphore(name))

    with ctx:
        x = [sb("x_in", [P, TT, D]), sb("x_ctx", [P, TT, D])]
        h = [sb("h_in", [P, TT, D]), sb("h_ctx", [P, TT, D])]
        hT = sb("hT", [P, KT, TOK])
        mrows = [sb(f"mrows{l}", [P, 3, 512]) for l in range(2)]
        gain = sb("gain", [P, D])
        keysT = sb("keysT", [P, HP * KEYS])
        amul, junk = keysT[:, 0:D], keysT[:, D:2 * D]
        mb = sb("mb", [P, D])
        wring = sb("wring", [P, SLOTS, SLOT_W])
        rows = sb("rows", [P, GROUP, D])
        zA = [sb("zA_in", [P, TT, WA]), sb("zA_ctx", [P, TT, WA])]
        kT = sb("kT", [P, H, 2 * TOK])
        vv = sb("vv", [P, 2 * TT, H * VH])
        YT = sb("YT", [P, 512])
        ypT = sb("ypT", [P, 512])
        ident = sb("ident", [P, P])
        sel = sb("sel", [P, 2, P])
        rope = sb("rope", [P, TT, 32])
        iota = sb("iota", [P, TOP])
        cvec = sb("cvec", [P, KT, 2])
        cth = sb("cth", [P, KT, 2])
        vecs = sb("vecs", [P, 58])
        hbg = sb("hbg", [P, 2, 24])
        ss = sb("ss", [P, 8])
        nwt = sb("nwt", [P, 8])
        nwi = sb("nwi", [P, 8], i32)
        a8 = sb("a8", [P, GROUP])
        g1 = sb("g1", [P, GROUP])
        g2 = sb("g2", [P, GROUP])
        th8 = sb("th8", [P, GROUP])
        act8 = sb("act8", [P, GROUP])
        diag = sb("diag", [P, DIAGS, P])
        accv = sb("accv", [P, 512])
        nmax, rsum, rinv = (sb(n, [P, 4]) for n in ("nmax", "rsum", "rinv"))
        idx = [sb(f"idx{t}", [P, P], u32) for t in range(TT)]
        gates = [sb(f"gates{t}", [P, P]) for t in range(TT)]
        idown = [sb(f"idown{n}", [P, GROUP], u32) for n in range(2)]
        iup = [sb(f"iup{n}", [P, GROUP], u32) for n in range(2)]
        U = sb("shared", [P, 10240])
        at = [0]

        def part(n):
            at[0] += n
            assert at[0] <= 10240, at
            return U[:, at[0] - n:at[0]]

        q = part(2 * 768).rearrange("p (t n) -> p t n", t=TT)
        kfull = part(2 * 768).rearrange("p (t n) -> p t n", t=TT)
        qT = part(H * TOK).rearrange("p (h n) -> p h n", h=H)
        at[0] = 2 * 1536
        sg = part(3 * 512).rearrange("p (j n) -> p j n", j=3)
        mtmp = part(512)
        at[0] = 0
        mixT = part(KT * TOK).rearrange("p (k n) -> p k n", k=KT)
        at[0] = 3072 + 2048
        pr = part(4 * 512).rearrange("p (a t n) -> p a t n", a=2, t=TT)
        pT = part(4 * TOK).rearrange("p (k n) -> p k n", k=4)
        attT = part(4 * TOK).rearrange("p (k n) -> p k n", k=4)
        ckn = part(2 * P).rearrange("p (t n) -> p t n", t=TT)
        ckT = part(TOK)
        rtmp = part(4 * P).rearrange("p (a n) -> p a n", a=4)
        at[0] = 3072 + 2048
        zfp = part(2 * 512).rearrange("p (t n) -> p t n", t=TT)
        T1 = part(2 * 512).rearrange("p (t n) -> p t n", t=TT)
        poolT = part(512)
        cqn = part(2 * QLORA).rearrange("p (t n) -> p t n", t=TT)
        cqT = part(2 * TOK).rearrange("p (k n) -> p k n", k=2)
        at[0] = 0
        s_sb = part(TT * 2048).rearrange("p (t n) -> p t n", t=TT)
        cand = part(2048)
        eq = part(2048)
        qpT = part(2 * 512).rearrange("p (a n) -> p a n", a=2)
        sv = part(HP * TOP).rearrange("p (i k) -> p i k", k=TOP)
        si = part(HP * TOP).bitcast(u32).rearrange("p (i k) -> p i k", k=TOP)
        sif = part(HP * TOP).rearrange("p (i k) -> p i k", k=TOP)
        ts = part(P).rearrange("p (i k) -> p i k", k=TOP)
        at[0] += 0
        pos = eq[:, 0:P].bitcast(u32).rearrange("p (i k) -> p i k", k=TOP)
        pa = junk[:, 0:P].bitcast(u32)
        fa, fb, ia, ib = (junk[:, n * P:(n + 1) * P] for n in range(1, 5))
        te = junk[:, 640:768].rearrange("p (i k) -> p i k", k=TOP)
        tsum = junk[:, 768:776]
        pos = junk[:, 896:1024].bitcast(u32).rearrange("p (i k) -> p i k", k=TOP)

        W2 = [wring[:, n, :] for n in range(SLOTS)] + [rows[:, 0:2, :].rearrange("p a n -> p (a n)")]
        gain2 = [gain, mb]
        at[0] = 0
        hid = part(FT * TOK).rearrange("p (k n) -> p k n", k=FT)
        fth = part(4 * TOK).rearrange("p (a n) -> p a n", a=4)
        ft2 = part(4 * TOK).rearrange("p (a n) -> p a n", a=4)
        at[0] = 0
        upad = part(8 * (TOK + PAD)).rearrange("p (c n) -> p c n", c=8)
        uc = part(8 * TOK).rearrange("p (c n) -> p c n", c=8)
        usq = part(8 * TOK).rearrange("p (c n) -> p c n", c=8)
        uth = part(8 * TOK).rearrange("p (c n) -> p c n", c=8)
        rln, rl2 = part(TOK), part(TOK)
        ctmp = part(2 * TOK).rearrange("p (a n) -> p a n", a=2)
        bout_b, vec2 = keysT[:, 0:D], keysT[:, D:D + 288]
        rli = rows[:, 2, 0:TOK].bitcast(i32)
        rli2 = rows[:, 2, TOK:2 * TOK].bitcast(i32)
        ones = rows[:, 3, 0:P]
        kT2 = kT[:, :, 0:TOK]
        qT2 = kT[:, :, TOK:2 * TOK]
        v2 = vv[:, :, :].rearrange("p a n -> p (a n)").rearrange("p (t n) -> p t n", t=TT)
        at[0] = 0
        attT2 = part(8 * TOK).rearrange("p (h n) -> p h n", h=8)
        hkT = part(KT * TOK).rearrange("p (k n) -> p k n", k=KT)
        p2 = part(4 * TOK).rearrange("p (a t n) -> p a t n", a=2, t=TT)
        pT2 = part(2 * TOK).rearrange("p (k n) -> p k n", k=2)
        dist = rows[:, 3, 512:1024].rearrange("p (t n) -> p t n", t=TT)

        ps = ctx.enter_context(nc.psum_tensor("ps", [P, 8, 512], f32))
        ROT = [0, 1, 2, 3, 5, 6, 7]
        ROT2, WIDE = [0, 1, 2, 3], [4, 5, 6, 7]
        UPB = 4
        UPV = 512

        mm_done = sem("mm_done")
        bank_free = [sem(f"bank_free{b}") for b in range(8)]
        mark = {n: sem(n) for n in MARKS}
        chunk_in = [sem(f"chunk_in{n}") for n in range(SLOTS)]
        row_in = [sem(f"row_in{n}") for n in range(GROUP)]
        ld_const, ld_x, ld_c, ld_gain, ld_keys, ld_mrow = (sem(n) for n in ("ld_const", "ld_x", "ld_c", "ld_gain", "ld_keys", "ld_mrow"))
        gain_used = sem("gain_used")
        dve_step, act_step = sem("dve_step"), sem("act_step")
        silu_t, silu_c = sem("silu_t"), sem("silu_c")
        down_done, upv_done, upp_done = sem("down_done"), sem("upv_done"), sem("upp_done")
        idx_copied, gelu_step, gelu_in, gelu_th, act_ready, diag_ready = (sem(n) for n in (
            "idx_copied", "gelu_step", "gelu_in", "gelu_th", "act_ready", "diag_ready"))
        slot_ok = sem("slot_ok")
        ss2, x2, h2m, ld_vec2, ones_set = (sem(n) for n in ("ss2", "x2", "h2m", "ld_vec2", "ones_set"))
        gain2_in = [sem(f"gain2_in{n}") for n in range(2)]
        gain2_used = sem("gain2_used")
        chunk2_in = [sem(f"chunk2_in{n}") for n in range(SLOTS2)]
        gate_th, gu_step = sem("gate_th"), sem("gu_step")
        conv_h, conv_th, conv_u, conv_y, ln_d, ln_v, ln_z, ln_t, ln_s = (sem(n) for n in (
            "conv_h", "conv_th", "conv_u", "conv_y", "ln_d", "ln_v", "ln_z", "ln_t", "ln_s"))
        s2_ready, p2_ready, bout_y = sem("s2_ready"), sem("p2_ready"), sem("bout_y")
        out_done = sem("out_done")

        mm_at, job_bank, job_use = {}, {}, {}
        uses = [0] * 8
        plan = chunk_plan()
        gu_base, chunk2_done = {}, []
        chunk_done = []

        def at_mark(eng, name, run, n):
            eng.wait_ge(mark[name], mark_base(name, run) + n)

        def at_mm(eng, key):
            eng.wait_ge(mm_done, mm_at[key])
            return ps[:, job_bank[key], :]

        def at_evac(eng, key):
            eng.wait_ge(bank_free[job_bank[key]], job_use[key])

        def release(ins, key):
            ins.then_inc(bank_free[job_bank[key]], 1)

        def norm_mark(run, k, n):
            firsts = {"c0": 0, "x0": 1, "x1": 4, "c1": 5}
            return (firsts[run] if k == 0 else {"x0": 2, "c0": 3, "x1": 6}[run]) * 2 + n

        block = ctx.enter_context(nc.Block())

        @block.tensor
        def _(pe):
            count = [0]
            rot = [0]
            chunk_no = [0]

            def job(key):
                b = ROT[rot[0] % len(ROT)]
                rot[0] += 1
                if uses[b]:
                    pe.wait_ge(bank_free[b], uses[b])
                uses[b] += 1
                job_bank[key], job_use[key] = b, uses[b]
                return ps[:, b, :]

            def ended(ins, key):
                count[0] += 1
                ins.then_inc(mm_done, 1)
                mm_at[key] = count[0]

            def chunk():
                n = chunk_no[0]
                chunk_no[0] += 1
                pe.wait_ge(chunk_in[n % SLOTS], 16 * (n // SLOTS + 1))
                return wring[:, n % SLOTS, 0:plan[n][2]]

            def chunk_end(n=1):
                chunk_done.extend([count[0]] * n)

            def bcast(key, run, j, half):
                s, l = RUNS[run]
                cc = 2 * j + half
                at_evac(pe, ("mod", l, cc))
                qd, a = 32 * (cc % 4), cc // 4
                ended(pe.matmul(job(key), sel[qd:qd + 2, s, :], mrows[l][qd:qd + 2, a, :], start=True, stop=True,
                                tile_position=(qd, 0)), key)

            def start():
                pe.wait_ge(ld_const, 16 * 6)

            def mod(l):
                pe.wait_ge(silu_c, 1)
                for cc in range(12):
                    qd = 32 * (cc % 4)
                    b = job(("mod", l, cc))
                    for half in range(2):
                        w = chunk()
                        for k in range(4):
                            last = pe.matmul(b[qd:qd + 2, :], cvec[:, 4 * half + k, :], w[:, k * 512:(k + 1) * 512],
                                             start=(half + k == 0), stop=(half == 1 and k == 3), tile_position=(0, qd))
                    ended(last, ("mod", l, cc))
                    chunk_end(2)

            def norm(run, k):
                for half in range(2):
                    bcast(("bs", run, k, half), run, 1 + 3 * k, half)
                for half in range(2):
                    bcast(("bh", run, k, half), run, 3 * k, half)

            def hT_(run, k):
                s = RUNS[run][0]
                for a in range(2):
                    for t in range(TT):
                        if k == 2:
                            pass
                        elif t == 0:
                            pe.wait_ge(mark["h"], norm_mark(run, k, a + 1))
                        else:
                            at_evac(pe, ("bh", run, k, a))
                        b = job(("hT", run, k, t, a))
                        for j in range(4):
                            last = pe.transpose(b[:, j * P:(j + 1) * P], h[s][:, t, (4 * a + j) * P:(4 * a + j + 1) * P], ident[:, :])
                        ended(last, ("hT", run, k, t, a))

            def hT_ready(run, k):
                for t in range(TT):
                    for a in range(2):
                        at_evac(pe, ("hT", run, k, t, a))

            def token_major(keys, lhs, width, halves=2):
                bs = [job(k) for k in keys]
                for c in range(2):
                    w = chunk()
                    for t in range(TT):
                        for k in range(4):
                            last = pe.matmul(bs[t][:, 0:width], lhs[:, 4 * c + k, t * P:(t + 1) * P], w[:, k * width:(k + 1) * width],
                                             start=(c + k == 0), stop=(c == 1 and k == 3))
                        if c == 1:
                            ended(last, keys[t])
                chunk_end(2)

            def zA_(run):
                hT_ready(run, 0)
                token_major([("zA", run, t) for t in range(TT)], hT, WA)

            def kv(run):
                b = job(("ckT", run))
                for t in range(TT):
                    at_mark(pe, "ckn", run, t + 1)
                    last = pe.transpose(b[:, t * P:(t + 1) * P], ckn[:, t, :], ident[:, :])
                ended(last, ("ckT", run))
                w = chunk()
                at_evac(pe, ("ckT", run))
                for t in range(TT):
                    for half in range(2):
                        key = ("kv", run, t, half)
                        ended(pe.matmul(job(key), ckT[:, t * P:(t + 1) * P], w[:, half * 512:(half + 1) * 512], start=True, stop=True), key)
                chunk_end()
                for t in range(TT):
                    at_mark(pe, "krr", run, t + 1)
                    for hq in range(2):
                        at_evac(pe, ("kv", run, t, hq))
                        b = job(("kT", run, t, hq))
                        for j in range(4):
                            hh = 4 * hq + j
                            last = pe.transpose(b[0:QK, j * P:(j + 1) * P], kfull[:, t, hh * QK:(hh + 1) * QK], ident[:, :])
                        ended(last, ("kT", run, t, hq))

            def zF(run):
                hT_ready(run, 2)
                token_major([("zF", run, t) for t in range(TT)], hT, WZ)

            def four(run):
                for t in range(TT):
                    at_evac(pe, ("zF", run, t))
                w = chunk().rearrange("p (k n) -> p k n", k=2)
                for ft in range(2):
                    b = job(("T1", run, ft))
                    for lt in range(TT):
                        last = pe.matmul(b, zfp[:, lt, ft * P:(ft + 1) * P], w[:, lt, 0:512], start=(lt == 0), stop=(lt == 1))
                    ended(last, ("T1", run, ft))
                wp = chunk().rearrange("p (k g n) -> p k g n", k=2, g=4)
                b = job(("P", run))
                for g in range(4):
                    for lt in range(TT):
                        po = 64 * (g % 2)
                        last = pe.matmul(b[po:po + 64, (g // 2) * TOK:(g // 2 + 1) * TOK], zfp[:, lt, TOK + g * 64:TOK + (g + 1) * 64],
                                         wp[:, lt, g, :], start=(lt == 0), stop=(lt == 1), tile_position=(0, po))
                ended(last, ("P", run))
                b = job(("Y", run))
                for ft in range(2):
                    at_evac(pe, ("T1", run, ft))
                for fo in range(2):
                    for ft in range(2):
                        for part_ in range(2):
                            last = pe.matmul(b[:, fo * TOK:(fo + 1) * TOK], w[:, ft, part_ * 512 + fo * P:part_ * 512 + (fo + 1) * P],
                                             T1[:, ft, part_ * TOK:(part_ + 1) * TOK], start=(ft + part_ == 0), stop=(ft + part_ == 2))
                ended(last, ("Y", run))
                chunk_end(2)
                wg = chunk()
                at_evac(pe, ("P", run))
                b = job(("G", run))
                for pair in range(2):
                    last = pe.matmul(b[:, pair * TOK:(pair + 1) * TOK], wg[:, pair * P:(pair + 1) * P], poolT[:, pair * TOK:(pair + 1) * TOK],
                                     start=True, stop=True)
                ended(last, ("G", run))
                chunk_end()

            def q_(run):
                b = job(("cqT", run))
                for t in range(TT):
                    at_mark(pe, "cqn", run, t + 1)
                    for k in range(2):
                        last = pe.transpose(b[:, k * TOK + t * P:k * TOK + (t + 1) * P], cqn[:, t, k * P:(k + 1) * P], ident[:, :])
                ended(last, ("cqT", run))
                w = chunk()
                at_evac(pe, ("cqT", run))
                for t in range(TT):
                    for half in range(2):
                        key = ("q", run, t, half)
                        b = job(key)
                        for k in range(2):
                            last = pe.matmul(b[:, 0:384], cqT[:, k, t * P:(t + 1) * P], w[:, k * 768 + half * 384:k * 768 + (half + 1) * 384],
                                             start=(k == 0), stop=(k == 1))
                        ended(last, key)
                chunk_end()
                for t in range(TT):
                    for half in range(2):
                        at_evac(pe, ("q", run, t, half))
                    if RUNS[run][0] == 0:
                        at_mark(pe, "qr", run, t + 1)
                    for hq in range(2):
                        b = job(("qT", run, t, hq))
                        for j in range(4):
                            hh = 4 * hq + j
                            last = pe.transpose(b[0:QK, j * P:(j + 1) * P], q[:, t, hh * QK:(hh + 1) * QK], ident[:, :])
                        ended(last, ("qT", run, t, hq))

            def att(run):
                nk = 4 if RUNS[run][0] == 0 else 2
                for r2 in {"x0": ("x0", "c0"), "c0": ("c0",), "x1": ("x1", "c1")}[run]:
                    for t in range(TT):
                        for hq in range(2):
                            at_evac(pe, ("kT", r2, t, hq))
                for t in range(TT):
                    for hq in range(2):
                        at_evac(pe, ("qT", run, t, hq))

                def scores(hh):
                    for t in range(TT):
                        key = ("s", run, hh, t)
                        ended(pe.matmul(job(key)[:, 0:nk * P], qT[0:QK, hh, t * P:(t + 1) * P], kT[0:QK, hh, 0:nk * P], start=True, stop=True), key)

                scores(0)
                for hh in range(H):
                    if hh + 1 < H:
                        scores(hh + 1)
                    for t in range(TT):
                        at_mark(pe, "pn", run, 2 * hh + t + 1)
                        b = job(("pT", run, hh, t))
                        for k in range(nk):
                            last = pe.transpose(b[:, k * P:(k + 1) * P], pr[:, hh % 2, t, k * P:(k + 1) * P], ident[:, :])
                        ended(last, ("pT", run, hh, t))
                    for t in range(TT):
                        at_evac(pe, ("pT", run, hh, t))
                    if hh % 2 == 0:
                        pv = job(("pv", run, hh // 2))
                    po = 64 * (hh % 2)
                    for k in range(nk):
                        last = pe.matmul(pv[po:po + VH, 0:TOK], vv[:, k, hh * VH:(hh + 1) * VH], pT[:, k, :],
                                         start=(k == 0), stop=(k == nk - 1), tile_position=(0, po))
                    if hh % 2:
                        ended(last, ("pv", run, hh // 2))

            def gate(run):
                s = RUNS[run][0]
                for n in range(4):
                    at_evac(pe, ("pv", run, n))
                at_evac(pe, ("Y", run))
                at_evac(pe, ("G", run))
                for dp in range(4):
                    for j in range(3):
                        w = chunk()
                        b = job(("g", run, dp, j))
                        for dt in range(2):
                            for k in range(KT):
                                last = pe.matmul(b[:, dt * TOK:(dt + 1) * TOK], w[:, k * 256 + dt * P:k * 256 + (dt + 1) * P], hT[:, k, :],
                                                 start=(k == 0), stop=(k == KT - 1))
                        ended(last, ("g", run, dp, j))
                        chunk_end()
                    w = chunk()
                    for j, ks in enumerate(([0, 1, 2, 3], [4, 5], [6, 7])):
                        b = job(("y", run, dp, j))
                        for dt in range(2):
                            for k in ks:
                                rhs = attT[:, k, :] if j == 0 else (YT, ypT)[j - 1][:, (k % 2) * TOK:(k % 2 + 1) * TOK]
                                last = pe.matmul(b[:, dt * TOK:(dt + 1) * TOK], w[:, k * 256 + dt * P:k * 256 + (dt + 1) * P], rhs,
                                                 start=(k == ks[0]), stop=(k == ks[-1]))
                        ended(last, ("y", run, dp, j))
                    chunk_end()

            def out_(run):
                at_mark(pe, "mixT", run, 4)
                for half in range(2):
                    bcast(("bm", run, half), run, 2, half)
                    token_major([("o", run, half, t) for t in range(TT)], mixT, 512)

            def pq(run):
                hT_ready(run, 1)
                pe.wait_ge(ld_keys, 16 * (["x0", "c0", "x1"].index(run) + 1))

                def queries(c):
                    w = chunk()
                    b = job(("qp", run, c))
                    for hp in range(2):
                        for k in range(KT):
                            last = pe.matmul(b[:, hp * TOK:(hp + 1) * TOK], w[:, k * 256 + hp * P:k * 256 + (hp + 1) * P],
                                             hT[:, k, :], start=(k == 0), stop=(k == KT - 1))
                    ended(last, ("qp", run, c))
                    chunk_end()

                queries(0)
                for c in range(8):
                    if c < 7:
                        queries(c + 1)
                    at_evac(pe, ("qp", run, c))
                    b = job(("sc", run, c))
                    for t in range(TT):
                        for hp in range(2):
                            last = pe.matmul(b[:, t * 256 + hp * P:t * 256 + (hp + 1) * P], qpT[:, c % 2, hp * TOK + t * P:hp * TOK + (t + 1) * P],
                                             keysT[:, (2 * c + hp) * P:(2 * c + hp + 1) * P], start=True, stop=True)
                    ended(last, ("sc", run, c))

            def gather(run, t):
                G = GATHER_NO[run, t]
                if G:
                    at_mark(pe, "fin", GATHERS[G - 1][0], GATHERS[G - 1][1] + 1)

                def up(g, first=False, last=False):
                    pos_ = 31 if last else 2 * g + 2
                    for j in range(GROUP):
                        pe.wait_ge(row_in[j], 16 * (32 * G + 1) + 16 * pos_)
                        pe.wait_ge(diag_ready, 8 * g + (P * G + j + 1))
                        pe.matmul(ps[:, UPB, :], diag[:, j % DIAGS, :], rows[:, j, UPV:D], start=(first and j == 0), stop=(last and j == GROUP - 1),
                                  skip_group_check=True).then_inc(upp_done, 1)

                up(0, first=True)
                with pe.Fori(1, GROUPS - 1) as g:
                    up(g)
                up(GROUPS - 1, last=True)

            def fin(run, t):
                for half in range(2):
                    bcast(("bf", run, t, half), run, 5, half)

            rots = {"a": 0, "w": 0}
            chunk2_no = [0]
            plan_2 = plan2()

            def job2(key, wide=False):
                banks, r = (WIDE, "w") if wide else (ROT2, "a")
                b = banks[rots[r] % 4]
                rots[r] += 1
                if uses[b]:
                    pe.wait_ge(bank_free[b], uses[b])
                uses[b] += 1
                job_bank[key], job_use[key] = b, uses[b]
                return ps[:, b, :]

            def chunk2():
                n = chunk2_no[0]
                chunk2_no[0] += 1
                pe.wait_ge(chunk2_in[n % SLOTS2], 16 * (n // SLOTS2 + 1))
                return W2[n % SLOTS2]

            def chunk2_end(n=1):
                chunk2_done.extend([count[0]] * n)

            def hT2(tag):
                for gi, (src, dst) in enumerate([(h[1], hkT), (h[0], hT)] if tag == "at" else [(h[0], hT)]):
                    for t in range(TT):
                        pe.wait_ge(h2m, H2_AT[tag] - (4 if tag == "at" else 2) + 2 * gi + t + 1)
                        for a in range(2):
                            key = ("hT2", tag, gi, t, a)
                            b = job2(key)
                            for j in range(4):
                                last = pe.transpose(b[:, j * P:(j + 1) * P], src[:, t, (4 * a + j) * P:(4 * a + j + 1) * P], ident[:, :])
                            ended(last, key)

            def hT2_ready(tag, gi=0):
                for t in range(TT):
                    for a in range(2):
                        at_evac(pe, ("hT2", tag, gi, t, a))

            def pair(b, w0, w1, j):
                for side, w in enumerate((w0, w1)):
                    for k in range(KT):
                        last = pe.matmul(b[:, side * TOK:(side + 1) * TOK], w[:, k * 256 + j * P:k * 256 + (j + 1) * P], hT[:, k, :],
                                         start=(k == 0), stop=(k == KT - 1))
                return last

            def gu(tag):
                hT2_ready(tag)
                n0, m0, use0, r0 = chunk2_no[0], count[0], list(uses), rots["a"]
                gu_base[tag] = (m0, r0)
                turns = FP_ // 2
                with pe.Fori(0, turns) as i:
                    for pr_ in range(2):
                        ws = []
                        for c in range(2):
                            n = n0 + 2 * pr_ + c
                            pe.wait_ge(chunk2_in[n % SLOTS2], 16 * i + 16 * (n // SLOTS2 + 1))
                            ws.append(W2[n % SLOTS2])
                        for j in range(2):
                            b = ROT2[(r0 + 2 * pr_ + j) % 4]
                            pe.wait_ge(bank_free[b], i + use0[b])
                            pair(ps[:, b, :], *ws, j).then_inc(mm_done, 1)
                for b in ROT2:
                    uses[b] += turns
                count[0] += 4 * turns
                rots["a"] += 4 * turns
                chunk2_no[0] += 4 * turns
                for i in range(turns):
                    chunk2_done.extend([m0 + 4 * i + 2] * 2 + [m0 + 4 * i + 4] * 2)
                ws = [chunk2(), chunk2()]
                for j in range(2):
                    key = ("gu", tag, j)
                    ended(pair(job2(key), *ws, j), key)
                chunk2_end(2)

            def dn(tag):
                keys = [("d", tag, t, half) for t in range(TT) for half in range(2)]
                bs = [job2(key, True) for key in keys]
                pe.wait_ge(gu_step, 2 * FT * (int(tag[1]) + 1) - 4)
                for c in range(FT // 2):
                    w = chunk2()
                    if c == FT // 2 - 1:
                        for j in range(2):
                            at_evac(pe, ("gu", tag, j))
                    for n, (t, half) in enumerate([(t, half) for t in range(TT) for half in range(2)]):
                        for k in range(2):
                            last = pe.matmul(bs[n], hid[:, 2 * c + k, t * P:(t + 1) * P], w[:, k * D + half * 512:k * D + (half + 1) * 512],
                                             start=(c + k == 0), stop=(c == FT // 2 - 1 and k == 1))
                        if c == FT // 2 - 1:
                            ended(last, keys[n])
                    if c < FT // 2 - 1:
                        ended(last, ("dn", tag, c))
                    chunk2_end()

            def token_major2(tag, lhs, name="d", wide=True, release_w=True):
                for half in range(2):
                    keys = [(name, tag, t, half) for t in range(TT)]
                    bs = [job2(key, wide) for key in keys]
                    for c in range(2):
                        w = chunk2()
                        for t in range(TT):
                            for k in range(4):
                                last = pe.matmul(bs[t], lhs[:, 4 * c + k, t * P:(t + 1) * P], w[:, k * 512:(k + 1) * 512],
                                                 start=(c + k == 0), stop=(c == 1 and k == 3))
                            if c == 1:
                                ended(last, keys[t])
                    chunk2_end(2)

            def cin():
                hT2_ready("cv")
                for dp in range(4):
                    ws = [chunk2(), chunk2()]
                    for j in range(2):
                        key = ("cin", 2 * dp + j)
                        ended(pair(job2(key), *ws, j), key)
                    chunk2_end(2)

            def ln():
                pe.wait_ge(ones_set, 1)
                b = job2(("mean",))
                for c in range(8):
                    pe.wait_ge(conv_y, c + 1)
                    last = pe.matmul(b[:, 0:TOK], ones, uc[:, c, :], start=(c == 0), stop=(c == 7))
                ended(last, ("mean",))
                b = job2(("var",))
                pe.wait_ge(ln_v, 1)
                for c in range(8):
                    last = pe.matmul(b[:, 0:TOK], ones, usq[:, c, :], start=(c == 0), stop=(c == 7))
                ended(last, ("var",))

            def cout():
                pe.wait_ge(ln_s, 1)
                token_major2("cv", uth)

            def qkv():
                for name, gi in (("k2", 0), ("v2", 0), ("q2", 1)):
                    hT2_ready("at", gi)
                    src = (hkT, hT)[gi]
                    if name == "v2":
                        token_major2("at", src, "v2", False)
                        continue
                    for c in range(4):
                        w = chunk2()
                        b = job2((name, c))
                        for j in range(2):
                            for k in range(KT):
                                last = pe.matmul(b[:, j * TOK:(j + 1) * TOK], w[:, k * 256 + j * P:k * 256 + (j + 1) * P], src[:, k, :],
                                                 start=(k == 0), stop=(k == KT - 1))
                        ended(last, (name, c))
                        chunk2_end()

            def moba():
                for c in range(4):
                    at_evac(pe, ("k2", c))
                    at_evac(pe, ("q2", c))
                for t in range(TT):
                    for half in range(2):
                        at_evac(pe, ("v2", "at", t, half))

                def scores(hh):
                    b = job2(("s2", hh))
                    for t in range(TT):
                        last = pe.matmul(b[:, t * TOK:(t + 1) * TOK], qT2[:, hh, t * P:(t + 1) * P], kT2[:, hh, :], start=True, stop=True)
                    ended(last, ("s2", hh))

                scores(0)
                for hh in range(H2):
                    if hh + 1 < H2:
                        scores(hh + 1)
                    b = job2(("pT2", hh))
                    for t in range(TT):
                        pe.wait_ge(p2_ready, 2 * hh + t + 1)
                        for k in range(2):
                            last = pe.transpose(b[:, k * TOK + t * P:k * TOK + (t + 1) * P], p2[:, hh % 2, t, k * P:(k + 1) * P], ident[:, :])
                    ended(last, ("pT2", hh))
                    at_evac(pe, ("pT2", hh))
                    b = job2(("pv2", hh))
                    for k in range(2):
                        last = pe.matmul(b[:, 0:TOK], v2[:, k, hh * DH:(hh + 1) * DH], pT2[:, k, :], start=(k == 0), stop=(k == 1))
                    ended(last, ("pv2", hh))

            def ao():
                for hh in range(H2):
                    at_evac(pe, ("pv2", hh))
                token_major2("at", attT2)

            program = {"hT2": hT2, "gu": gu, "dn": dn, "cin": cin, "ln": ln, "cout": cout, "qkv": qkv, "moba": moba, "ao": ao,
                       "start": start, "mod": mod, "norm": norm, "hT": hT_, "zA": zA_, "kv": kv, "zF": zF, "four": four, "q": q_, "att": att,
                       "gate": gate, "out": out_, "pq": pq, "gather": gather, "fin": fin}
            for name, *args in ORDER + ORDER2:
                if name in program:
                    program[name](*args)
            assert chunk_no[0] == len(plan) == len(chunk_done)
            assert chunk2_no[0] == len(plan_2) == len(chunk2_done)

        @block.scalar
        def _(act):
            own = [0]

            def alone(ins):
                own[0] += 1
                ins.then_inc(act_step, 1)
                act.wait_ge(act_step, own[0])

            def copy(dst, src, key, scale=None):
                release(act.activation(dst, src, ACT.Copy) if scale is None else act.activation(dst, src, ACT.Copy, scale=scale), key)

            def squares(src, n, scratch):
                return act.activation(scratch, src, ACT.Square, accum_out=ss[:, n:n + 1])

            def start():
                act.wait_ge(ld_const, 16 * 6)
                act.activation(cth[:, :, :], cvec[:, :, :], ACT.Tanh, scale=0.5).then_inc(silu_t, 1)

            def norm(run, k):
                s = RUNS[run][0]
                if k:
                    at_mark(act, "resid", run, 4)
                elif RUNS[run][1] == 0:
                    act.wait_ge((ld_x, ld_c)[s], 16)
                else:
                    at_mark(act, "fin", ("x0", "c0")[s], 2)
                for t in range(TT):
                    squares(x[s][:, t, :], t, h[s][:, t, :]).then_inc(mark["ss"], 1)

            def hT_(run, k):
                s = RUNS[run][0]
                for a in range(2):
                    for t in range(TT):
                        key = ("hT", run, k, t, a)
                        b = at_mm(act, key)
                        copy(hT[:, 4 * a:4 * a + 4, t * P:(t + 1) * P], b.rearrange("p (j n) -> p j n", j=4), key)

            def zA_(run):
                s = RUNS[run][0]
                for t in range(TT):
                    key = ("zA", run, t)
                    b = at_mm(act, key)
                    copy(zA[s][:, t, :], b[:, 0:WA], key)

            def kv(run):
                s, l = RUNS[run]
                for t in range(TT):
                    at_evac(act, ("zA", run, t))
                    squares(zA[s][:, t, QLORA:QLORA + KVLORA], 2 + t, ckn[:, t, :]).then_inc(mark["kvss"], 1)
                key = ("ckT", run)
                b = at_mm(act, key)
                release(act.activation(ckT[:, :], b[:, 0:TOK], ACT.Copy, scale=vecs[:, 29 * l:29 * l + 1]), key)
                for t in range(TT):
                    for half in range(2):
                        key = ("kv", run, t, half)
                        b = at_mm(act, key).rearrange("p (h n) -> p h n", h=4)
                        kd = kfull[:, t, half * 4 * QK:(half + 1) * 4 * QK].rearrange("p (h n) -> p h n", h=4)
                        act.activation(kd[:, :, 0:NOPE], b[:, :, 0:NOPE], ACT.Copy)
                        ko = (0 if s else TT) + t
                        copy(vv[:, ko, half * 4 * VH:(half + 1) * 4 * VH].rearrange("p (h n) -> p h n", h=4), b[:, :, NOPE:NOPE + VH], key)
                for t in range(TT):
                    for hq in range(2):
                        key = ("kT", run, t, hq)
                        b = at_mm(act, key)[0:QK, :].rearrange("p (h n) -> p h n", h=4)
                        ko = ((0 if s else TT) + t) * P
                        copy(kT[0:QK, 4 * hq:4 * hq + 4, ko:ko + P], b, key)

            def zF(run):
                for t in range(TT):
                    key = ("zF", run, t)
                    copy(zfp[:, t, :], at_mm(act, key), key)

            def four(run):
                for ft in range(2):
                    key = ("T1", run, ft)
                    copy(T1[:, ft, :], at_mm(act, key), key)
                copy(poolT, at_mm(act, ("P", run)), ("P", run))
                copy(YT[:, :], at_mm(act, ("Y", run)), ("Y", run))
                b = at_mm(act, ("G", run))
                l = RUNS[run][1]
                for pair in range(2):
                    last = act.activation(ypT[:, pair * TOK:(pair + 1) * TOK], b[:, pair * TOK:(pair + 1) * TOK], ACT.Copy,
                                          scale=vecs[:, 29 * l + 3 + pair:29 * l + 4 + pair])
                release(last, ("G", run))

            def q_(run):
                s, l = RUNS[run]
                for t in range(TT):
                    squares(zA[s][:, t, 0:QLORA], 4 + t, cqn[:, t, :]).then_inc(mark["qss"], 1)
                b = at_mm(act, ("cqT", run))
                for k in range(2):
                    last = act.activation(cqT[:, k, :], b[:, k * TOK:(k + 1) * TOK], ACT.Copy, scale=vecs[:, 29 * l + 1 + k:29 * l + 2 + k])
                release(last, ("cqT", run))
                for t in range(TT):
                    for half in range(2):
                        key = ("q", run, t, half)
                        copy(q[:, t, half * 384:(half + 1) * 384], at_mm(act, key)[:, 0:384], key)
                for t in range(TT):
                    for hq in range(2):
                        key = ("qT", run, t, hq)
                        b = at_mm(act, key)[0:QK, :].rearrange("p (h n) -> p h n", h=4)
                        copy(qT[0:QK, 4 * hq:4 * hq + 4, t * P:(t + 1) * P], b, key, scale=ATT_SCALE)

            def att(run):
                nk = 4 if RUNS[run][0] == 0 else 2

                def exps(hh):
                    for t in range(TT):
                        key = ("s", run, hh, t)
                        at_mark(act, "nmax", run, 2 * hh + t + 1)
                        if hh >= 2:
                            act.wait_ge(mm_done, mm_at["pT", run, hh - 2, t])
                        c = 2 * (hh % 2) + t
                        release(act.activation(pr[:, hh % 2, t, 0:nk * P], at_mm(act, key)[:, 0:nk * P], ACT.Exp,
                                               bias=nmax[:, c:c + 1], accum_out=rsum[:, c:c + 1]), key)

                exps(0)
                for hh in range(H):
                    if hh + 1 < H:
                        exps(hh + 1)
                    for t in range(TT):
                        key = ("pT", run, hh, t)
                        b = at_mm(act, key)[:, 0:nk * P].rearrange("p (k n) -> p k n", k=nk)
                        copy(pT[:, 0:nk, t * P:(t + 1) * P], b, key)
                    if hh % 2:
                        key = ("pv", run, hh // 2)
                        copy(attT[:, hh // 2, :], at_mm(act, key)[:, 0:TOK], key)

            def gate(run):
                l = RUNS[run][1]
                for dp in range(4):
                    if dp:
                        at_mark(act, "mixT", run, dp)
                    for j in range(3):
                        key = ("g", run, dp, j)
                        b = at_mm(act, key)
                        for dt in range(2):
                            c = j * 8 + dp * 2 + dt
                            last = act.activation(sg[:, j, dt * TOK:(dt + 1) * TOK], b[:, dt * TOK:(dt + 1) * TOK], ACT.Tanh,
                                                  bias=hbg[:, l, c:c + 1], scale=0.5)
                        release(last, key)

            def out_(run):
                for half in range(2):
                    key = ("bm", run, half)
                    copy(mb[:, half * 512:(half + 1) * 512], at_mm(act, key), key, scale=0.5)

            def pq(run):
                prev = {"x0": None, "c0": "x0", "x1": "c0"}[run]
                for c in range(9):
                    if c < 8:
                        key = ("qp", run, c)
                        copy(qpT[:, c % 2, :], at_mm(act, key), key)
                    if c:
                        key = ("sc", run, c - 1)
                        b = at_mm(act, key).rearrange("p (t n) -> p t n", t=TT)
                        copy(s_sb[:, :, (c - 1) * 256:c * 256], b, key)

            def route(run, t):
                at_mark(act, "topd", run, t + 1)
                act.activation(te, te, ACT.Exp).then_inc(mark["tope"], 1)

            def gather(run, t):
                G = GATHER_NO[run, t]

                def diags(g):
                    act.wait_ge(act_ready, g + (GROUPS * G + 1))
                    for j in range(GROUP):
                        if not (isinstance(g, int) and g == 0 and j < DIAGS and G == 0):
                            act.wait_ge(upp_done, 8 * g + (P * G - DIAGS + j + 1))
                        act.activation(diag[:, j % DIAGS, :], ident[:, :], ACT.Copy, scale=act8[:, j:j + 1]).then_inc(diag_ready, 1)

                def tanh(g):
                    act.wait_ge(gelu_in, g + (GROUPS * G + 1))
                    act.activation(th8[:, :], g2[:, :], ACT.Tanh, scale=GELU_C).then_inc(gelu_th, 1)

                tanh(0)
                diags(0)
                tanh(1)
                with act.Fori(2, GROUPS) as g:
                    diags(g - 1)
                    tanh(g)
                diags(GROUPS - 1)

            def fin(run, t):
                for half in range(2):
                    key = ("bf", run, t, half)
                    copy(mb[:, half * 512:(half + 1) * 512], at_mm(act, key), key, scale=0.5)

            def final():
                at_mark(act, "fin", "x1", 2)
                for t in range(TT):
                    squares(x[0][:, t, :], t, h[0][:, t, :]).then_inc(mark["ss"], 1)

            def pre(tag):
                act.wait_ge(x2, x2_before(tag))
                for t in range(TT):
                    squares(x[0][:, t, :], t, h[0][:, t, :]).then_inc(ss2, 1)

            def hT2(tag):
                for gi, dst in enumerate([hkT, hT] if tag == "at" else [hT]):
                    for t in range(TT):
                        for a in range(2):
                            key = ("hT2", tag, gi, t, a)
                            copy(dst[:, 4 * a:4 * a + 4, t * P:(t + 1) * P], at_mm(act, key).rearrange("p (j n) -> p j n", j=4), key)

            def gu(tag):
                m0, r0 = gu_base[tag]
                with act.Fori(0, FP_ // 2) as i:
                    for j in range(4):
                        b = ROT2[(r0 + j) % 4]
                        act.wait_ge(mm_done, 4 * i + (m0 + j + 1))
                        act.activation(fth[:, j, :], ps[:, b, 0:TOK], ACT.Tanh, scale=0.5).then_inc(gate_th, 1)
                for j in range(2):
                    act.activation(fth[:, j, :], at_mm(act, ("gu", tag, j))[:, 0:TOK], ACT.Tanh, scale=0.5).then_inc(gate_th, 1)

            def post(tag):
                for t in range(TT):
                    for half in range(2):
                        cols = slice(half * 512, (half + 1) * 512)
                        if tag == "cv":
                            act.wait_ge(bout_y, 2 * t + half + 1)
                            src, scratch = h[1][:, t, cols], h[0][:, t, cols]
                        else:
                            src, scratch = at_mm(act, ("d", tag, t, half)), h[1][:, t, cols]
                        squares(src, 2 * t + half, scratch).then_inc(ss2, 1)

            def cin():
                act.wait_ge(conv_h, 1)
                for c in range(8):
                    b = at_mm(act, ("cin", c))
                    if c >= 2:
                        act.wait_ge(conv_u, c - 1)
                    act.activation(ctmp[:, c % 2, :], b[:, TOK:2 * TOK], ACT.Tanh, bias=vec2[:, 8 + c:9 + c], scale=0.5).then_inc(conv_th, 1)

            def ln():
                act.wait_ge(ln_d, 1)
                act.activation(usq, uc, ACT.Square).then_inc(ln_v, 1)
                act.wait_ge(ln_d, 2)
                for c in range(8):
                    act.activation(usq[:, c, :], uc[:, c, :], ACT.Identity, bias=vec2[:, 280 + c:281 + c], scale=vec2[:, 272 + c:273 + c]).then_inc(ln_z, 1)
                act.wait_ge(ln_z, 8)
                act.activation(uth, usq, ACT.Tanh).then_inc(ln_t, 1)

            def qkv():
                for c in range(4):
                    b = at_mm(act, ("k2", c)).rearrange("p (h n) -> p h n", h=2)
                    copy(kT2[:, 2 * c:2 * c + 2, :], b, ("k2", c))
                for half in range(2):
                    for t in range(TT):
                        key = ("v2", "at", t, half)
                        copy(v2[:, t, half * 512:(half + 1) * 512], at_mm(act, key), key)
                for c in range(4):
                    b = at_mm(act, ("q2", c)).rearrange("p (h n) -> p h n", h=2)
                    copy(qT2[:, 2 * c:2 * c + 2, :], b, ("q2", c), scale=DH ** -0.5)

            def moba():
                def exps(hh):
                    for t in range(TT):
                        c = 2 * (hh % 2) + t
                        act.wait_ge(s2_ready, 2 * hh + t + 1)
                        pp = p2[:, hh % 2, t, :]
                        act.activation(pp, pp, ACT.Exp, bias=nmax[:, c:c + 1], accum_out=rsum[:, c:c + 1]).then_inc(act_step, 1)

                exps(0)
                for hh in range(H2):
                    if hh + 1 < H2:
                        exps(hh + 1)
                    copy(pT2.rearrange("p k n -> p (k n)"), at_mm(act, ("pT2", hh)), ("pT2", hh))
                    copy(attT2[:, hh, :], at_mm(act, ("pv2", hh))[:, 0:TOK], ("pv2", hh))

            program = {"pre": pre, "hT2": hT2, "gu": gu, "post": post, "cin": cin, "ln": ln, "qkv": qkv, "moba": moba,
                       "start": start, "norm": norm, "hT": hT_, "zA": zA_, "kv": kv, "zF": zF, "four": four, "q": q_, "att": att,
                       "gate": gate, "out": out_, "pq": pq, "route": route, "gather": gather, "fin": fin, "final": final}
            for name, *args in ORDER + ORDER2:
                if name in program:
                    program[name](*args)

        @block.vector
        def _(dve):
            own = [0]

            def v(ins):
                own[0] += 1
                ins.then_inc(dve_step, 1)
                dve.wait_ge(dve_step, own[0])

            def rsqrt(dst, src, n, width):
                var, t, y = nwt[:, 0:n], nwt[:, 2:2 + n], nwi[:, 2:2 + n].bitcast(f32)
                v(dve.tensor_scalar(var, src, 1.0 / width, EPS, ALU.mult, ALU.add))
                v(dve.tensor_single_scalar(nwi[:, 0:n], var.bitcast(i32), 1, ALU.logical_shift_right))
                v(dve.tensor_scalar(nwi[:, 2:2 + n], nwi[:, 0:n], -1.0, 1597463007.0, ALU.mult, ALU.add))
                for i in range(4):
                    v(dve.tensor_tensor(t, y, y, ALU.mult))
                    v(dve.tensor_tensor(t, t, var, ALU.mult))
                    v(dve.tensor_scalar(t, t, -0.5, 1.5, ALU.mult, ALU.add))
                    v(dve.tensor_tensor(dst if i == 3 else y, y, t, ALU.mult))

            def start():
                dve.wait_ge(ld_const, 16 * 6)
                v(dve.tensor_scalar(hbg[:, :, :], vecs[:, :].rearrange("p (l n) -> p l n", l=2)[:, :, 5:29], 0.5, None, ALU.mult))
                dve.wait_ge(silu_t, 1)
                v(dve.scalar_tensor_tensor(cth[:, :, :], cth[:, :, :], 1.0, cvec[:, :, :], ALU.add, ALU.mult))
                dve.tensor_scalar(cvec[:, :, :], cth[:, :, :], 0.5, None, ALU.mult).then_inc(silu_c, 1)

            def mod(l):
                dve.wait_ge(ld_mrow, 16 * (l + 1))
                for cc in range(12):
                    key = ("mod", l, cc)
                    b = at_mm(dve, key)
                    qd, a = 32 * (cc % 4), cc // 4
                    m = mrows[l][qd:qd + 2, a, :]
                    release(dve.tensor_tensor(m, m, b[qd:qd + 2, :], ALU.add), key)

            gains = [0]

            def norm(run, k):
                s = RUNS[run][0]
                dve.wait_ge(mark["ss"], norm_mark(run, k, 2))
                rsqrt(ss[:, 6:8], ss[:, 0:2], 2, D)
                gains[0] += 1
                dve.wait_ge(ld_gain, 16 * gains[0])
                for half in range(2):
                    cols = slice(half * 512, (half + 1) * 512)
                    key = ("bs", run, k, half)
                    b = at_mm(dve, key)
                    release(dve.scalar_tensor_tensor(amul[:, cols], b, 1.0, gain[:, cols], ALU.add, ALU.mult), key)
                for half in range(2):
                    at_evac(dve, ("bs", run, k, half))
                for t in range(TT):
                    ins = dve.scalar_tensor_tensor(h[s][:, t, :], x[s][:, t, :], ss[:, 6 + t:7 + t], amul[:, :], ALU.mult, ALU.mult)
                    if t == TT - 1:
                        ins.then_inc(gain_used, 1)
                        dve.wait_ge(gain_used, gains[0])
                    else:
                        v(ins)
                for half in range(2):
                    cols = slice(half * 512, (half + 1) * 512)
                    key = ("bh", run, k, half)
                    b = at_mm(dve, key)
                    dve.tensor_tensor(h[s][:, 0, cols], h[s][:, 0, cols], b, ALU.add).then_inc(mark["h"], 1)
                    release(dve.tensor_tensor(h[s][:, 1, cols], h[s][:, 1, cols], b, ALU.add), key)

            def rotate(src, dst, t, heads, signal):
                cs = rope[:, t, 0:16].rearrange("p (r e) -> p r e", r=2).unsqueeze(1).broadcast_to([P, heads, 2, 8])
                sn = rope[:, t, 16:32].rearrange("p (r e) -> p r e", r=2).unsqueeze(1).broadcast_to([P, heads, 2, 8])
                s5 = src.rearrange("p h (r two e) -> p h r two e", r=2, two=2)
                d5 = dst.rearrange("p h (r two e) -> p h r two e", r=2, two=2)
                t4 = [rtmp[:, n, 0:heads * 16].rearrange("p (h r e) -> p h r e", h=heads, r=2) for n in range(4)]
                dve.tensor_tensor(t4[0], s5[:, :, :, 0, :], cs, ALU.mult)
                dve.tensor_tensor(t4[1], s5[:, :, :, 1, :], sn, ALU.mult)
                dve.tensor_tensor(t4[2], s5[:, :, :, 0, :], sn, ALU.mult)
                v(dve.tensor_tensor(t4[3], s5[:, :, :, 1, :], cs, ALU.mult))
                dve.tensor_tensor(d5[:, :, :, 0, :], t4[0], t4[1], ALU.subtract)
                signal(dve.tensor_tensor(d5[:, :, :, 1, :], t4[2], t4[3], ALU.add))

            def kv(run):
                s = RUNS[run][0]
                at_mark(dve, "kvss", run, 2)
                rsqrt(ss[:, 6:8], ss[:, 2:4], 2, KVLORA)
                for t in range(TT):
                    dve.tensor_scalar(ckn[:, t, :], zA[s][:, t, QLORA:QLORA + KVLORA], ss[:, 6 + t:7 + t], None, ALU.mult).then_inc(mark["ckn"], 1)
                for t in range(TT):
                    kr = zA[s][:, t, QLORA + KVLORA:WA].unsqueeze(1)
                    if s == 0:
                        rotate(kr, kr, t, 1, v)
                    kd = kfull[:, t, :].rearrange("p (h n) -> p h n", h=H)
                    dve.tensor_copy(kd[:, :, NOPE:QK], kr.broadcast_to([P, H, ROPE])).then_inc(mark["krr"], 1)

            def q_(run):
                s = RUNS[run][0]
                at_mark(dve, "qss", run, 2)
                rsqrt(ss[:, 6:8], ss[:, 4:6], 2, QLORA)
                for t in range(TT):
                    dve.tensor_scalar(cqn[:, t, :], zA[s][:, t, 0:QLORA], ss[:, 6 + t:7 + t], None, ALU.mult).then_inc(mark["cqn"], 1)
                if s == 0:
                    for t in range(TT):
                        for half in range(2):
                            at_evac(dve, ("q", run, t, half))
                        qv = q[:, t, :].rearrange("p (h n) -> p h n", h=H)[:, :, NOPE:QK]
                        rotate(qv, qv, t, H, lambda ins: ins.then_inc(mark["qr"], 1))
                        at_mark(dve, "qr", run, t + 1)

            def att(run):
                nk = 4 if RUNS[run][0] == 0 else 2

                def maxima(hh):
                    for t in range(TT):
                        key = ("s", run, hh, t)
                        c = 2 * (hh % 2) + t
                        dve.tensor_reduce(nmax[:, c:c + 1], at_mm(dve, key)[:, 0:nk * P], axis=AX.X, op=ALU.max, negate=True).then_inc(mark["nmax"], 1)

                maxima(0)
                for hh in range(H):
                    for t in range(TT):
                        at_evac(dve, ("s", run, hh, t))
                        c = 2 * (hh % 2) + t
                        v(dve.reciprocal(rinv[:, c:c + 1], rsum[:, c:c + 1]))
                        pp = pr[:, hh % 2, t, 0:nk * P]
                        dve.tensor_scalar(pp, pp, rinv[:, c:c + 1], None, ALU.mult).then_inc(mark["pn"], 1)
                    if hh + 1 < H:
                        maxima(hh + 1)

            def gate(run):
                for dp in range(4):
                    for j in range(3):
                        key = ("y", run, dp, j)
                        at_evac(dve, ("g", run, dp, j))
                        b = at_mm(dve, key)
                        m = mixT[:, 2 * dp:2 * dp + 2, :].rearrange("p k n -> p (k n)")
                        release(dve.scalar_tensor_tensor(mtmp if j else m, sg[:, j, :], 1.0, b, ALU.add, ALU.mult), key)
                        at_evac(dve, key)
                        if j == 1:
                            v(dve.tensor_tensor(m, m, mtmp, ALU.add))
                        elif j == 2:
                            dve.tensor_tensor(m, m, mtmp, ALU.add).then_inc(mark["mixT"], 1)

            def out_(run):
                s = RUNS[run][0]
                for half in range(2):
                    cols = slice(half * 512, (half + 1) * 512)
                    at_evac(dve, ("bm", run, half))
                    for t in range(TT):
                        key = ("o", run, half, t)
                        b = at_mm(dve, key)
                        release(dve.tensor_tensor(amul[:, t * 512:(t + 1) * 512], b, mb[:, cols], ALU.mult), key)
                        at_evac(dve, key)
                        dve.tensor_tensor(x[s][:, t, cols], x[s][:, t, cols], amul[:, t * 512:(t + 1) * 512], ALU.add).then_inc(mark["resid"], 1)

            def top16(val, ind, src):
                v(dve.max(val[:, 0:8], src))
                dve.max_index(ind[:, 0:8], val[:, 0:8], src)
                v(dve.match_replace(src, val[:, 0:8], src, NEG))
                v(dve.max(val[:, 8:16], src))
                v(dve.max_index(ind[:, 8:16], val[:, 8:16], src))

            def route(run, t):
                l = RUNS[run][1]
                for c in range(8):
                    at_evac(dve, ("sc", run, c))
                for i in range(HP):
                    top16(sv[:, i, :], si[:, i, :], s_sb[:, t, i * KEYS:(i + 1) * KEYS])
                v(dve.tensor_copy(sif, si))
                sv4 = sv.rearrange("p (h two) k -> p h two k", two=2)
                sf4 = sif.rearrange("p (h two) k -> p h two k", two=2)
                for hh in range(H):
                    c3 = cand[:, hh * 256:(hh + 1) * 256].rearrange("p (a b) -> p a b", a=TOP)
                    v(dve.tensor_tensor(c3, sv4[:, hh, 0, :].unsqueeze(2).broadcast_to([P, TOP, TOP]),
                                        sv4[:, hh, 1, :].unsqueeze(1).broadcast_to([P, TOP, TOP]), ALU.add))
                for hh in range(H):
                    top16(ts[:, hh, :], pos[:, hh, :], cand[:, hh * 256:(hh + 1) * 256])
                v(dve.tensor_tensor(te, ts, ts[:, :, 0:1].broadcast_to([P, H, TOP]), ALU.subtract))
                posf = pos.rearrange("p h k -> p (h k)")
                v(dve.tensor_single_scalar(pa, posf, 4, ALU.logical_shift_right))
                v(dve.tensor_copy(fa, pa))
                v(dve.tensor_single_scalar(pa, posf, TOP - 1, ALU.bitwise_and))
                dve.tensor_copy(fb, pa).then_inc(mark["topd"], 1)
                at_mark(dve, "topd", run, t + 1)
                e3 = eq.rearrange("p (n k) -> p n k", k=TOP)
                e4 = eq.rearrange("p (h n k) -> p h n k", h=H, k=TOP)
                for which, f, i_ in ((0, fa, ia), (1, fb, ib)):
                    v(dve.tensor_tensor(e3, f.unsqueeze(2).broadcast_to([P, P, TOP]), iota[:, :].unsqueeze(1).broadcast_to([P, P, TOP]), ALU.is_equal))
                    v(dve.tensor_tensor(e4, e4, sf4[:, :, which, :].unsqueeze(2).broadcast_to([P, H, TOP, TOP]), ALU.mult))
                    v(dve.tensor_reduce(i_, e3, axis=AX.X, op=ALU.add))
                v(dve.scalar_tensor_tensor(ia, ia, float(KEYS), ib, ALU.mult, ALU.add))
                v(dve.tensor_scalar(idx[t][:, :], ia, float(l * KEYS * KEYS), None, ALU.add))
                at_mark(dve, "tope", run, t + 1)
                v(dve.tensor_reduce(tsum, te, axis=AX.X, op=ALU.add))
                v(dve.reciprocal(tsum, tsum))
                dve.tensor_tensor(gates[t][:, :].rearrange("p (h k) -> p h k", k=TOP), te,
                                  tsum.unsqueeze(2).broadcast_to([P, H, TOP]), ALU.mult).then_inc(mark["route"], 1)

            def gather(run, t):
                s = RUNS[run][0]
                G = GATHER_NO[run, t]
                at_mark(dve, "route", run, t + 1)
                v(dve.memset(accv[:, :], 0.0))

                def down(g, first=False):
                    for j in range(GROUP):
                        dve.wait_ge(row_in[j], (16 * (32 * G + 1)) if first else 32 * g + 16 * (32 * G))
                        dve.tensor_tensor_reduce(out=rows[:, j, :], in0=rows[:, j, :], in1=h[s][:, t, :], scale=1.0, scalar=0.0,
                                                 op0=ALU.mult, op1=ALU.add, accum_out=a8[:, j:j + 1]).then_inc(down_done, 1)
                    base = 3 * GROUPS * G
                    dve.wait_ge(down_done, 8 * g + (P * G + GROUP))
                    dve.tensor_tensor(g1[:, :], a8[:, :], a8[:, :], ALU.mult).then_inc(gelu_step, 1)
                    dve.wait_ge(gelu_step, 3 * g + (base + 1))
                    dve.tensor_scalar(g1[:, :], g1[:, :], GELU_A, 1.0, ALU.mult, ALU.add).then_inc(gelu_step, 1)
                    dve.wait_ge(gelu_step, 3 * g + (base + 2))
                    dve.tensor_tensor(g2[:, :], g1[:, :], a8[:, :], ALU.mult).then_inc(gelu_in, 1)

                def up(g, last=False):
                    for j in range(GROUP):
                        dve.wait_ge(row_in[j], (16 * (32 * G + 32)) if last else 32 * g + (16 * (32 * G + 3)))
                        if isinstance(g, int) and g == 0 and j == 0:
                            dve.wait_ge(act_ready, GROUPS * G + 1)
                        else:
                            dve.wait_ge(upv_done, 8 * g + (P * G + j))
                        dve.scalar_tensor_tensor(accv[:, :], rows[:, j, 0:UPV], act8[:, j:j + 1], accv[:, :], ALU.mult, ALU.add).then_inc(upv_done, 1)

                def act_of(g, first=False):
                    base = 3 * GROUPS * G
                    dve.wait_ge(gelu_th, g + (GROUPS * G + 1))
                    dve.scalar_tensor_tensor(g1[:, :], th8[:, :], 1.0, a8[:, :], ALU.add, ALU.mult).then_inc(gelu_step, 1)
                    dve.wait_ge(gelu_step, 3 * g + (base + 3))
                    if not first:
                        dve.wait_ge(diag_ready, 8 * g + P * G)
                        dve.wait_ge(upv_done, 8 * g + P * G)
                    gt = gates[t][:, 0:GROUP] if first else gates[t][:, bass.ds(g * GROUP, GROUP)]
                    dve.tensor_tensor(act8[:, :], g1[:, :], gt, ALU.mult).then_inc(act_ready, 1)
                    dve.wait_ge(act_ready, g + (GROUPS * G + 1))

                down(0, True)
                act_of(0, True)
                down(1)
                up(0)
                act_of(1)
                with dve.Fori(2, GROUPS) as g:
                    down(g)
                    up(g - 1)
                    act_of(g)
                up(GROUPS - 1, True)

            def fin(run, t):
                s = RUNS[run][0]
                G = GATHER_NO[run, t]
                for half in range(2):
                    at_evac(dve, ("bf", run, t, half))
                dve.wait_ge(upv_done, P * (G + 1))
                v(dve.tensor_tensor(accv[:, :], accv[:, :], mb[:, 0:UPV], ALU.mult))
                dve.wait_ge(upp_done, P * (G + 1))
                v(dve.tensor_tensor(mb[:, UPV:D], ps[:, UPB, :], mb[:, UPV:D], ALU.mult))
                v(dve.tensor_tensor(x[s][:, t, 0:UPV], x[s][:, t, 0:UPV], accv[:, :], ALU.add))
                dve.tensor_tensor(x[s][:, t, UPV:D], x[s][:, t, UPV:D], mb[:, UPV:D], ALU.add).then_inc(mark["fin"], 1)
                at_mark(dve, "fin", run, t + 1)

            def final():
                dve.wait_ge(mark["ss"], 2 * 8)
                rsqrt(ss[:, 6:8], ss[:, 0:2], 2, D)
                gains[0] += 1
                dve.wait_ge(ld_gain, 16 * gains[0])
                for t in range(TT):
                    dve.scalar_tensor_tensor(x[0][:, t, :], x[0][:, t, :], ss[:, 6 + t:7 + t], gain[:, :], ALU.mult, ALU.mult).then_inc(x2, 1)

            g2n = [0]

            def next_gain():
                n = g2n[0]
                g2n[0] += 1
                dve.wait_ge(gain2_in[n % 2], 16 * (n // 2 + 1))
                return gain2[n % 2]

            def pre(tag):
                dve.wait_ge(ss2, SS2_AT["pre", tag])
                rsqrt(ss[:, 6:8], ss[:, 0:2], 2, D)
                for dst in ([h[1], h[0]] if tag == "at" else [h[0]]):
                    g = next_gain()
                    for t in range(TT):
                        dve.scalar_tensor_tensor(dst[:, t, :], x[0][:, t, :], ss[:, 6 + t:7 + t], g[:, :], ALU.mult, ALU.mult).then_inc(h2m, 1)
                    dve.wait_ge(h2m, H2_AT[tag] - (2 if dst is h[1] else 0))
                    dve.sem_inc(gain2_used, 1)

            def gu(tag):
                m0, r0 = gu_base[tag]
                n = int(tag[1])
                done = FT * n

                def silu_up(b, j, kt, th_at, step_at):
                    dve.wait_ge(gate_th, th_at)
                    dve.scalar_tensor_tensor(ft2[:, j, :], fth[:, j, :], 1.0, ps[:, b, 0:TOK], ALU.add, ALU.mult).then_inc(gu_step, 1)
                    dve.wait_ge(gu_step, step_at)
                    return dve.tensor_tensor(hid[:, kt, :] if isinstance(kt, int) else hid[:, bass.ds(kt, 1), :], ft2[:, j, :] if isinstance(kt, int) else ft2[:, j:j + 1, :],
                                             ps[:, b, TOK:2 * TOK] if isinstance(kt, int) else ps[:, b:b + 1, TOK:2 * TOK], ALU.mult)

                with dve.Fori(0, FP_ // 2) as i:
                    for j in range(4):
                        b = ROT2[(r0 + j) % 4]
                        ins = silu_up(b, j, 4 * i + j, 4 * i + (done + j + 1), 8 * i + (2 * done + 2 * j + 1))
                        ins.then_inc(gu_step, 1)
                        dve.wait_ge(gu_step, 8 * i + (2 * done + 2 * j + 2))
                        dve.sem_inc(bank_free[b], 1)
                for j in range(2):
                    key = ("gu", tag, j)
                    ins = silu_up(job_bank[key], j, FT - 2 + j, done + FT - 1 + j, 2 * (done + FT) - 3 + 2 * j)
                    ins.then_inc(gu_step, 1)
                    dve.wait_ge(gu_step, 2 * (done + FT) - 2 + 2 * j)
                    dve.sem_inc(bank_free[job_bank[key]], 1)

            def post(tag):
                ffn = tag[0] == "f"
                if tag == "cv":
                    for t in range(TT):
                        for half in range(2):
                            cols = slice(half * 512, (half + 1) * 512)
                            key = ("d", tag, t, half)
                            dve.tensor_tensor(h[1][:, t, cols], at_mm(dve, key), bout_b[:, cols], ALU.add).then_inc(bout_y, 1)
                            dve.wait_ge(bout_y, 2 * t + half + 1)
                            dve.sem_inc(bank_free[job_bank[key]], 1)
                g = next_gain()
                dve.wait_ge(ss2, SS2_AT["post", tag])
                s4 = ss[:, 0:4].rearrange("p (t a) -> p t a", t=TT)
                v(dve.tensor_tensor(nwt[:, 4:6], s4[:, :, 0], s4[:, :, 1], ALU.add))
                rsqrt(ss[:, 6:8], nwt[:, 4:6], 2, (4 if ffn else 1) * D)
                if ffn:
                    v(dve.tensor_scalar(ss[:, 6:8], ss[:, 6:8], 0.25, None, ALU.mult))
                for t in range(TT):
                    for half in range(2):
                        cols = slice(half * 512, (half + 1) * 512)
                        key = ("d", tag, t, half)
                        src = h[1][:, t, cols] if tag == "cv" else at_mm(dve, key)
                        v(dve.scalar_tensor_tensor(h[1][:, t, cols], src, ss[:, 6 + t:7 + t], g[:, cols], ALU.mult, ALU.mult))
                        if tag != "cv":
                            dve.sem_inc(bank_free[job_bank[key]], 1)
                    if t == TT - 1:
                        dve.sem_inc(gain2_used, 1)
                    dve.tensor_tensor(x[0][:, t, :], x[0][:, t, :], h[1][:, t, :], ALU.add).then_inc(x2, 1)
                dve.wait_ge(x2, X2_AT[tag])

            def cin():
                dve.wait_ge(ld_vec2, 16 * 2)
                v(dve.memset(upad[:, :, 0:PAD], 0.0))
                dve.memset(ones, 1.0 / D).then_inc(ones_set, 1)
                v(dve.tensor_scalar(vec2[:, 8:16], vec2[:, 8:16], 0.5, None, ALU.mult))
                dve.tensor_scalar(vec2[:, 272:288], vec2[:, 272:288], 0.5, None, ALU.mult).then_inc(conv_h, 1)
                for c in range(8):
                    key = ("cin", c)
                    b = at_mm(dve, key)
                    tmp = rows[:, 2, 512:512 + TOK]
                    dve.wait_ge(conv_th, c + 1)
                    v(dve.tensor_scalar(tmp, b[:, 0:TOK], vec2[:, c:c + 1], 0.5, ALU.add, ALU.mult))
                    dve.scalar_tensor_tensor(upad[:, c, PAD:PAD + TOK], ctmp[:, c % 2, :], 1.0, tmp, ALU.add, ALU.mult).then_inc(conv_u, 1)
                    dve.wait_ge(conv_u, c + 1)
                    dve.sem_inc(bank_free[job_bank[key]], 1)
                    for j in range(TAPS):
                        w = vec2[:, 16 + j * 8 + c:17 + j * 8 + c]
                        if j == 0:
                            v(dve.tensor_scalar(uc[:, c, :], upad[:, c, 0:TOK], w, vec2[:, 264 + c:265 + c], ALU.mult, ALU.add))
                        else:
                            ins = dve.scalar_tensor_tensor(uc[:, c, :], upad[:, c, j:j + TOK], w, uc[:, c, :], ALU.mult, ALU.add)
                            if j < TAPS - 1:
                                v(ins)
                            else:
                                ins.then_inc(conv_y, 1)
                                dve.wait_ge(conv_y, c + 1)

            def ln():
                b = at_mm(dve, ("mean",))
                bc = b[:, 0:TOK].unsqueeze(1).broadcast_to([P, 8, TOK])
                dve.tensor_tensor(uc, uc, bc, ALU.subtract).then_inc(ln_d, 1)
                dve.wait_ge(ln_d, 1)
                dve.sem_inc(bank_free[job_bank["mean",]], 1)
                b = at_mm(dve, ("var",))
                v(dve.tensor_scalar(rl2, b[:, 0:TOK], LN_EPS, None, ALU.add))
                dve.sem_inc(bank_free[job_bank["var",]], 1)
                y = rli.bitcast(f32)
                v(dve.tensor_single_scalar(rli2, rl2.bitcast(i32), 1, ALU.logical_shift_right))
                v(dve.tensor_scalar(rli, rli2, -1.0, 1597463007.0, ALU.mult, ALU.add))
                for i in range(4):
                    v(dve.tensor_tensor(rln, y, y, ALU.mult))
                    v(dve.tensor_tensor(rln, rln, rl2, ALU.mult))
                    v(dve.tensor_scalar(rln, rln, -0.5, 1.5, ALU.mult, ALU.add))
                    v(dve.tensor_tensor(y, y, rln, ALU.mult))
                dve.wait_ge(ln_v, 1)
                dve.tensor_tensor(uc, uc, y.unsqueeze(1).broadcast_to([P, 8, TOK]), ALU.mult).then_inc(ln_d, 1)
                dve.wait_ge(ln_t, 1)
                dve.scalar_tensor_tensor(uth, uth, 1.0, usq, ALU.add, ALU.mult).then_inc(ln_s, 1)

            def moba():
                dve.wait_ge(ld_vec2, 16 * 3)
                e0 = [0]

                def biased(hh):
                    for t in range(TT):
                        c = 2 * (hh % 2) + t
                        b = at_mm(dve, ("s2", hh))
                        if hh >= 2:
                            dve.wait_ge(mm_done, mm_at["pT2", hh - 2])
                        pp = p2[:, hh % 2, t, :]
                        v(dve.scalar_tensor_tensor(pp, dist[:, t, :], -(2.0 ** -(hh + 1)), b[:, t * TOK:(t + 1) * TOK], ALU.mult, ALU.add))
                        if t:
                            dve.sem_inc(bank_free[job_bank["s2", hh]], 1)
                        dve.tensor_reduce(nmax[:, c:c + 1], pp, axis=AX.X, op=ALU.max, negate=True).then_inc(s2_ready, 1)

                biased(0)
                for hh in range(H2):
                    if hh + 1 < H2:
                        biased(hh + 1)
                    for t in range(TT):
                        c = 2 * (hh % 2) + t
                        dve.wait_ge(act_step, 2 * hh + t + 1)
                        v(dve.reciprocal(rinv[:, c:c + 1], rsum[:, c:c + 1]))
                        pp = p2[:, hh % 2, t, :]
                        dve.tensor_scalar(pp, pp, rinv[:, c:c + 1], None, ALU.mult).then_inc(p2_ready, 1)

            program = {"pre": pre, "gu": gu, "post": post, "cin": cin, "ln": ln, "moba": moba,
                       "start": start, "mod": mod, "norm": norm, "kv": kv, "q": q_, "att": att, "gate": gate, "out": out_, "route": route,
                       "gather": gather, "fin": fin, "final": final}
            for name, *args in ORDER + ORDER2:
                if name in program:
                    program[name](*args)

        @block.sync
        def _(sp):
            for dst, src in ((cvec[:, :, :], A["cvec"]), (ident[:, :], A["ident"]), (sel[:, :, :], A["sel"]), (rope[:, :, :], A["rope"]),
                             (iota[:, :], A["iota"]), (vecs[:, :], A["vecs"])):
                sp.dma_start(dst, src).then_inc(ld_const, 16)
            sp.dma_start(x[1][:, :, :], A["ctx"].rearrange("(t p) d -> p t d", p=P)).then_inc(ld_c, 16)
            sp.dma_start(mrows[0][:, :, :], A["bmod"][0]).then_inc(ld_mrow, 16)
            gains, n = [0], [0]

            def chunks(k):
                for _ in range(k):
                    c = n[0]
                    n[0] += 1
                    if c >= SLOTS:
                        sp.wait_ge(mm_done, chunk_done[c - SLOTS])
                    name, at_, width = plan[c]
                    sp.dma_start(wring[:, c % SLOTS, 0:width], A[name][at_] if at_ else A[name]).then_inc(chunk_in[c % SLOTS], 16)

            def load_gain(vec):
                if gains[0]:
                    sp.wait_ge(gain_used, gains[0])
                gains[0] += 1
                sp.dma_start(gain[:, :], vec.unsqueeze(0).broadcast_to([P, D])).then_inc(ld_gain, 16)

            for name, *args in ORDER:
                if name == "mod":
                    if args[0]:
                        sp.dma_start(mrows[1][:, :, :], A["bmod"][1]).then_inc(ld_mrow, 16)
                    chunks(24)
                    if not args[0]:
                        sp.dma_start(x[0][:, :, :], A["x"].rearrange("(t p) d -> p t d", p=P)).then_inc(ld_x, 16)
                elif name == "norm":
                    load_gain(A["norm2_g" if args[1] else "norm1_g"][RUNS[args[0]][1]])
                elif name == "final":
                    load_gain(A["final_g"])
                elif name == "pq":
                    prev = {"x0": None, "c0": "x0", "x1": "c0"}[args[0]]
                    if prev:
                        sp.wait_ge(mm_done, mm_at["sc", prev, 7])
                    chunks(2)
                    sp.wait_ge(gain_used, gains[0])
                    sp.dma_start(keysT[:, :], A["keysT"][RUNS[args[0]][1]]).then_inc(ld_keys, 16)
                    chunks(6)
                else:
                    chunks({"zA": 2, "kv": 1, "zF": 2, "four": 3, "q": 1, "gate": 16, "out": 4}.get(name, 0))

            plan_2 = plan2()
            n2, g2n = [0], [0]

            def slot2_free(c):
                if c >= SLOTS2:
                    sp.wait_ge(mm_done, chunk2_done[c - SLOTS2])
                elif c < SLOTS:
                    last = max(m for m in range(len(plan)) if m % SLOTS == c)
                    sp.wait_ge(mm_done, chunk_done[last])
                else:
                    sp.wait_ge(x2, 2)

            def chunks2(k):
                for _ in range(k):
                    c = n2[0]
                    n2[0] += 1
                    slot2_free(c)
                    name, at_ = plan_2[c]
                    sp.dma_start(W2[c % SLOTS2], A[name][at_]).then_inc(chunk2_in[c % SLOTS2], 16)

            def load_gain2(vec):
                n = g2n[0]
                g2n[0] += 1
                if n >= 2:
                    sp.wait_ge(gain2_used, n - 1)
                else:
                    sp.wait_ge(x2, 2)
                sp.dma_start(gain2[n % 2][:, :], vec.unsqueeze(0).broadcast_to([P, D])).then_inc(gain2_in[n % 2], 16)

            for name, *args in ORDER2:
                if name == "pre":
                    tag = args[0]
                    if tag[0] == "f":
                        load_gain2(A["ffn_pre"][int(tag[1])])
                        load_gain2(A["ffn_post"][int(tag[1])])
                    elif tag == "cv":
                        sp.wait_ge(x2, X2_AT["f0"])
                        load_gain2(A["mix_pre"][0])
                        load_gain2(A["mix_post"][0])
                        sp.dma_start(vec2, A["vec2"]).then_inc(ld_vec2, 16)
                        sp.dma_start(bout_b, A["b_out"].unsqueeze(0).broadcast_to([P, D])).then_inc(ld_vec2, 16)
                    else:
                        load_gain2(A["kv_norm"])
                        load_gain2(A["mix_pre"][1])
                        sp.dma_start(dist, A["dist"]).then_inc(ld_vec2, 16)
                elif name == "gu":
                    chunks2(4)
                    n0 = n2[0]
                    f = plan_2[n0][1][0]
                    done0 = [chunk2_done[n0 + c - SLOTS2] for c in range(4)]
                    assert [chunk2_done[n0 + 4 * i + c - SLOTS2] for i in range(4) for c in range(4)] == [4 * i + done0[c] for i in range(4) for c in range(4)]
                    with sp.Fori(0, FP_ // 2 - 1) as i:
                        for c in range(4):
                            sp.wait_ge(mm_done, 4 * i + done0[c])
                            sp.dma_start(W2[(n0 + c) % SLOTS2], A["wgu"][f, bass.ds(4 * i + (4 + c), 1)].rearrange("a p n -> p (a n)")).then_inc(chunk2_in[(n0 + c) % SLOTS2], 16)
                    n2[0] += 4 * (FP_ // 2 - 1)
                    chunks2(2)
                elif name == "post" and args[0] == "at":
                    load_gain2(A["mix_post"][1])
                elif name == "store":
                    sp.wait_ge(x2, X2_AT["f3"])
                    sp.dma_start(out.rearrange("(t p) d -> p t d", p=P), x[0][:, :, :]).then_inc(out_done, 16)
                    sp.wait_ge(out_done, 16)
                else:
                    chunks2({"dn": FT // 2, "cin": 8, "cout": 4, "qkv": 12, "ao": 4}.get(name, 0))

        @block.gpsimd
        def _(pool):
            copies = [0]

            def gather(run, t):
                G = GATHER_NO[run, t]
                at_mark(pool, "route", run, t + 1)
                if G:
                    at_mark(pool, "fin", GATHERS[G - 1][0], GATHERS[G - 1][1] + 1)

                def fetch(table, offs, j):
                    pool.sem_inc(slot_ok, 1)
                    pool.indirect_dma_start(out=rows[:, j, :], out_offset=None, in_=table,
                                            in_offset=bass.IndirectOffsetOnAxis(ap=offs[:, j:j + 1], axis=0)).then_inc(row_in[j], 16)

                def down(g, par, first=None):
                    src = idx[t][:, 0:GROUP] if first == 0 else idx[t][:, bass.ds(g * GROUP, GROUP)]
                    pool.tensor_copy(idown[par][:, :], src).then_inc(idx_copied, 1)
                    pool.wait_ge(idx_copied, 2 * g + (2 * GROUPS * G + (1 if first == 0 else 0)))
                    for j in range(GROUP):
                        if first == 1:
                            pool.wait_ge(down_done, P * G + j + 1)
                        elif first is None:
                            pool.wait_ge(upv_done, 8 * g + (P * G - 2 * GROUP + j + 1))
                            pool.wait_ge(upp_done, 8 * g + (P * G - 2 * GROUP + j + 1))
                        fetch(A["peer_down"], idown[par], j)

                def up(g, par, last=False):
                    pool.tensor_copy(iup[par][:, :], idx[t][:, bass.ds(g * GROUP, GROUP)]).then_inc(idx_copied, 1)
                    pool.wait_ge(idx_copied, 2 * g + (2 * GROUPS * G + (2 if last else 3)))
                    for j in range(GROUP):
                        if last:
                            pool.wait_ge(upv_done, 8 * g + (P * G - GROUP + j + 1))
                            pool.wait_ge(upp_done, 8 * g + (P * G - GROUP + j + 1))
                        else:
                            pool.wait_ge(down_done, 8 * g + (P * G + GROUP + j + 1))
                        fetch(A["peer_up"], iup[par], j)

                down(0, 0, 0)
                down(1, 1, 1)
                up(0, 0)
                with pool.Fori(1, GROUPS // 2) as m:
                    down(m * 2, 0)
                    up(m * 2 - 1, 1)
                    down(m * 2 + 1, 1)
                    up(m * 2, 0)
                up(GROUPS - 1, 1, True)

            for name, *args in ORDER:
                if name == "gather":
                    gather(*args)


def tiles(w, k0, nk, c0, nc):
    return w[k0 * P:(k0 + nk) * P, c0:c0 + nc].reshape(nk, P, nc).transpose(1, 0, 2).reshape(P, nk * nc)


def column_chunks(w, nk, nc):
    return np.stack([np.stack([tiles(w, k0, nk, c0, nc) for k0 in range(0, w.shape[0] // P, nk)]) for c0 in range(0, w.shape[1], nc)])


def constants():
    n = np.arange(TOK)
    ang = 2 * np.pi * ((n[:, None] * n[None, :]) % TOK) / TOK
    dft = np.concatenate([np.cos(ang), np.sin(ang), -np.sin(ang)], 1).astype(np.float32) / np.float32(16)
    pool = np.zeros((4, TOK, TOK), np.float32)
    for g, w in enumerate((2, 4, 8, 16)):
        lo, hi = np.clip(n - w // 2, 0, TOK), np.clip(n - w // 2 + w, 0, TOK)
        for t in range(TOK):
            pool[g, lo[t]:hi[t], t] = np.float32(1) / np.float32(hi[t] - lo[t])
            pool[g, t, t] -= 1
    half = ROPE // 2
    inv = (np.float32(10000.0) ** (-np.arange(0, half, 2, dtype=np.float32) / half)).astype(np.float32)
    ar, ac = ((n // 64).astype(np.float32)[:, None] * inv), ((n % 64).astype(np.float32)[:, None] * inv)
    rope = np.concatenate([np.cos(ar), np.cos(ac), np.sin(ar), np.sin(ac)], 1).astype(np.float32)
    sel = np.zeros((P, 2, P), np.float32)
    for qd in range(4):
        for s in range(2):
            sel[32 * qd + s, s] = 1
    return {
        "dft": tiles(dft, 0, 2, 0, 768), "poolm": pool.reshape(4, 2, P, TOK).transpose(2, 1, 0, 3).reshape(P, -1),
        "rope": rope.reshape(TT, P, 32).transpose(1, 0, 2), "sel": sel, "ident": np.eye(P, dtype=np.float32),
        "dist": np.where(n[:, None] >= n[None, :], n[:, None] - n[None, :], 1e33).astype(np.float32).reshape(TT, P, TOK).transpose(1, 0, 2),
        "iota": np.tile(np.arange(TOP, dtype=np.float32), (P, 1)),
    }


def layout(i):
    cols = lambda v: v.reshape(-1, P).T
    bmod = np.zeros((2, P, 3, 512), np.float32)
    for l in range(2):
        for cc in range(12):
            for s in range(2):
                bmod[l, 32 * (cc % 4) + s, cc // 4] = i["b_mod"][l, cc * 512:(cc + 1) * 512]
    wgrp = np.zeros((2, P, 2, P), np.float32)
    for l in range(2):
        for g in range(4):
            po = 64 * (g % 2)
            wgrp[l, po:po + 64, g // 2, po:po + 64] = i["w_grp"][l, g]
    vecs = [np.concatenate([cols(i["kv_norm_g"][l]), cols(i["q_norm_g"][l]), cols(i["pool_scale"][l]), cols(i["b_gate"][l])], 1) for l in range(2)]
    w_in = i["w_in"]
    a = {
        "x": i["x"][0], "ctx": i["ctx"][0],
        "cvec": np.stack([cols(i["c"][0]), cols(i["c_ctx"])], 2),
        "bmod": bmod, "vecs": np.concatenate(vecs, 1), "norm1_g": i["norm1_g"], "norm2_g": i["norm2_g"], "final_g": i["final_g"],
        "wmod": np.stack([column_chunks(i["w_mod"][l], 4, 512).reshape(24, P, SLOT_W) for l in range(2)]),
        "wA": np.stack([column_chunks(w_in[l][:, 0:WA], 4, WA)[0] for l in range(2)]),
        "wZ": np.stack([column_chunks(w_in[l][:, WA:WA + WZ], 4, WZ)[0] for l in range(2)]),
        "wG": np.stack([column_chunks(w_in[l][:, WA + WZ:], 8, 256).reshape(3, 4, P, SLOT_W).transpose(1, 0, 2, 3) for l in range(2)]),
        "wO": np.stack([column_chunks(np.concatenate([i["w_oa"][l], i["w_ob"][l], i["w_oc"][l]], 0), 8, 256)[:, 0] for l in range(2)]),
        "wuq": np.stack([tiles(i["w_uq"][l], 0, 2, 0, 768) for l in range(2)]), "wukv": i["w_ukv"], "wgrp": wgrp.reshape(2, P, 256),
        "wout": np.stack([column_chunks(i["w_out"][l], 4, 512).reshape(4, P, SLOT_W) for l in range(2)]),
        "wpq": np.stack([column_chunks(i["w_pq"][l], 8, 256)[:, 0] for l in range(2)]),
        "keysT": i["peer_keys"].transpose(0, 4, 1, 2, 3).reshape(2, P, HP * KEYS),
        "peer_down": i["peer_down"].reshape(-1, D), "peer_up": i["peer_up"].reshape(-1, D),
    }
    gu = i["ffn_w_gate_up_2"].reshape(4, D, 2, FF)
    v2 = [cols(i[n][0]) for n in ("conv_b_in_2",)] + [i["conv_w_dw_2"][0].reshape(TAPS, 8, P).transpose(2, 0, 1).reshape(P, TAPS * 8)]
    v2 += [cols(i[n][0]) for n in ("conv_b_dw_2", "conv_ln_g_2", "conv_ln_b_2")]
    a.update({
        "wgu": np.stack([np.stack([column_chunks(gu[n, :, g], 8, 256)[:, 0] for g in range(2)], 1).reshape(2 * FP_, P, SLOT_W) for n in range(4)]),
        "wdn": np.stack([np.stack([tiles(w, 2 * c, 2, 0, D) for c in range(FT // 2)]) for w in i["ffn_w_down_2"].reshape(4, FF, D)]),
        "ffn_pre": i["ffn_norm_pre_2"].reshape(4, D), "ffn_post": i["ffn_norm_post_2"].reshape(4, D),
        "mix_pre": i["mix_norm_pre_2"], "mix_post": i["mix_norm_post_2"], "kv_norm": i["kv_norm_2"], "b_out": i["conv_b_out_2"][0],
        "vec2": np.concatenate(v2, 1),
        "cwin": np.stack([column_chunks(i["conv_w_in_2"][0][:, s * D:(s + 1) * D], 8, 256)[:, 0] for s in range(2)], 1).reshape(8, P, SLOT_W),
        "cwout": column_chunks(i["conv_w_out_2"][0], 4, 512).reshape(4, P, SLOT_W),
        "w2k": column_chunks(i["w_kv_2"][:, 0:D], 8, 256)[:, 0], "w2v": column_chunks(i["w_kv_2"][:, D:], 4, 512).reshape(4, P, SLOT_W),
        "w2q": column_chunks(i["attn_w_q_2"][0], 8, 256)[:, 0], "w2o": column_chunks(i["attn_w_o_2"][0], 4, 512).reshape(4, P, SLOT_W),
    })
    a.update(constants())
    return {k: np.ascontiguousarray(v, dtype=np.float32) for k, v in a.items()}


def kernel(**inputs):
    import concourse.bacc as bacc
    from concourse.bass_utils import run_bass_kernel_spmd

    nc = bacc.Bacc("TRN2", target_bir_lowering=False, num_devices=1)
    arrays = {f"in_{name}": a for name, a in layout({k: np.asarray(v) for k, v in inputs.items()}).items()}
    A = {name[3:]: nc.dram_tensor(name, a.shape, mybir.dt.from_np(a.dtype), kind="ExternalInput").ap() for name, a in arrays.items()}
    out = nc.dram_tensor("out_0", (TOK, D), mybir.dt.float32, kind="ExternalOutput").ap()
    build(nc, A, out)
    result = run_bass_kernel_spmd(nc, [arrays], core_ids=[0])
    return result.results[0]["out_0"].reshape(1, TOK, D)
```

```python
from contextlib import ExitStack

import numpy as np

import concourse.bass as bass
from concourse import mybir

P = 128
D = 1024
KT = D // P
TOK = 256
TT = TOK // P
EPS = 1e-6
H = 8
NOPE, ROPE, VH = 64, 32, 64
QK = NOPE + ROPE
QLORA, KVLORA = 256, 128
ATT_SCALE = QK ** -0.5
WA = QLORA + KVLORA + ROPE
WZ = 512
HP = 16
KEYS = 128
TOP = 16
NEG = -3.0e38
GROUP = 8
GROUPS = P // GROUP
SLOTS = 3
SLOT_W = 2048
DIAGS = 4
GELU_C = 0.7978845608028654
GELU_A = 0.044715

RUNS = {"c0": (1, 0), "x0": (0, 0), "x1": (0, 1), "c1": (1, 1)}
GATHERS = [(r, t) for r in ("x0", "c0", "x1") for t in range(TT)]
GATHER_NO = {g: n for n, g in enumerate(GATHERS)}


def keys_stages(r):
    return [("norm", r, 0), ("hT", r, 0), ("zA", r)] + [("kv", r, k) for k in range(4)]


def branches(r):
    return [[("zF", r)], [("four", r, 0), ("q", r, 0)], [("four", r, 1), ("q", r, 1)], [("q", r, 2)], [("q", r, 3)]]


def heads(r):
    return [[("att", r, i)] for i in range(H + 2)]


def mixing(r):
    return [[("gate", r, dp, part)] for dp in range(4) for part in ((0, 1) if r != "x1" else (1,))] + [[("out", r, half)] for half in range(2)] + [[("norm", r, 1)], [("hT", r, 1)]]


def scoring(r):
    return [[("pq", r, 0)], [("pq", r, 1)], [("pq", r, 2), ("route", r, 0, 0), ("route", r, 0, 1)],
            [("pq", r, 3), ("route", r, 0, 2), ("route", r, 0, 3), ("route", r, 0, 8)]]


def ranking(r, t):
    first = [[("route", r, t, 0)], [("route", r, t, 1)], [("route", r, t, 2)], [("route", r, t, 3)], [("route", r, t, 8)]]
    rest = [[("route", r, t, k)] for k in (4, 5, 6, 7, 9)]
    return first + rest if t else [[("pq", r, 4)] + rest[0]] + rest[1:]


HEAVY = ("zF", "zA", "gate", "gpre", "out", "pq")


def during(r, t, pieces, first=0):
    slots, rest = [], list(pieces)
    for n in range(GROUPS):
        a = rest.pop(0) if rest and n >= first else []
        b = rest.pop(0) if rest and n >= first and not (rest[0][0][0] in HEAVY and a and a[0][0] in HEAVY) else []
        slots.append((a, b))
    out, n = [], 0
    while n < GROUPS:
        m = n + 1
        if not slots[n][0] and not slots[n][1]:
            while m < GROUPS and not slots[m][0] and not slots[m][1]:
                m += 1
        out.append(("gather", r, t, n, m, *slots[n]))
        n = m
    return out + [("fin", r, t)], rest


def flat(pieces):
    return [st for p in pieces for st in p]


def interleave(a, b):
    out, k = [], 0
    for n, st in enumerate(a):
        out.append(st)
        while k < (n + 1) * len(b) // len(a):
            out.append(b[k])
            k += 1
    return out


def mods(l, ccs):
    return [("mod", l, cc) for cc in ccs]


def order():
    o = [("start",)] + mods(0, range(4))
    x = branches("x0")
    units = [[st] for st in keys_stages("c0") + keys_stages("x0")] + [x[0], x[1] + x[2]] + x[3:] + heads("x0")
    o += flat(interleave(units, [[st] for st in mods(0, range(4, 12))]))
    o += flat(mixing("x0") + scoring("x0"))
    beside = ranking("x0", 0) + ranking("x0", 1) + [[("hT", "c0", 2)]] + branches("c0") + heads("c0") + mixing("c0") + scoring("c0") + ranking("c0", 0)
    for t in range(TT):
        part, beside = during("x0", t, beside)
        o += part
    o += flat(beside)
    m = [[st] for st in mods(1, range(12))]
    r = ranking("c0", 1)
    gates_ = [[("gpre", "x1", dp, j)] for dp in range(3) for j in range(3)]
    beside = [x + y for x, y in zip(m, r)] + m[len(r):] + [[st] for st in keys_stages("x1")] + branches("x1") + gates_
    for t in range(TT):
        part, beside = during("c0", t, beside)
        o += part
    o += flat(beside)
    k = keys_stages("c1")
    o += k[0:1] + [("gpre", "x1", 3, j) for j in range(3)] + k[1:] + flat(heads("x1") + mixing("x1") + scoring("x1"))
    part, beside = during("x1", 0, ranking("x1", 0) + ranking("x1", 1))
    assert not beside
    o += part + during("x1", 1, [])[0]
    return o + [("final",)]


ORDER = order()
STAGES = [st for e in ORDER for st in (e[5] + e[6] if e[0] == "gather" else [e])]

FF = 2816
FT = FF // P
FP_ = FT // 2
TAPS = 31
PAD = TAPS - 1
H2, DH = 8, 128
LN_EPS = 1e-5
BLOCKS = ["f0", "cv", "f1", "f2", "at", "f3"]


def block_stages(tag):
    inner = {"f": [("gu", tag), ("dn", tag)], "c": [("cin",), ("dw",), ("ln",), ("cout",)], "a": [("qkv",), ("moba",), ("ao",)]}[tag[0]]
    return [("pre", tag), ("hT2", tag)] + inner + [("post", tag)]


ORDER2 = [st for tag in BLOCKS for st in block_stages(tag)] + [("store",)]
SS2_AT, X2_AT, H2_AT = {}, {"start": 2}, {}
_s, _x, _h = 0, 2, 0
for _st in ORDER2:
    if _st[0] == "pre":
        _s += 2
        SS2_AT["pre", _st[1]] = _s
        _h += 4 if _st[1] == "at" else 2
        H2_AT[_st[1]] = _h
    elif _st[0] == "post":
        _s += 4
        SS2_AT["post", _st[1]] = _s
        _x += 2
        X2_AT[_st[1]] = _x


def x2_before(tag):
    n = BLOCKS.index(tag)
    return X2_AT[BLOCKS[n - 1]] if n else X2_AT["start"]


def plan2():
    plan = []
    for name, *args in ORDER2:
        if name in ("gu", "dn"):
            n = int(args[0][1])
            plan += [("wgu" if name == "gu" else "wdn", (n, c)) for c in range(2 * FP_ if name == "gu" else FT // 2)]
        elif name == "cin":
            plan += [("cwin", (c,)) for c in range(8)]
        elif name == "cout":
            plan += [("cwout", (c,)) for c in range(4)]
        elif name == "qkv":
            plan += [("w2k", (c,)) for c in range(4)] + [("w2v", (c,)) for c in range(4)] + [("w2q", (c,)) for c in range(4)]
        elif name == "ao":
            plan += [("w2o", (c,)) for c in range(4)]
    return plan


SLOTS2 = 4

MARKS = {
    "h": (2, ["c0", "x0", "x1", "c1"]),
    "ckn": (2, ["c0", "x0", "x1", "c1"]),
    "krr": (2, ["c0", "x0", "x1", "c1"]),
    "cqn": (2, ["x0", "c0", "x1"]),
    "qr": (2, ["x0", "x1"]),
    "nmax": (16, ["x0", "c0", "x1"]),
    "pn": (16, ["x0", "c0", "x1"]),
    "mixT": (4, ["x0", "c0", "x1"]),
    "resid": (4, ["x0", "c0", "x1"]),
    "topd": (4, ["x0", "c0", "x1"]),
    "route": (4, ["x0", "c0", "x1"]),
    "fin": (2, ["x0", "c0", "x1"]),
    "ss": (4, ["c0", "x0", "x1", "c1"]),
    "kvss": (2, ["c0", "x0", "x1", "c1"]),
    "qss": (2, ["x0", "c0", "x1"]),
    "tope": (4, ["x0", "c0", "x1"]),
}


def mark_base(name, run):
    per, runs = MARKS[name]
    return per * runs.index(run)


def chunk_plan():
    plan = []
    for st in STAGES:
        name = st[0]
        if name == "mod":
            plan += [("wmod", (st[1], 2 * st[2] + n), SLOT_W) for n in range(2)]
            continue
        if name in ("start", "final"):
            continue
        l = RUNS[st[1]][1]
        if name == "zA":
            plan += [("wA", (l, n), 4 * WA) for n in range(2)]
        elif name == "kv":
            plan += [("wukv", (l,), D)] if st[2] == 2 else []
        elif name == "zF":
            plan += [("wZ", (l, n), SLOT_W) for n in range(2)]
        elif name == "four":
            plan += [("wgrp", (l,), 256)] if st[2] else [("dft", (), 2 * 768), ("poolm", (), SLOT_W)]
        elif name == "q":
            plan += [("wuq", (l,), 2 * H * QK)] if st[2] == 2 else []
        elif name == "gate":
            dp = st[2]
            js = () if st[1] == "x1" else (2,) if st[3] else (0, 1)
            plan += [("wG", (l, dp, j), SLOT_W) for j in js] + ([("wO", (l, dp), SLOT_W)] if st[3] else [])
        elif name == "gpre":
            plan += [("wG", (l, *st[2:]), SLOT_W)]
        elif name == "out":
            plan += [("wout", (l, 2 * st[2] + n), SLOT_W) for n in range(2)]
        elif name == "pq":
            plan += [("wpq", (l, 2 * st[2] + n), SLOT_W) for n in range(2)] if st[2] < 4 else []
    return plan


def build(nc, A, out):
    f32, i32, u32 = mybir.dt.float32, mybir.dt.int32, mybir.dt.uint32
    ALU, ACT, AX = mybir.AluOpType, mybir.ActivationFunctionType, mybir.AxisListType
    ctx = ExitStack()

    def sb(name, shape, dt=f32):
        return ctx.enter_context(nc.sbuf_tensor(name, shape, dt))

    def sem(name):
        return ctx.enter_context(nc.semaphore(name))

    with ctx:
        x = [sb("x_in", [P, TT, D]), sb("x_ctx", [P, TT, D])]
        h = [sb("h_in", [P, TT, D]), sb("h_ctx", [P, TT, D])]
        hT = sb("hT", [P, KT, TOK])
        mrows = [sb(f"mrows{l}", [P, 3, 512]) for l in range(2)]
        gain = sb("gain", [P, D])
        keysT = sb("keysT", [P, HP * KEYS])
        amul, junk = keysT[:, 0:D], keysT[:, D:2 * D]
        mb = sb("mb", [P, D])
        wring = sb("wring", [P, SLOTS, SLOT_W])
        rows = sb("rows", [P, GROUP, D])
        zA = [sb("zA_in", [P, TT, WA]), sb("zA_ctx", [P, TT, WA])]
        kT = sb("kT", [P, H, 2 * TOK])
        vv = sb("vv", [P, 2 * TT, H * VH])
        YT = sb("YT", [P, 512])
        ypT = sb("ypT", [P, 512])
        ident = sb("ident", [P, P])
        sel = sb("sel", [P, 2, P])
        rope = sb("rope", [P, TT, 32])
        iota = sb("iota", [P, TOP])
        cvec = sb("cvec", [P, KT, 2])
        cth = sb("cth", [P, KT, 2])
        vecs = sb("vecs", [P, 58])
        hbg = sb("hbg", [P, 2, 24])
        ss = sb("ss", [P, 8])
        nwt = sb("nwt", [P, 8])
        nwi = sb("nwi", [P, 8], i32)
        a8 = sb("a8", [P, GROUP])
        g1 = sb("g1", [P, GROUP])
        g2 = sb("g2", [P, GROUP])
        th8 = sb("th8", [P, GROUP])
        act8 = sb("act8", [P, GROUP])
        diag = sb("diag", [P, DIAGS, P])
        accv = sb("accv", [P, 512])
        nmax, rsum, rinv = (sb(n, [P, 4]) for n in ("nmax", "rsum", "rinv"))
        idx = [sb(f"idx{t}", [P, P], u32) for t in range(TT)]
        gates = [sb(f"gates{t}", [P, P]) for t in range(TT)]
        idown = [sb(f"idown{n}", [P, GROUP], u32) for n in range(2)]
        iup = [sb(f"iup{n}", [P, GROUP], u32) for n in range(2)]
        U = sb("shared", [P, 10240])
        at = [0]

        def part(n):
            at[0] += n
            assert at[0] <= 10240, at
            return U[:, at[0] - n:at[0]]

        q = part(2 * 768).rearrange("p (t n) -> p t n", t=TT)
        kfull = part(2 * 768).rearrange("p (t n) -> p t n", t=TT)
        qT = part(H * TOK).rearrange("p (h n) -> p h n", h=H)
        at[0] = 2 * 1536
        sg = part(3 * 512).rearrange("p (j n) -> p j n", j=3)
        mtmp = part(512)
        at[0] = 0
        mixT = part(KT * TOK).rearrange("p (k n) -> p k n", k=KT)
        at[0] = 3072 + 2048
        pr = part(4 * 512).rearrange("p (a t n) -> p a t n", a=2, t=TT)
        pT = part(4 * TOK).rearrange("p (k n) -> p k n", k=4)
        attT = part(4 * TOK).rearrange("p (k n) -> p k n", k=4)
        ckn = part(2 * P).rearrange("p (t n) -> p t n", t=TT)
        ckT = part(TOK)
        rtmp = part(4 * P).rearrange("p (a n) -> p a n", a=4)
        at[0] = 3072 + 2048
        zfp = part(2 * 512).rearrange("p (t n) -> p t n", t=TT)
        T1 = part(2 * 512).rearrange("p (t n) -> p t n", t=TT)
        poolT = part(512)
        cqn = part(2 * QLORA).rearrange("p (t n) -> p t n", t=TT)
        cqT = part(2 * TOK).rearrange("p (k n) -> p k n", k=2)
        at[0] = 0
        s_sb = part(TT * 2048).rearrange("p (t n) -> p t n", t=TT)
        cand = part(512).rearrange("p (a n) -> p a n", a=2)
        eq = part(1024)
        qpT = part(2 * 512).rearrange("p (a n) -> p a n", a=2)
        sv, sif = (part(HP * TOP).rearrange("p (i k) -> p i k", k=TOP) for _ in range(2))
        si = part(HP * TOP).bitcast(u32).rearrange("p (i k) -> p i k", k=TOP)
        ts, te = (part(P).rearrange("p (i k) -> p i k", k=TOP) for _ in range(2))
        fa, fb, ia, ib = (part(P) for _ in range(4))
        pos = part(P).bitcast(u32).rearrange("p (i k) -> p i k", k=TOP)
        pa = part(P).bitcast(u32)
        tsum = part(H)

        def gate_at(run, dp, j):
            if run != "x1":
                return sg[:, j, :]
            if dp == 3:
                return (mb[:, 0:512], mb[:, 512:D], zA[0].rearrange("p t n -> p (t n)")[:, 0:512])[j]
            if j == 0:
                return U[:, dp * 512:(dp + 1) * 512]
            n = 2 * dp + j - 1
            return h[0][:, n // 2, (n % 2) * 512:(n % 2 + 1) * 512] if n < 4 else junk[:, (n - 4) * 512:(n - 3) * 512]

        W2 = [wring[:, n, :] for n in range(SLOTS)] + [rows[:, 0:2, :].rearrange("p a n -> p (a n)")]
        gain2 = [gain, mb]
        at[0] = 0
        hid = part(FT * TOK).rearrange("p (k n) -> p k n", k=FT)
        fth = part(4 * TOK).rearrange("p (a n) -> p a n", a=4)
        ft2 = part(4 * TOK).rearrange("p (a n) -> p a n", a=4)
        at[0] = 0
        upad = part(8 * (TOK + PAD)).rearrange("p (c n) -> p c n", c=8)
        uc = part(8 * TOK).rearrange("p (c n) -> p c n", c=8)
        usq = part(8 * TOK).rearrange("p (c n) -> p c n", c=8)
        uth = part(8 * TOK).rearrange("p (c n) -> p c n", c=8)
        rln, rl2 = part(TOK), part(TOK)
        ctmp = part(2 * TOK).rearrange("p (a n) -> p a n", a=2)
        bout_b, vec2 = keysT[:, 0:D], keysT[:, D:D + 288]
        rli = rows[:, 2, 0:TOK].bitcast(i32)
        rli2 = rows[:, 2, TOK:2 * TOK].bitcast(i32)
        ones = rows[:, 3, 0:P]
        kT2 = kT[:, :, 0:TOK]
        qT2 = kT[:, :, TOK:2 * TOK]
        v2 = vv[:, :, :].rearrange("p a n -> p (a n)").rearrange("p (t n) -> p t n", t=TT)
        at[0] = 0
        attT2 = part(8 * TOK).rearrange("p (h n) -> p h n", h=8)
        hkT = part(KT * TOK).rearrange("p (k n) -> p k n", k=KT)
        p2 = part(4 * TOK).rearrange("p (a t n) -> p a t n", a=2, t=TT)
        pT2 = part(2 * TOK).rearrange("p (k n) -> p k n", k=2)
        dist = rows[:, 3, 512:1024].rearrange("p (t n) -> p t n", t=TT)

        ps = ctx.enter_context(nc.psum_tensor("ps", [P, 8, 512], f32))
        ROT = [0, 1, 2, 3, 5, 6, 7]
        ROT2, WIDE = [0, 1, 2, 3], [4, 5, 6, 7]
        UPB = 4
        UPV = 512

        mm_done = sem("mm_done")
        bank_free = [sem(f"bank_free{b}") for b in range(8)]
        mark = {n: sem(n) for n in MARKS}
        chunk_in = [sem(f"chunk_in{n}") for n in range(SLOTS)]
        row_in = [sem(f"row_in{n}") for n in range(GROUP)]
        ld_const, ld_x, ld_c, ld_gain, ld_keys, ld_mrow = (sem(n) for n in ("ld_const", "ld_x", "ld_c", "ld_gain", "ld_keys", "ld_mrow"))
        gain_used = sem("gain_used")
        dve_step, act_step = sem("dve_step"), sem("act_step")
        silu_t, silu_c = sem("silu_t"), sem("silu_c")
        down_done, upv_done, upp_done = sem("down_done"), sem("upv_done"), sem("upp_done")
        idx_copied, gelu_step, gelu_in, gelu_th, act_ready, diag_ready = (sem(n) for n in (
            "idx_copied", "gelu_step", "gelu_in", "gelu_th", "act_ready", "diag_ready"))
        slot_ok = sem("slot_ok")
        ss2, x2, h2m, ld_vec2, ones_set = (sem(n) for n in ("ss2", "x2", "h2m", "ld_vec2", "ones_set"))
        gain2_in = [sem(f"gain2_in{n}") for n in range(2)]
        gain2_used = sem("gain2_used")
        chunk2_in = [sem(f"chunk2_in{n}") for n in range(SLOTS2)]
        gate_th, gu_step = sem("gate_th"), sem("gu_step")
        conv_h, conv_th, conv_u, conv_y, ln_d, ln_v, ln_z, ln_t, ln_s = (sem(n) for n in (
            "conv_h", "conv_th", "conv_u", "conv_y", "ln_d", "ln_v", "ln_z", "ln_t", "ln_s"))
        s2_ready, p2_ready, bout_y = sem("s2_ready"), sem("p2_ready"), sem("bout_y")
        out_done = sem("out_done")

        mm_at, job_bank, job_use = {}, {}, {}
        uses = [0] * 8
        plan = chunk_plan()
        gu_base, chunk2_done = {}, []
        chunk_done = {}

        def at_mark(eng, name, run, n):
            eng.wait_ge(mark[name], mark_base(name, run) + n)

        def at_mm(eng, key):
            eng.wait_ge(mm_done, mm_at[key])
            return ps[:, job_bank[key], :]

        def at_evac(eng, key):
            eng.wait_ge(bank_free[job_bank[key]], job_use[key])

        def release(ins, key):
            ins.then_inc(bank_free[job_bank[key]], 1)

        def norm_mark(run, k, n):
            firsts = {"c0": 0, "x0": 1, "x1": 4, "c1": 5}
            return (firsts[run] if k == 0 else {"x0": 2, "c0": 3, "x1": 6}[run]) * 2 + n

        def is_group(n, which):
            return isinstance(n, int) and n == which

        def groups(eng, n0, n1, body):
            lo, hi = max(n0, 2), min(n1, GROUPS - 1)
            for n in range(n0, min(n1, 2)):
                body(n)
            if hi - lo > 1:
                with eng.Fori(lo, hi) as n:
                    body(n)
            elif hi - lo == 1:
                body(lo)
            if n1 == GROUPS and n0 < GROUPS:
                body(GROUPS - 1)

        block = ctx.enter_context(nc.Block())

        @block.tensor
        def _(pe):
            count = [0]
            rot = [0]
            chunk_no = [0]

            def job(key):
                b = ROT[rot[0] % len(ROT)]
                rot[0] += 1
                if uses[b]:
                    pe.wait_ge(bank_free[b], uses[b])
                uses[b] += 1
                job_bank[key], job_use[key] = b, uses[b]
                return ps[:, b, :]

            def ended(ins, key):
                count[0] += 1
                ins.then_inc(mm_done, 1)
                mm_at[key] = count[0]

            def chunk():
                n = chunk_no[0]
                chunk_no[0] += 1
                pe.wait_ge(chunk_in[n % SLOTS], 16 * (n // SLOTS + 1))
                return wring[:, n % SLOTS, 0:plan[n][2]]

            def chunk_end(n=1):
                for _ in range(n):
                    chunk_done[len(chunk_done)] = count[0]

            def bcast(key, run, j, half):
                s, l = RUNS[run]
                cc = 2 * j + half
                at_evac(pe, ("mod", l, cc))
                qd, a = 32 * (cc % 4), cc // 4
                ended(pe.matmul(job(key), sel[qd:qd + 2, s, :], mrows[l][qd:qd + 2, a, :], start=True, stop=True,
                                tile_position=(qd, 0)), key)

            def start():
                pe.wait_ge(ld_const, 16 * 6)

            def mod(l, cc):
                if l + cc == 0:
                    pe.wait_ge(silu_c, 1)
                qd = 32 * (cc % 4)
                b = job(("mod", l, cc))
                for half in range(2):
                    w = chunk()
                    for k in range(4):
                        last = pe.matmul(b[qd:qd + 2, :], cvec[:, 4 * half + k, :], w[:, k * 512:(k + 1) * 512],
                                         start=(half + k == 0), stop=(half == 1 and k == 3), tile_position=(0, qd))
                ended(last, ("mod", l, cc))
                chunk_end(2)

            def norm(run, k):
                for half in range(2):
                    bcast(("bs", run, k, half), run, 1 + 3 * k, half)
                for half in range(2):
                    bcast(("bh", run, k, half), run, 3 * k, half)

            hT_now = [None]

            def hT_(run, k):
                s = RUNS[run][0]
                hT_now[0] = (run, k)
                for a in range(2):
                    for t in range(TT):
                        if k == 2:
                            pass
                        elif t == 0:
                            pe.wait_ge(mark["h"], norm_mark(run, k, a + 1))
                        else:
                            at_evac(pe, ("bh", run, k, a))
                        b = job(("hT", run, k, t, a))
                        for j in range(4):
                            last = pe.transpose(b[:, j * P:(j + 1) * P], h[s][:, t, (4 * a + j) * P:(4 * a + j + 1) * P], ident[:, :])
                        ended(last, ("hT", run, k, t, a))

            def hT_ready():
                for t in range(TT):
                    for a in range(2):
                        at_evac(pe, ("hT", *hT_now[0], t, a))

            def token_major(keys, lhs, width, halves=2):
                bs = [job(k) for k in keys]
                for c in range(2):
                    w = chunk()
                    for t in range(TT):
                        for k in range(4):
                            last = pe.matmul(bs[t][:, 0:width], lhs[:, 4 * c + k, t * P:(t + 1) * P], w[:, k * width:(k + 1) * width],
                                             start=(c + k == 0), stop=(c == 1 and k == 3))
                        if c == 1:
                            ended(last, keys[t])
                chunk_end(2)

            def zA_(run):
                hT_ready()
                token_major([("zA", run, t) for t in range(TT)], hT, WA)

            def kv(run, step):
                if step == 1:
                    b = job(("ckT", run))
                    for t in range(TT):
                        at_mark(pe, "ckn", run, t + 1)
                        last = pe.transpose(b[:, t * P:(t + 1) * P], ckn[:, t, :], ident[:, :])
                    ended(last, ("ckT", run))
                elif step == 2:
                    w = chunk()
                    at_evac(pe, ("ckT", run))
                    for t in range(TT):
                        for half in range(2):
                            key = ("kv", run, t, half)
                            ended(pe.matmul(job(key), ckT[:, t * P:(t + 1) * P], w[:, half * 512:(half + 1) * 512], start=True, stop=True), key)
                    chunk_end()
                elif step == 3:
                    for t in range(TT):
                        at_mark(pe, "krr", run, t + 1)
                        for hq in range(2):
                            at_evac(pe, ("kv", run, t, hq))
                            b = job(("kT", run, t, hq))
                            for j in range(4):
                                hh = 4 * hq + j
                                last = pe.transpose(b[0:QK, j * P:(j + 1) * P], kfull[:, t, hh * QK:(hh + 1) * QK], ident[:, :])
                            ended(last, ("kT", run, t, hq))

            def zF(run):
                hT_ready()
                token_major([("zF", run, t) for t in range(TT)], hT, WZ)

            dft_now = [None]

            def four(run, step):
                if step == 0:
                    for t in range(TT):
                        at_evac(pe, ("zF", run, t))
                    w = dft_now[0] = chunk().rearrange("p (k n) -> p k n", k=2)
                    for ft in range(2):
                        b = job(("T1", run, ft))
                        for lt in range(TT):
                            last = pe.matmul(b, zfp[:, lt, ft * P:(ft + 1) * P], w[:, lt, 0:512], start=(lt == 0), stop=(lt == 1))
                        ended(last, ("T1", run, ft))
                    wp = chunk().rearrange("p (k g n) -> p k g n", k=2, g=4)
                    b = job(("P", run))
                    for g in range(4):
                        for lt in range(TT):
                            po = 64 * (g % 2)
                            last = pe.matmul(b[po:po + 64, (g // 2) * TOK:(g // 2 + 1) * TOK], zfp[:, lt, TOK + g * 64:TOK + (g + 1) * 64],
                                             wp[:, lt, g, :], start=(lt == 0), stop=(lt == 1), tile_position=(0, po))
                    ended(last, ("P", run))
                    return
                w = dft_now[0]
                b = job(("Y", run))
                for ft in range(2):
                    at_evac(pe, ("T1", run, ft))
                for fo in range(2):
                    for ft in range(2):
                        for part_ in range(2):
                            last = pe.matmul(b[:, fo * TOK:(fo + 1) * TOK], w[:, ft, part_ * 512 + fo * P:part_ * 512 + (fo + 1) * P],
                                             T1[:, ft, part_ * TOK:(part_ + 1) * TOK], start=(ft + part_ == 0), stop=(ft + part_ == 2))
                ended(last, ("Y", run))
                chunk_end(2)
                wg = chunk()
                at_evac(pe, ("P", run))
                b = job(("G", run))
                for pair in range(2):
                    last = pe.matmul(b[:, pair * TOK:(pair + 1) * TOK], wg[:, pair * P:(pair + 1) * P], poolT[:, pair * TOK:(pair + 1) * TOK],
                                     start=True, stop=True)
                ended(last, ("G", run))
                chunk_end()

            def q_(run, step):
                if step == 1:
                    b = job(("cqT", run))
                    for t in range(TT):
                        at_mark(pe, "cqn", run, t + 1)
                        for k in range(2):
                            last = pe.transpose(b[:, k * TOK + t * P:k * TOK + (t + 1) * P], cqn[:, t, k * P:(k + 1) * P], ident[:, :])
                    ended(last, ("cqT", run))
                elif step == 2:
                    w = chunk()
                    at_evac(pe, ("cqT", run))
                    for t in range(TT):
                        for half in range(2):
                            key = ("q", run, t, half)
                            b = job(key)
                            for k in range(2):
                                last = pe.matmul(b[:, 0:384], cqT[:, k, t * P:(t + 1) * P], w[:, k * 768 + half * 384:k * 768 + (half + 1) * 384],
                                                 start=(k == 0), stop=(k == 1))
                            ended(last, key)
                    chunk_end()
                elif step == 3:
                    for t in range(TT):
                        for half in range(2):
                            at_evac(pe, ("q", run, t, half))
                        if RUNS[run][0] == 0:
                            at_mark(pe, "qr", run, t + 1)
                        for hq in range(2):
                            b = job(("qT", run, t, hq))
                            for j in range(4):
                                hh = 4 * hq + j
                                last = pe.transpose(b[0:QK, j * P:(j + 1) * P], q[:, t, hh * QK:(hh + 1) * QK], ident[:, :])
                            ended(last, ("qT", run, t, hq))

            def att(run, i):
                nk = 4 if RUNS[run][0] == 0 else 2
                if i == 0:
                    for r2 in {"x0": ("x0", "c0"), "c0": ("c0",), "x1": ("x1", "c1")}[run]:
                        for t in range(TT):
                            for hq in range(2):
                                at_evac(pe, ("kT", r2, t, hq))
                    for t in range(TT):
                        for hq in range(2):
                            at_evac(pe, ("qT", run, t, hq))
                if i < H:
                    for t in range(TT):
                        key = ("s", run, i, t)
                        ended(pe.matmul(job(key)[:, 0:nk * P], qT[0:QK, i, t * P:(t + 1) * P], kT[0:QK, i, 0:nk * P], start=True, stop=True), key)
                if i >= 2:
                    hh = i - 2
                    for t in range(TT):
                        at_evac(pe, ("pT", run, hh, t))
                    if hh % 2 == 0:
                        job(("pv", run, hh // 2))
                    pv = ps[:, job_bank["pv", run, hh // 2], :]
                    po = 64 * (hh % 2)
                    for k in range(nk):
                        last = pe.matmul(pv[po:po + VH, 0:TOK], vv[:, k, hh * VH:(hh + 1) * VH], pT[:, k, :],
                                         start=(k == 0), stop=(k == nk - 1), tile_position=(0, po))
                    ended(last, ("pvh", run, hh))
                    if hh % 2:
                        mm_at["pv", run, hh // 2] = count[0]
                if 1 <= i <= H:
                    hh = i - 1
                    for t in range(TT):
                        at_mark(pe, "pn", run, 2 * hh + t + 1)
                        b = job(("pT", run, hh, t))
                        for k in range(nk):
                            last = pe.transpose(b[:, k * P:(k + 1) * P], pr[:, hh % 2, t, k * P:(k + 1) * P], ident[:, :])
                        ended(last, ("pT", run, hh, t))

            def gpre(run, dp, j):
                hT_ready()
                w = chunk()
                b = job(("g", run, dp, j))
                for dt in range(2):
                    for k in range(KT):
                        last = pe.matmul(b[:, dt * TOK:(dt + 1) * TOK], w[:, k * 256 + dt * P:k * 256 + (dt + 1) * P], hT[:, k, :],
                                         start=(k == 0), stop=(k == KT - 1))
                ended(last, ("g", run, dp, j))
                chunk_end()

            def gate(run, dp, part_):
                if dp + part_ == 0:
                    hT_ready()
                for j in (() if run == "x1" else (2,) if part_ else (0, 1)):
                    gpre(run, dp, j)
                if not part_:
                    return
                if dp == 0:
                    for n in range(4):
                        at_evac(pe, ("pv", run, n))
                    at_evac(pe, ("Y", run))
                    at_evac(pe, ("G", run))
                w = chunk()
                for j, ks in enumerate(([0, 1, 2, 3], [4, 5], [6, 7])):
                    b = job(("y", run, dp, j))
                    for dt in range(2):
                        for k in ks:
                            rhs = attT[:, k, :] if j == 0 else (YT, ypT)[j - 1][:, (k % 2) * TOK:(k % 2 + 1) * TOK]
                            last = pe.matmul(b[:, dt * TOK:(dt + 1) * TOK], w[:, k * 256 + dt * P:k * 256 + (dt + 1) * P], rhs,
                                             start=(k == ks[0]), stop=(k == ks[-1]))
                    ended(last, ("y", run, dp, j))
                chunk_end()

            def out_(run, half):
                at_mark(pe, "mixT", run, 4)
                bcast(("bm", run, half), run, 2, half)
                token_major([("o", run, half, t) for t in range(TT)], mixT, 512)

            def pq(run, i):
                if i == 0:
                    hT_ready()
                if i == 1:
                    pe.wait_ge(ld_keys, 16 * (["x0", "c0", "x1"].index(run) + 1))

                def queries(c):
                    w = chunk()
                    b = job(("qp", run, c))
                    for hp in range(2):
                        for k in range(KT):
                            last = pe.matmul(b[:, hp * TOK:(hp + 1) * TOK], w[:, k * 256 + hp * P:k * 256 + (hp + 1) * P],
                                             hT[:, k, :], start=(k == 0), stop=(k == KT - 1))
                    ended(last, ("qp", run, c))
                    chunk_end()

                def scores(c):
                    at_evac(pe, ("qp", run, c))
                    b = job(("sc", run, c))
                    for t in range(TT):
                        for hp in range(2):
                            last = pe.matmul(b[:, t * 256 + hp * P:t * 256 + (hp + 1) * P], qpT[:, c % 2, hp * TOK + t * P:hp * TOK + (t + 1) * P],
                                             keysT[:, (2 * c + hp) * P:(2 * c + hp + 1) * P], start=True, stop=True)
                    ended(last, ("sc", run, c))

                for c in (2 * i, 2 * i + 1):
                    if i < 4:
                        queries(c)
                    if i:
                        scores(c - 2)

            def gather(run, t, n0, n1, beside_a, beside_b):
                G = GATHER_NO[run, t]

                def up(g, first=False, last=False):
                    pos_ = 31 if last else 2 * g + 2
                    for j in range(GROUP):
                        pe.wait_ge(row_in[j], 16 * (32 * G + 1) + 16 * pos_)
                        pe.wait_ge(diag_ready, 8 * g + (P * G + j + 1))
                        pe.matmul(ps[:, UPB, :], diag[:, j % DIAGS, :], rows[:, j, UPV:D], start=(first and j == 0), stop=(last and j == GROUP - 1),
                                  skip_group_check=True).then_inc(upp_done, 1)

                run_stages(beside_a)
                if n0 <= 1 < n1 and G:
                    at_mark(pe, "fin", GATHERS[G - 1][0], GATHERS[G - 1][1] + 1)
                groups(pe, n0, n1, lambda n: is_group(n, 0) or up(n - 1, first=is_group(n, 1)))
                run_stages(beside_b)
                if n1 == GROUPS:
                    up(GROUPS - 1, last=True)

            def fin(run, t):
                for half in range(2):
                    bcast(("bf", run, t, half), run, 5, half)

            rots = {"a": 0, "w": 0}
            chunk2_no = [0]
            plan_2 = plan2()

            def job2(key, wide=False):
                banks, r = (WIDE, "w") if wide else (ROT2, "a")
                b = banks[rots[r] % 4]
                rots[r] += 1
                if uses[b]:
                    pe.wait_ge(bank_free[b], uses[b])
                uses[b] += 1
                job_bank[key], job_use[key] = b, uses[b]
                return ps[:, b, :]

            def chunk2():
                n = chunk2_no[0]
                chunk2_no[0] += 1
                pe.wait_ge(chunk2_in[n % SLOTS2], 16 * (n // SLOTS2 + 1))
                return W2[n % SLOTS2]

            def chunk2_end(n=1):
                chunk2_done.extend([count[0]] * n)

            def hT2(tag):
                for gi, (src, dst) in enumerate([(h[1], hkT), (h[0], hT)] if tag == "at" else [(h[0], hT)]):
                    for t in range(TT):
                        pe.wait_ge(h2m, H2_AT[tag] - (4 if tag == "at" else 2) + 2 * gi + t + 1)
                        for a in range(2):
                            key = ("hT2", tag, gi, t, a)
                            b = job2(key)
                            for j in range(4):
                                last = pe.transpose(b[:, j * P:(j + 1) * P], src[:, t, (4 * a + j) * P:(4 * a + j + 1) * P], ident[:, :])
                            ended(last, key)

            def hT2_ready(tag, gi=0):
                for t in range(TT):
                    for a in range(2):
                        at_evac(pe, ("hT2", tag, gi, t, a))

            def pair(b, w0, w1, j):
                for side, w in enumerate((w0, w1)):
                    for k in range(KT):
                        last = pe.matmul(b[:, side * TOK:(side + 1) * TOK], w[:, k * 256 + j * P:k * 256 + (j + 1) * P], hT[:, k, :],
                                         start=(k == 0), stop=(k == KT - 1))
                return last

            def gu(tag):
                hT2_ready(tag)
                n0, m0, use0, r0 = chunk2_no[0], count[0], list(uses), rots["a"]
                gu_base[tag] = (m0, r0)
                turns = FP_ // 2
                with pe.Fori(0, turns) as i:
                    for pr_ in range(2):
                        ws = []
                        for c in range(2):
                            n = n0 + 2 * pr_ + c
                            pe.wait_ge(chunk2_in[n % SLOTS2], 16 * i + 16 * (n // SLOTS2 + 1))
                            ws.append(W2[n % SLOTS2])
                        for j in range(2):
                            b = ROT2[(r0 + 2 * pr_ + j) % 4]
                            pe.wait_ge(bank_free[b], i + use0[b])
                            pair(ps[:, b, :], *ws, j).then_inc(mm_done, 1)
                for b in ROT2:
                    uses[b] += turns
                count[0] += 4 * turns
                rots["a"] += 4 * turns
                chunk2_no[0] += 4 * turns
                for i in range(turns):
                    chunk2_done.extend([m0 + 4 * i + 2] * 2 + [m0 + 4 * i + 4] * 2)
                ws = [chunk2(), chunk2()]
                for j in range(2):
                    key = ("gu", tag, j)
                    ended(pair(job2(key), *ws, j), key)
                chunk2_end(2)

            def dn(tag):
                keys = [("d", tag, t, half) for t in range(TT) for half in range(2)]
                bs = [job2(key, True) for key in keys]
                pe.wait_ge(gu_step, 2 * FT * (int(tag[1]) + 1) - 4)
                for c in range(FT // 2):
                    w = chunk2()
                    if c == FT // 2 - 1:
                        for j in range(2):
                            at_evac(pe, ("gu", tag, j))
                    for n, (t, half) in enumerate([(t, half) for t in range(TT) for half in range(2)]):
                        for k in range(2):
                            last = pe.matmul(bs[n], hid[:, 2 * c + k, t * P:(t + 1) * P], w[:, k * D + half * 512:k * D + (half + 1) * 512],
                                             start=(c + k == 0), stop=(c == FT // 2 - 1 and k == 1))
                        if c == FT // 2 - 1:
                            ended(last, keys[n])
                    if c < FT // 2 - 1:
                        ended(last, ("dn", tag, c))
                    chunk2_end()

            def token_major2(tag, lhs, name="d", wide=True, release_w=True):
                for half in range(2):
                    keys = [(name, tag, t, half) for t in range(TT)]
                    bs = [job2(key, wide) for key in keys]
                    for c in range(2):
                        w = chunk2()
                        for t in range(TT):
                            for k in range(4):
                                last = pe.matmul(bs[t], lhs[:, 4 * c + k, t * P:(t + 1) * P], w[:, k * 512:(k + 1) * 512],
                                                 start=(c + k == 0), stop=(c == 1 and k == 3))
                            if c == 1:
                                ended(last, keys[t])
                    chunk2_end(2)

            def cin():
                hT2_ready("cv")
                for dp in range(4):
                    ws = [chunk2(), chunk2()]
                    for j in range(2):
                        key = ("cin", 2 * dp + j)
                        ended(pair(job2(key), *ws, j), key)
                    chunk2_end(2)

            def ln():
                pe.wait_ge(ones_set, 1)
                b = job2(("mean",))
                for c in range(8):
                    pe.wait_ge(conv_y, c + 1)
                    last = pe.matmul(b[:, 0:TOK], ones, uc[:, c, :], start=(c == 0), stop=(c == 7))
                ended(last, ("mean",))
                b = job2(("var",))
                pe.wait_ge(ln_v, 1)
                for c in range(8):
                    last = pe.matmul(b[:, 0:TOK], ones, usq[:, c, :], start=(c == 0), stop=(c == 7))
                ended(last, ("var",))

            def cout():
                pe.wait_ge(ln_s, 1)
                token_major2("cv", uth)

            def qkv():
                for name, gi in (("k2", 0), ("v2", 0), ("q2", 1)):
                    hT2_ready("at", gi)
                    src = (hkT, hT)[gi]
                    if name == "v2":
                        token_major2("at", src, "v2", False)
                        continue
                    for c in range(4):
                        w = chunk2()
                        b = job2((name, c))
                        for j in range(2):
                            for k in range(KT):
                                last = pe.matmul(b[:, j * TOK:(j + 1) * TOK], w[:, k * 256 + j * P:k * 256 + (j + 1) * P], src[:, k, :],
                                                 start=(k == 0), stop=(k == KT - 1))
                        ended(last, (name, c))
                        chunk2_end()

            def moba():
                for c in range(4):
                    at_evac(pe, ("k2", c))
                    at_evac(pe, ("q2", c))
                for t in range(TT):
                    for half in range(2):
                        at_evac(pe, ("v2", "at", t, half))

                def scores(hh):
                    b = job2(("s2", hh))
                    for t in range(TT):
                        last = pe.matmul(b[:, t * TOK:(t + 1) * TOK], qT2[:, hh, t * P:(t + 1) * P], kT2[:, hh, :], start=True, stop=True)
                    ended(last, ("s2", hh))

                scores(0)
                for hh in range(H2):
                    if hh + 1 < H2:
                        scores(hh + 1)
                    b = job2(("pT2", hh))
                    for t in range(TT):
                        pe.wait_ge(p2_ready, 2 * hh + t + 1)
                        for k in range(2):
                            last = pe.transpose(b[:, k * TOK + t * P:k * TOK + (t + 1) * P], p2[:, hh % 2, t, k * P:(k + 1) * P], ident[:, :])
                    ended(last, ("pT2", hh))
                    at_evac(pe, ("pT2", hh))
                    b = job2(("pv2", hh))
                    for k in range(2):
                        last = pe.matmul(b[:, 0:TOK], v2[:, k, hh * DH:(hh + 1) * DH], pT2[:, k, :], start=(k == 0), stop=(k == 1))
                    ended(last, ("pv2", hh))

            def ao():
                for hh in range(H2):
                    at_evac(pe, ("pv2", hh))
                token_major2("at", attT2)

            program = {"hT2": hT2, "gu": gu, "dn": dn, "cin": cin, "ln": ln, "cout": cout, "qkv": qkv, "moba": moba, "ao": ao,
                       "start": start, "mod": mod, "norm": norm, "hT": hT_, "zA": zA_, "kv": kv, "zF": zF, "four": four, "q": q_, "att": att,
                       "gate": gate, "gpre": gpre, "out": out_, "pq": pq, "gather": gather, "fin": fin}

            def run_stages(stages):
                for name, *args in stages:
                    if name in program:
                        program[name](*args)

            run_stages(ORDER + ORDER2)
            assert chunk_no[0] == len(plan) == len(chunk_done)
            assert chunk2_no[0] == len(plan_2) == len(chunk2_done)

        @block.scalar
        def _(act):
            own = [0]

            def alone(ins):
                own[0] += 1
                ins.then_inc(act_step, 1)
                act.wait_ge(act_step, own[0])

            def copy(dst, src, key, scale=None):
                release(act.activation(dst, src, ACT.Copy) if scale is None else act.activation(dst, src, ACT.Copy, scale=scale), key)

            def squares(src, n, scratch):
                return act.activation(scratch, src, ACT.Square, accum_out=ss[:, n:n + 1])

            def start():
                act.wait_ge(ld_const, 16 * 6)
                act.activation(cth[:, :, :], cvec[:, :, :], ACT.Tanh, scale=0.5).then_inc(silu_t, 1)

            def norm(run, k):
                s = RUNS[run][0]
                if k:
                    at_mark(act, "resid", run, 4)
                elif RUNS[run][1] == 0:
                    act.wait_ge((ld_x, ld_c)[s], 16)
                else:
                    at_mark(act, "fin", ("x0", "c0")[s], 2)
                for t in range(TT):
                    squares(x[s][:, t, :], t, h[s][:, t, :]).then_inc(mark["ss"], 1)

            def hT_(run, k):
                s = RUNS[run][0]
                for a in range(2):
                    for t in range(TT):
                        key = ("hT", run, k, t, a)
                        b = at_mm(act, key)
                        copy(hT[:, 4 * a:4 * a + 4, t * P:(t + 1) * P], b.rearrange("p (j n) -> p j n", j=4), key)

            def zA_(run):
                s = RUNS[run][0]
                for t in range(TT):
                    key = ("zA", run, t)
                    b = at_mm(act, key)
                    copy(zA[s][:, t, :], b[:, 0:WA], key)

            def kv(run, step):
                s, l = RUNS[run]
                if step == 0:
                    for t in range(TT):
                        at_evac(act, ("zA", run, t))
                        squares(zA[s][:, t, QLORA:QLORA + KVLORA], 2 + t, ckn[:, t, :]).then_inc(mark["kvss"], 1)
                elif step == 1:
                    key = ("ckT", run)
                    b = at_mm(act, key)
                    release(act.activation(ckT[:, :], b[:, 0:TOK], ACT.Copy, scale=vecs[:, 29 * l:29 * l + 1]), key)
                elif step == 2:
                    for t in range(TT):
                        for half in range(2):
                            key = ("kv", run, t, half)
                            b = at_mm(act, key).rearrange("p (h n) -> p h n", h=4)
                            kd = kfull[:, t, half * 4 * QK:(half + 1) * 4 * QK].rearrange("p (h n) -> p h n", h=4)
                            act.activation(kd[:, :, 0:NOPE], b[:, :, 0:NOPE], ACT.Copy)
                            ko = (0 if s else TT) + t
                            copy(vv[:, ko, half * 4 * VH:(half + 1) * 4 * VH].rearrange("p (h n) -> p h n", h=4), b[:, :, NOPE:NOPE + VH], key)
                else:
                    for t in range(TT):
                        for hq in range(2):
                            key = ("kT", run, t, hq)
                            b = at_mm(act, key)[0:QK, :].rearrange("p (h n) -> p h n", h=4)
                            ko = ((0 if s else TT) + t) * P
                            copy(kT[0:QK, 4 * hq:4 * hq + 4, ko:ko + P], b, key)

            def zF(run):
                for t in range(TT):
                    key = ("zF", run, t)
                    copy(zfp[:, t, :], at_mm(act, key), key)

            def four(run, step):
                if step == 0:
                    for ft in range(2):
                        key = ("T1", run, ft)
                        copy(T1[:, ft, :], at_mm(act, key), key)
                    copy(poolT, at_mm(act, ("P", run)), ("P", run))
                    return
                copy(YT[:, :], at_mm(act, ("Y", run)), ("Y", run))
                b = at_mm(act, ("G", run))
                l = RUNS[run][1]
                for pair in range(2):
                    last = act.activation(ypT[:, pair * TOK:(pair + 1) * TOK], b[:, pair * TOK:(pair + 1) * TOK], ACT.Copy,
                                          scale=vecs[:, 29 * l + 3 + pair:29 * l + 4 + pair])
                release(last, ("G", run))

            def q_(run, step):
                s, l = RUNS[run]
                if step == 0:
                    for t in range(TT):
                        squares(zA[s][:, t, 0:QLORA], 4 + t, cqn[:, t, :]).then_inc(mark["qss"], 1)
                elif step == 1:
                    b = at_mm(act, ("cqT", run))
                    for k in range(2):
                        last = act.activation(cqT[:, k, :], b[:, k * TOK:(k + 1) * TOK], ACT.Copy, scale=vecs[:, 29 * l + 1 + k:29 * l + 2 + k])
                    release(last, ("cqT", run))
                elif step == 2:
                    for t in range(TT):
                        for half in range(2):
                            key = ("q", run, t, half)
                            copy(q[:, t, half * 384:(half + 1) * 384], at_mm(act, key)[:, 0:384], key)
                else:
                    for t in range(TT):
                        for hq in range(2):
                            key = ("qT", run, t, hq)
                            b = at_mm(act, key)[0:QK, :].rearrange("p (h n) -> p h n", h=4)
                            copy(qT[0:QK, 4 * hq:4 * hq + 4, t * P:(t + 1) * P], b, key, scale=ATT_SCALE)

            def att(run, i):
                nk = 4 if RUNS[run][0] == 0 else 2
                if i < H:
                    for t in range(TT):
                        key = ("s", run, i, t)
                        at_mark(act, "nmax", run, 2 * i + t + 1)
                        if i >= 2:
                            act.wait_ge(mm_done, mm_at["pT", run, i - 2, t])
                        c = 2 * (i % 2) + t
                        release(act.activation(pr[:, i % 2, t, 0:nk * P], at_mm(act, key)[:, 0:nk * P], ACT.Exp,
                                               bias=nmax[:, c:c + 1], accum_out=rsum[:, c:c + 1]), key)
                if i >= 2 and i % 2:
                    key = ("pv", run, (i - 2) // 2)
                    copy(attT[:, (i - 2) // 2, :], at_mm(act, key)[:, 0:TOK], key)
                if 1 <= i <= H:
                    if i >= 2:
                        act.wait_ge(mm_done, mm_at["pvh", run, i - 2])
                    for t in range(TT):
                        key = ("pT", run, i - 1, t)
                        b = at_mm(act, key)[:, 0:nk * P].rearrange("p (k n) -> p k n", k=nk)
                        copy(pT[:, 0:nk, t * P:(t + 1) * P], b, key)

            def gpre(run, dp, j):
                l = RUNS[run][1]
                key = ("g", run, dp, j)
                b = at_mm(act, key)
                dst = gate_at(run, dp, j)
                for dt in range(2):
                    c = j * 8 + dp * 2 + dt
                    last = act.activation(dst[:, dt * TOK:(dt + 1) * TOK], b[:, dt * TOK:(dt + 1) * TOK], ACT.Tanh,
                                          bias=hbg[:, l, c:c + 1], scale=0.5)
                release(last, key)

            def gate(run, dp, part_):
                if dp and not part_:
                    at_mark(act, "mixT", run, dp)
                for j in (() if run == "x1" else (2,) if part_ else (0, 1)):
                    gpre(run, dp, j)

            def out_(run, half):
                key = ("bm", run, half)
                copy(mb[:, half * 512:(half + 1) * 512], at_mm(act, key), key, scale=0.5)

            def pq(run, i):
                for c in (2 * i, 2 * i + 1):
                    if i:
                        key = ("sc", run, c - 2)
                        b = at_mm(act, key).rearrange("p (t n) -> p t n", t=TT)
                        copy(s_sb[:, :, (c - 2) * 256:(c - 1) * 256], b, key)
                    if i < 4:
                        key = ("qp", run, c)
                        copy(qpT[:, c % 2, :], at_mm(act, key), key)

            def route(run, t, k):
                if k >= 8:
                    hs = slice(4 * (k - 8), 4 * (k - 7))
                    at_mark(act, "topd", run, 2 * t + k - 7)
                    act.activation(te[:, hs, :], te[:, hs, :], ACT.Exp).then_inc(mark["tope"], 1)

            def gather(run, t, n0, n1, beside_a, beside_b):
                G = GATHER_NO[run, t]

                def diags(g):
                    act.wait_ge(act_ready, g + (GROUPS * G + 1))
                    for j in range(GROUP):
                        if not (isinstance(g, int) and g == 0 and j < DIAGS and G == 0):
                            act.wait_ge(upp_done, 8 * g + (P * G - DIAGS + j + 1))
                        act.activation(diag[:, j % DIAGS, :], ident[:, :], ACT.Copy, scale=act8[:, j:j + 1]).then_inc(diag_ready, 1)

                def tanh(g):
                    act.wait_ge(gelu_in, g + (GROUPS * G + 1))
                    act.activation(th8[:, :], g2[:, :], ACT.Tanh, scale=GELU_C).then_inc(gelu_th, 1)

                if beside_a or beside_b:
                    if n0:
                        diags(n0 - 1)
                    run_stages(beside_a)
                    tanh(n0)
                    run_stages(beside_b)
                else:
                    groups(act, n0, n1, lambda n: (is_group(n, 0) or diags(n - 1), tanh(n)))
                if n1 == GROUPS:
                    diags(GROUPS - 1)

            def fin(run, t):
                for half in range(2):
                    key = ("bf", run, t, half)
                    copy(mb[:, half * 512:(half + 1) * 512], at_mm(act, key), key, scale=0.5)

            def final():
                at_mark(act, "fin", "x1", 2)
                for t in range(TT):
                    squares(x[0][:, t, :], t, h[0][:, t, :]).then_inc(mark["ss"], 1)

            def pre(tag):
                act.wait_ge(x2, x2_before(tag))
                for t in range(TT):
                    squares(x[0][:, t, :], t, h[0][:, t, :]).then_inc(ss2, 1)

            def hT2(tag):
                for gi, dst in enumerate([hkT, hT] if tag == "at" else [hT]):
                    for t in range(TT):
                        for a in range(2):
                            key = ("hT2", tag, gi, t, a)
                            copy(dst[:, 4 * a:4 * a + 4, t * P:(t + 1) * P], at_mm(act, key).rearrange("p (j n) -> p j n", j=4), key)

            def gu(tag):
                m0, r0 = gu_base[tag]
                with act.Fori(0, FP_ // 2) as i:
                    for j in range(4):
                        b = ROT2[(r0 + j) % 4]
                        act.wait_ge(mm_done, 4 * i + (m0 + j + 1))
                        act.activation(fth[:, j, :], ps[:, b, 0:TOK], ACT.Tanh, scale=0.5).then_inc(gate_th, 1)
                for j in range(2):
                    act.activation(fth[:, j, :], at_mm(act, ("gu", tag, j))[:, 0:TOK], ACT.Tanh, scale=0.5).then_inc(gate_th, 1)

            def post(tag):
                for t in range(TT):
                    for half in range(2):
                        cols = slice(half * 512, (half + 1) * 512)
                        if tag == "cv":
                            act.wait_ge(bout_y, 2 * t + half + 1)
                            src, scratch = h[1][:, t, cols], h[0][:, t, cols]
                        else:
                            src, scratch = at_mm(act, ("d", tag, t, half)), h[1][:, t, cols]
                        squares(src, 2 * t + half, scratch).then_inc(ss2, 1)

            def cin():
                act.wait_ge(conv_h, 1)
                for c in range(8):
                    b = at_mm(act, ("cin", c))
                    if c >= 2:
                        act.wait_ge(conv_u, c - 1)
                    act.activation(ctmp[:, c % 2, :], b[:, TOK:2 * TOK], ACT.Tanh, bias=vec2[:, 8 + c:9 + c], scale=0.5).then_inc(conv_th, 1)

            def ln():
                act.wait_ge(ln_d, 1)
                act.activation(usq, uc, ACT.Square).then_inc(ln_v, 1)
                act.wait_ge(ln_d, 2)
                for c in range(8):
                    act.activation(usq[:, c, :], uc[:, c, :], ACT.Identity, bias=vec2[:, 280 + c:281 + c], scale=vec2[:, 272 + c:273 + c]).then_inc(ln_z, 1)
                act.wait_ge(ln_z, 8)
                act.activation(uth, usq, ACT.Tanh).then_inc(ln_t, 1)

            def qkv():
                for c in range(4):
                    b = at_mm(act, ("k2", c)).rearrange("p (h n) -> p h n", h=2)
                    copy(kT2[:, 2 * c:2 * c + 2, :], b, ("k2", c))
                for half in range(2):
                    for t in range(TT):
                        key = ("v2", "at", t, half)
                        copy(v2[:, t, half * 512:(half + 1) * 512], at_mm(act, key), key)
                for c in range(4):
                    b = at_mm(act, ("q2", c)).rearrange("p (h n) -> p h n", h=2)
                    copy(qT2[:, 2 * c:2 * c + 2, :], b, ("q2", c), scale=DH ** -0.5)

            def moba():
                def exps(hh):
                    for t in range(TT):
                        c = 2 * (hh % 2) + t
                        act.wait_ge(s2_ready, 2 * hh + t + 1)
                        pp = p2[:, hh % 2, t, :]
                        act.activation(pp, pp, ACT.Exp, bias=nmax[:, c:c + 1], accum_out=rsum[:, c:c + 1]).then_inc(act_step, 1)

                exps(0)
                for hh in range(H2):
                    if hh + 1 < H2:
                        exps(hh + 1)
                    copy(pT2.rearrange("p k n -> p (k n)"), at_mm(act, ("pT2", hh)), ("pT2", hh))
                    copy(attT2[:, hh, :], at_mm(act, ("pv2", hh))[:, 0:TOK], ("pv2", hh))

            program = {"pre": pre, "hT2": hT2, "gu": gu, "post": post, "cin": cin, "ln": ln, "qkv": qkv, "moba": moba,
                       "start": start, "norm": norm, "hT": hT_, "zA": zA_, "kv": kv, "zF": zF, "four": four, "q": q_, "att": att,
                       "gate": gate, "gpre": gpre, "out": out_, "pq": pq, "route": route, "gather": gather, "fin": fin, "final": final}

            def run_stages(stages):
                for name, *args in stages:
                    if name in program:
                        program[name](*args)

            run_stages(ORDER + ORDER2)

        @block.vector
        def _(dve):
            own = [0]

            def v(ins):
                own[0] += 1
                ins.then_inc(dve_step, 1)
                dve.wait_ge(dve_step, own[0])

            def rsqrt(dst, src, n, width):
                var, t, y = nwt[:, 0:n], nwt[:, 2:2 + n], nwi[:, 2:2 + n].bitcast(f32)
                v(dve.tensor_scalar(var, src, 1.0 / width, EPS, ALU.mult, ALU.add))
                v(dve.tensor_single_scalar(nwi[:, 0:n], var.bitcast(i32), 1, ALU.logical_shift_right))
                v(dve.tensor_scalar(nwi[:, 2:2 + n], nwi[:, 0:n], -1.0, 1597463007.0, ALU.mult, ALU.add))
                for i in range(4):
                    v(dve.tensor_tensor(t, y, y, ALU.mult))
                    v(dve.tensor_tensor(t, t, var, ALU.mult))
                    v(dve.tensor_scalar(t, t, -0.5, 1.5, ALU.mult, ALU.add))
                    v(dve.tensor_tensor(dst if i == 3 else y, y, t, ALU.mult))

            def start():
                dve.wait_ge(ld_const, 16 * 6)
                v(dve.tensor_scalar(hbg[:, :, :], vecs[:, :].rearrange("p (l n) -> p l n", l=2)[:, :, 5:29], 0.5, None, ALU.mult))
                dve.wait_ge(silu_t, 1)
                v(dve.scalar_tensor_tensor(cth[:, :, :], cth[:, :, :], 1.0, cvec[:, :, :], ALU.add, ALU.mult))
                dve.tensor_scalar(cvec[:, :, :], cth[:, :, :], 0.5, None, ALU.mult).then_inc(silu_c, 1)

            def mod(l, cc):
                if cc == 0:
                    dve.wait_ge(ld_mrow, 16 * (l + 1))
                key = ("mod", l, cc)
                b = at_mm(dve, key)
                qd, a = 32 * (cc % 4), cc // 4
                m = mrows[l][qd:qd + 2, a, :]
                release(dve.tensor_tensor(m, m, b[qd:qd + 2, :], ALU.add), key)

            gains = [0]

            def norm(run, k):
                s = RUNS[run][0]
                dve.wait_ge(mark["ss"], norm_mark(run, k, 2))
                rsqrt(ss[:, 6:8], ss[:, 0:2], 2, D)
                gains[0] += 1
                dve.wait_ge(ld_gain, 16 * gains[0])
                for half in range(2):
                    cols = slice(half * 512, (half + 1) * 512)
                    key = ("bs", run, k, half)
                    b = at_mm(dve, key)
                    release(dve.scalar_tensor_tensor(amul[:, cols], b, 1.0, gain[:, cols], ALU.add, ALU.mult), key)
                for half in range(2):
                    at_evac(dve, ("bs", run, k, half))
                for t in range(TT):
                    ins = dve.scalar_tensor_tensor(h[s][:, t, :], x[s][:, t, :], ss[:, 6 + t:7 + t], amul[:, :], ALU.mult, ALU.mult)
                    if t == TT - 1:
                        ins.then_inc(gain_used, 1)
                        dve.wait_ge(gain_used, gains[0])
                    else:
                        v(ins)
                for half in range(2):
                    cols = slice(half * 512, (half + 1) * 512)
                    key = ("bh", run, k, half)
                    b = at_mm(dve, key)
                    dve.tensor_tensor(h[s][:, 0, cols], h[s][:, 0, cols], b, ALU.add).then_inc(mark["h"], 1)
                    release(dve.tensor_tensor(h[s][:, 1, cols], h[s][:, 1, cols], b, ALU.add), key)

            def rotate(src, dst, t, heads, signal):
                cs = rope[:, t, 0:16].rearrange("p (r e) -> p r e", r=2).unsqueeze(1).broadcast_to([P, heads, 2, 8])
                sn = rope[:, t, 16:32].rearrange("p (r e) -> p r e", r=2).unsqueeze(1).broadcast_to([P, heads, 2, 8])
                s5 = src.rearrange("p h (r two e) -> p h r two e", r=2, two=2)
                d5 = dst.rearrange("p h (r two e) -> p h r two e", r=2, two=2)
                t4 = [rtmp[:, n, 0:heads * 16].rearrange("p (h r e) -> p h r e", h=heads, r=2) for n in range(4)]
                dve.tensor_tensor(t4[0], s5[:, :, :, 0, :], cs, ALU.mult)
                dve.tensor_tensor(t4[1], s5[:, :, :, 1, :], sn, ALU.mult)
                dve.tensor_tensor(t4[2], s5[:, :, :, 0, :], sn, ALU.mult)
                v(dve.tensor_tensor(t4[3], s5[:, :, :, 1, :], cs, ALU.mult))
                dve.tensor_tensor(d5[:, :, :, 0, :], t4[0], t4[1], ALU.subtract)
                signal(dve.tensor_tensor(d5[:, :, :, 1, :], t4[2], t4[3], ALU.add))

            def kv(run, step):
                if step:
                    return
                s = RUNS[run][0]
                at_mark(dve, "kvss", run, 2)
                rsqrt(ss[:, 6:8], ss[:, 2:4], 2, KVLORA)
                for t in range(TT):
                    dve.tensor_scalar(ckn[:, t, :], zA[s][:, t, QLORA:QLORA + KVLORA], ss[:, 6 + t:7 + t], None, ALU.mult).then_inc(mark["ckn"], 1)
                for t in range(TT):
                    kr = zA[s][:, t, QLORA + KVLORA:WA].unsqueeze(1)
                    if s == 0:
                        rotate(kr, kr, t, 1, v)
                    kd = kfull[:, t, :].rearrange("p (h n) -> p h n", h=H)
                    dve.tensor_copy(kd[:, :, NOPE:QK], kr.broadcast_to([P, H, ROPE])).then_inc(mark["krr"], 1)

            def q_(run, step):
                s = RUNS[run][0]
                if step == 0:
                    at_mark(dve, "qss", run, 2)
                    rsqrt(ss[:, 6:8], ss[:, 4:6], 2, QLORA)
                    for t in range(TT):
                        dve.tensor_scalar(cqn[:, t, :], zA[s][:, t, 0:QLORA], ss[:, 6 + t:7 + t], None, ALU.mult).then_inc(mark["cqn"], 1)
                elif step == 2 and s == 0:
                    for t in range(TT):
                        for half in range(2):
                            at_evac(dve, ("q", run, t, half))
                        qv = q[:, t, :].rearrange("p (h n) -> p h n", h=H)[:, :, NOPE:QK]
                        rotate(qv, qv, t, H, lambda ins: ins.then_inc(mark["qr"], 1))
                        at_mark(dve, "qr", run, t + 1)

            def att(run, i):
                nk = 4 if RUNS[run][0] == 0 else 2
                if i >= H:
                    return
                for t in range(TT):
                    key = ("s", run, i, t)
                    c = 2 * (i % 2) + t
                    dve.tensor_reduce(nmax[:, c:c + 1], at_mm(dve, key)[:, 0:nk * P], axis=AX.X, op=ALU.max, negate=True).then_inc(mark["nmax"], 1)
                for t in range(TT):
                    at_evac(dve, ("s", run, i, t))
                    c = 2 * (i % 2) + t
                    v(dve.reciprocal(rinv[:, c:c + 1], rsum[:, c:c + 1]))
                    pp = pr[:, i % 2, t, 0:nk * P]
                    dve.tensor_scalar(pp, pp, rinv[:, c:c + 1], None, ALU.mult).then_inc(mark["pn"], 1)

            def gate(run, dp, part_):
                if not part_:
                    return
                for j in range(3):
                    key = ("y", run, dp, j)
                    at_evac(dve, ("g", run, dp, j))
                    b = at_mm(dve, key)
                    m = mixT[:, 2 * dp:2 * dp + 2, :].rearrange("p k n -> p (k n)")
                    release(dve.scalar_tensor_tensor(mtmp if j else m, gate_at(run, dp, j), 1.0, b, ALU.add, ALU.mult), key)
                    at_evac(dve, key)
                    if j == 1:
                        v(dve.tensor_tensor(m, m, mtmp, ALU.add))
                    elif j == 2:
                        dve.tensor_tensor(m, m, mtmp, ALU.add).then_inc(mark["mixT"], 1)

            def out_(run, half):
                s = RUNS[run][0]
                cols = slice(half * 512, (half + 1) * 512)
                at_evac(dve, ("bm", run, half))
                for t in range(TT):
                    key = ("o", run, half, t)
                    b = at_mm(dve, key)
                    release(dve.tensor_tensor(amul[:, t * 512:(t + 1) * 512], b, mb[:, cols], ALU.mult), key)
                    at_evac(dve, key)
                    dve.tensor_tensor(x[s][:, t, cols], x[s][:, t, cols], amul[:, t * 512:(t + 1) * 512], ALU.add).then_inc(mark["resid"], 1)

            def top16(val, ind, src):
                v(dve.max(val[:, 0:8], src))
                dve.max_index(ind[:, 0:8], val[:, 0:8], src)
                v(dve.match_replace(src, val[:, 0:8], src, NEG))
                v(dve.max(val[:, 8:16], src))
                v(dve.max_index(ind[:, 8:16], val[:, 8:16], src))

            def route(run, t, k):
                l = RUNS[run][1]
                if k < 8:
                    at_evac(dve, ("sc", run, k))
                    for i in (2 * k, 2 * k + 1):
                        top16(sv[:, i, :], si[:, i, :], s_sb[:, t, i * KEYS:(i + 1) * KEYS])
                    v(dve.tensor_copy(sif[:, 2 * k:2 * k + 2, :], si[:, 2 * k:2 * k + 2, :]))
                    v(dve.tensor_tensor(cand[:, k % 2, :].rearrange("p (a b) -> p a b", a=TOP), sv[:, 2 * k, :].unsqueeze(2).broadcast_to([P, TOP, TOP]),
                                        sv[:, 2 * k + 1, :].unsqueeze(1).broadcast_to([P, TOP, TOP]), ALU.add))
                    top16(ts[:, k, :], pos[:, k, :], cand[:, k % 2, :])
                    return
                half = k - 8
                hs, cols = slice(4 * half, 4 * half + 4), slice(64 * half, 64 * half + 64)
                v(dve.tensor_tensor(te[:, hs, :], ts[:, hs, :], ts[:, hs, 0:1].broadcast_to([P, 4, TOP]), ALU.subtract))
                posf = pos.rearrange("p h k -> p (h k)")[:, cols]
                v(dve.tensor_single_scalar(pa[:, cols], posf, 4, ALU.logical_shift_right))
                v(dve.tensor_copy(fa[:, cols], pa[:, cols]))
                v(dve.tensor_single_scalar(pa[:, cols], posf, TOP - 1, ALU.bitwise_and))
                dve.tensor_copy(fb[:, cols], pa[:, cols]).then_inc(mark["topd"], 1)
                at_mark(dve, "topd", run, 2 * t + half + 1)
                e3 = eq.rearrange("p (n k) -> p n k", k=TOP)
                e4 = eq.rearrange("p (h n k) -> p h n k", h=4, k=TOP)
                sf4 = sif.rearrange("p (h two) k -> p h two k", two=2)
                for which, f, i_ in ((0, fa, ia), (1, fb, ib)):
                    v(dve.tensor_tensor(e3, f[:, cols].unsqueeze(2).broadcast_to([P, 64, TOP]), iota[:, :].unsqueeze(1).broadcast_to([P, 64, TOP]), ALU.is_equal))
                    v(dve.tensor_tensor(e4, e4, sf4[:, hs, which, :].unsqueeze(2).broadcast_to([P, 4, TOP, TOP]), ALU.mult))
                    v(dve.tensor_reduce(i_[:, cols], e3, axis=AX.X, op=ALU.add))
                v(dve.scalar_tensor_tensor(ia[:, cols], ia[:, cols], float(KEYS), ib[:, cols], ALU.mult, ALU.add))
                v(dve.tensor_scalar(idx[t][:, cols], ia[:, cols], float(l * KEYS * KEYS), None, ALU.add))
                at_mark(dve, "tope", run, 2 * t + half + 1)
                v(dve.tensor_reduce(tsum[:, hs], te[:, hs, :], axis=AX.X, op=ALU.add))
                v(dve.reciprocal(tsum[:, hs], tsum[:, hs]))
                dve.tensor_tensor(gates[t][:, cols].rearrange("p (h k) -> p h k", k=TOP), te[:, hs, :],
                                  tsum[:, hs].unsqueeze(2).broadcast_to([P, 4, TOP]), ALU.mult).then_inc(mark["route"], 1)
                at_mark(dve, "route", run, 2 * t + half + 1)

            def gather(run, t, n0, n1, beside_a, beside_b):
                s = RUNS[run][0]
                G = GATHER_NO[run, t]
                if n0 == 0:
                    v(dve.memset(accv[:, :], 0.0))

                def down(g, first=False):
                    for j in range(GROUP):
                        dve.wait_ge(row_in[j], (16 * (32 * G + 1)) if first else 32 * g + 16 * (32 * G))
                        dve.tensor_tensor_reduce(out=rows[:, j, :], in0=rows[:, j, :], in1=h[s][:, t, :], scale=1.0, scalar=0.0,
                                                 op0=ALU.mult, op1=ALU.add, accum_out=a8[:, j:j + 1]).then_inc(down_done, 1)
                    base = 3 * GROUPS * G
                    dve.wait_ge(down_done, 8 * g + (P * G + GROUP))
                    dve.tensor_tensor(g1[:, :], a8[:, :], a8[:, :], ALU.mult).then_inc(gelu_step, 1)
                    dve.wait_ge(gelu_step, 3 * g + (base + 1))
                    dve.tensor_scalar(g1[:, :], g1[:, :], GELU_A, 1.0, ALU.mult, ALU.add).then_inc(gelu_step, 1)
                    dve.wait_ge(gelu_step, 3 * g + (base + 2))
                    dve.tensor_tensor(g2[:, :], g1[:, :], a8[:, :], ALU.mult).then_inc(gelu_in, 1)

                def up(g, last=False):
                    for j in range(GROUP):
                        dve.wait_ge(row_in[j], (16 * (32 * G + 32)) if last else 32 * g + (16 * (32 * G + 3)))
                        if isinstance(g, int) and g == 0 and j == 0:
                            dve.wait_ge(act_ready, GROUPS * G + 1)
                        else:
                            dve.wait_ge(upv_done, 8 * g + (P * G + j))
                        dve.scalar_tensor_tensor(accv[:, :], rows[:, j, 0:UPV], act8[:, j:j + 1], accv[:, :], ALU.mult, ALU.add).then_inc(upv_done, 1)

                def act_of(g, first=False):
                    base = 3 * GROUPS * G
                    dve.wait_ge(gelu_th, g + (GROUPS * G + 1))
                    dve.scalar_tensor_tensor(g1[:, :], th8[:, :], 1.0, a8[:, :], ALU.add, ALU.mult).then_inc(gelu_step, 1)
                    dve.wait_ge(gelu_step, 3 * g + (base + 3))
                    if not first:
                        dve.wait_ge(diag_ready, 8 * g + P * G)
                        dve.wait_ge(upv_done, 8 * g + P * G)
                    gt = gates[t][:, 0:GROUP] if first else gates[t][:, bass.ds(g * GROUP, GROUP)]
                    dve.tensor_tensor(act8[:, :], g1[:, :], gt, ALU.mult).then_inc(act_ready, 1)
                    dve.wait_ge(act_ready, g + (GROUPS * G + 1))

                def group(n, stages_a=(), stages_b=()):
                    first = is_group(n, 0)
                    down(n, first)
                    run_stages(stages_a)
                    if not first:
                        up(n - 1)
                    act_of(n, first)
                    run_stages(stages_b)

                if beside_a or beside_b:
                    group(n0, beside_a, beside_b)
                else:
                    groups(dve, n0, n1, group)
                if n1 == GROUPS:
                    up(GROUPS - 1, True)

            def fin(run, t):
                s = RUNS[run][0]
                G = GATHER_NO[run, t]
                for half in range(2):
                    at_evac(dve, ("bf", run, t, half))
                dve.wait_ge(upv_done, P * (G + 1))
                v(dve.tensor_tensor(accv[:, :], accv[:, :], mb[:, 0:UPV], ALU.mult))
                dve.wait_ge(upp_done, P * (G + 1))
                v(dve.tensor_tensor(mb[:, UPV:D], ps[:, UPB, :], mb[:, UPV:D], ALU.mult))
                v(dve.tensor_tensor(x[s][:, t, 0:UPV], x[s][:, t, 0:UPV], accv[:, :], ALU.add))
                dve.tensor_tensor(x[s][:, t, UPV:D], x[s][:, t, UPV:D], mb[:, UPV:D], ALU.add).then_inc(mark["fin"], 1)
                at_mark(dve, "fin", run, t + 1)

            def final():
                dve.wait_ge(mark["ss"], 2 * 8)
                rsqrt(ss[:, 6:8], ss[:, 0:2], 2, D)
                gains[0] += 1
                dve.wait_ge(ld_gain, 16 * gains[0])
                for t in range(TT):
                    dve.scalar_tensor_tensor(x[0][:, t, :], x[0][:, t, :], ss[:, 6 + t:7 + t], gain[:, :], ALU.mult, ALU.mult).then_inc(x2, 1)

            g2n = [0]

            def next_gain():
                n = g2n[0]
                g2n[0] += 1
                dve.wait_ge(gain2_in[n % 2], 16 * (n // 2 + 1))
                return gain2[n % 2]

            def pre(tag):
                dve.wait_ge(ss2, SS2_AT["pre", tag])
                rsqrt(ss[:, 6:8], ss[:, 0:2], 2, D)
                for dst in ([h[1], h[0]] if tag == "at" else [h[0]]):
                    g = next_gain()
                    for t in range(TT):
                        dve.scalar_tensor_tensor(dst[:, t, :], x[0][:, t, :], ss[:, 6 + t:7 + t], g[:, :], ALU.mult, ALU.mult).then_inc(h2m, 1)
                    dve.wait_ge(h2m, H2_AT[tag] - (2 if dst is h[1] else 0))
                    dve.sem_inc(gain2_used, 1)

            def gu(tag):
                m0, r0 = gu_base[tag]
                n = int(tag[1])
                done = FT * n

                def silu_up(b, j, kt, th_at, step_at):
                    dve.wait_ge(gate_th, th_at)
                    dve.scalar_tensor_tensor(ft2[:, j, :], fth[:, j, :], 1.0, ps[:, b, 0:TOK], ALU.add, ALU.mult).then_inc(gu_step, 1)
                    dve.wait_ge(gu_step, step_at)
                    return dve.tensor_tensor(hid[:, kt, :] if isinstance(kt, int) else hid[:, bass.ds(kt, 1), :], ft2[:, j, :] if isinstance(kt, int) else ft2[:, j:j + 1, :],
                                             ps[:, b, TOK:2 * TOK] if isinstance(kt, int) else ps[:, b:b + 1, TOK:2 * TOK], ALU.mult)

                with dve.Fori(0, FP_ // 2) as i:
                    for j in range(4):
                        b = ROT2[(r0 + j) % 4]
                        ins = silu_up(b, j, 4 * i + j, 4 * i + (done + j + 1), 8 * i + (2 * done + 2 * j + 1))
                        ins.then_inc(gu_step, 1)
                        dve.wait_ge(gu_step, 8 * i + (2 * done + 2 * j + 2))
                        dve.sem_inc(bank_free[b], 1)
                for j in range(2):
                    key = ("gu", tag, j)
                    ins = silu_up(job_bank[key], j, FT - 2 + j, done + FT - 1 + j, 2 * (done + FT) - 3 + 2 * j)
                    ins.then_inc(gu_step, 1)
                    dve.wait_ge(gu_step, 2 * (done + FT) - 2 + 2 * j)
                    dve.sem_inc(bank_free[job_bank[key]], 1)

            def post(tag):
                ffn = tag[0] == "f"
                if tag == "cv":
                    for t in range(TT):
                        for half in range(2):
                            cols = slice(half * 512, (half + 1) * 512)
                            key = ("d", tag, t, half)
                            dve.tensor_tensor(h[1][:, t, cols], at_mm(dve, key), bout_b[:, cols], ALU.add).then_inc(bout_y, 1)
                            dve.wait_ge(bout_y, 2 * t + half + 1)
                            dve.sem_inc(bank_free[job_bank[key]], 1)
                g = next_gain()
                dve.wait_ge(ss2, SS2_AT["post", tag])
                s4 = ss[:, 0:4].rearrange("p (t a) -> p t a", t=TT)
                v(dve.tensor_tensor(nwt[:, 4:6], s4[:, :, 0], s4[:, :, 1], ALU.add))
                rsqrt(ss[:, 6:8], nwt[:, 4:6], 2, (4 if ffn else 1) * D)
                if ffn:
                    v(dve.tensor_scalar(ss[:, 6:8], ss[:, 6:8], 0.25, None, ALU.mult))
                for t in range(TT):
                    for half in range(2):
                        cols = slice(half * 512, (half + 1) * 512)
                        key = ("d", tag, t, half)
                        src = h[1][:, t, cols] if tag == "cv" else at_mm(dve, key)
                        v(dve.scalar_tensor_tensor(h[1][:, t, cols], src, ss[:, 6 + t:7 + t], g[:, cols], ALU.mult, ALU.mult))
                        if tag != "cv":
                            dve.sem_inc(bank_free[job_bank[key]], 1)
                    if t == TT - 1:
                        dve.sem_inc(gain2_used, 1)
                    dve.tensor_tensor(x[0][:, t, :], x[0][:, t, :], h[1][:, t, :], ALU.add).then_inc(x2, 1)
                dve.wait_ge(x2, X2_AT[tag])

            def cin():
                dve.wait_ge(ld_vec2, 16 * 2)
                v(dve.memset(upad[:, :, 0:PAD], 0.0))
                dve.memset(ones, 1.0 / D).then_inc(ones_set, 1)
                v(dve.tensor_scalar(vec2[:, 8:16], vec2[:, 8:16], 0.5, None, ALU.mult))
                dve.tensor_scalar(vec2[:, 272:288], vec2[:, 272:288], 0.5, None, ALU.mult).then_inc(conv_h, 1)
                for c in range(8):
                    key = ("cin", c)
                    b = at_mm(dve, key)
                    tmp = rows[:, 2, 512:512 + TOK]
                    dve.wait_ge(conv_th, c + 1)
                    v(dve.tensor_scalar(tmp, b[:, 0:TOK], vec2[:, c:c + 1], 0.5, ALU.add, ALU.mult))
                    dve.scalar_tensor_tensor(upad[:, c, PAD:PAD + TOK], ctmp[:, c % 2, :], 1.0, tmp, ALU.add, ALU.mult).then_inc(conv_u, 1)
                    dve.wait_ge(conv_u, c + 1)
                    dve.sem_inc(bank_free[job_bank[key]], 1)
                    for j in range(TAPS):
                        w = vec2[:, 16 + j * 8 + c:17 + j * 8 + c]
                        if j == 0:
                            v(dve.tensor_scalar(uc[:, c, :], upad[:, c, 0:TOK], w, vec2[:, 264 + c:265 + c], ALU.mult, ALU.add))
                        else:
                            ins = dve.scalar_tensor_tensor(uc[:, c, :], upad[:, c, j:j + TOK], w, uc[:, c, :], ALU.mult, ALU.add)
                            if j < TAPS - 1:
                                v(ins)
                            else:
                                ins.then_inc(conv_y, 1)
                                dve.wait_ge(conv_y, c + 1)

            def ln():
                b = at_mm(dve, ("mean",))
                bc = b[:, 0:TOK].unsqueeze(1).broadcast_to([P, 8, TOK])
                dve.tensor_tensor(uc, uc, bc, ALU.subtract).then_inc(ln_d, 1)
                dve.wait_ge(ln_d, 1)
                dve.sem_inc(bank_free[job_bank["mean",]], 1)
                b = at_mm(dve, ("var",))
                v(dve.tensor_scalar(rl2, b[:, 0:TOK], LN_EPS, None, ALU.add))
                dve.sem_inc(bank_free[job_bank["var",]], 1)
                y = rli.bitcast(f32)
                v(dve.tensor_single_scalar(rli2, rl2.bitcast(i32), 1, ALU.logical_shift_right))
                v(dve.tensor_scalar(rli, rli2, -1.0, 1597463007.0, ALU.mult, ALU.add))
                for i in range(4):
                    v(dve.tensor_tensor(rln, y, y, ALU.mult))
                    v(dve.tensor_tensor(rln, rln, rl2, ALU.mult))
                    v(dve.tensor_scalar(rln, rln, -0.5, 1.5, ALU.mult, ALU.add))
                    v(dve.tensor_tensor(y, y, rln, ALU.mult))
                dve.wait_ge(ln_v, 1)
                dve.tensor_tensor(uc, uc, y.unsqueeze(1).broadcast_to([P, 8, TOK]), ALU.mult).then_inc(ln_d, 1)
                dve.wait_ge(ln_t, 1)
                dve.scalar_tensor_tensor(uth, uth, 1.0, usq, ALU.add, ALU.mult).then_inc(ln_s, 1)

            def moba():
                dve.wait_ge(ld_vec2, 16 * 3)
                e0 = [0]

                def biased(hh):
                    for t in range(TT):
                        c = 2 * (hh % 2) + t
                        b = at_mm(dve, ("s2", hh))
                        if hh >= 2:
                            dve.wait_ge(mm_done, mm_at["pT2", hh - 2])
                        pp = p2[:, hh % 2, t, :]
                        v(dve.scalar_tensor_tensor(pp, dist[:, t, :], -(2.0 ** -(hh + 1)), b[:, t * TOK:(t + 1) * TOK], ALU.mult, ALU.add))
                        if t:
                            dve.sem_inc(bank_free[job_bank["s2", hh]], 1)
                        dve.tensor_reduce(nmax[:, c:c + 1], pp, axis=AX.X, op=ALU.max, negate=True).then_inc(s2_ready, 1)

                biased(0)
                for hh in range(H2):
                    if hh + 1 < H2:
                        biased(hh + 1)
                    for t in range(TT):
                        c = 2 * (hh % 2) + t
                        dve.wait_ge(act_step, 2 * hh + t + 1)
                        v(dve.reciprocal(rinv[:, c:c + 1], rsum[:, c:c + 1]))
                        pp = p2[:, hh % 2, t, :]
                        dve.tensor_scalar(pp, pp, rinv[:, c:c + 1], None, ALU.mult).then_inc(p2_ready, 1)

            program = {"pre": pre, "gu": gu, "post": post, "cin": cin, "ln": ln, "moba": moba,
                       "start": start, "mod": mod, "norm": norm, "kv": kv, "q": q_, "att": att, "gate": gate, "out": out_, "route": route,
                       "gather": gather, "fin": fin, "final": final}

            def run_stages(stages):
                for name, *args in stages:
                    if name in program:
                        program[name](*args)

            run_stages(ORDER + ORDER2)

        @block.sync
        def _(sp):
            for dst, src in ((cvec[:, :, :], A["cvec"]), (ident[:, :], A["ident"]), (sel[:, :, :], A["sel"]), (rope[:, :, :], A["rope"]),
                             (iota[:, :], A["iota"]), (vecs[:, :], A["vecs"])):
                sp.dma_start(dst, src).then_inc(ld_const, 16)
            sp.dma_start(x[1][:, :, :], A["ctx"].rearrange("(t p) d -> p t d", p=P)).then_inc(ld_c, 16)
            sp.dma_start(mrows[0][:, :, :], A["bmod"][0]).then_inc(ld_mrow, 16)
            gains, n = [0], [0]

            def chunks(k):
                for _ in range(k):
                    c = n[0]
                    n[0] += 1
                    if c >= SLOTS:
                        sp.wait_ge(mm_done, chunk_done[c - SLOTS])
                    name, at_, width = plan[c]
                    sp.dma_start(wring[:, c % SLOTS, 0:width], A[name][at_] if at_ else A[name]).then_inc(chunk_in[c % SLOTS], 16)

            def load_gain(vec):
                if gains[0]:
                    sp.wait_ge(gain_used, gains[0])
                gains[0] += 1
                sp.dma_start(gain[:, :], vec.unsqueeze(0).broadcast_to([P, D])).then_inc(ld_gain, 16)

            def per_stage(name, *args):
                if name == "gate":
                    return 1 if args[0] == "x1" else 2
                if name in ("kv", "q"):
                    return int(args[1] == 2)
                return {"mod": 2, "zA": 2, "zF": 2, "four": 2 - args[-1] if name == "four" else 0, "gpre": 1, "out": 2}.get(name, 2 * (name == "pq" and args[1] < 4))

            for name, *args in STAGES:
                if name == "mod" and args == [1, 0]:
                    sp.dma_start(mrows[1][:, :, :], A["bmod"][1]).then_inc(ld_mrow, 16)
                if name == "norm":
                    load_gain(A["norm2_g" if args[1] else "norm1_g"][RUNS[args[0]][1]])
                elif name == "final":
                    load_gain(A["final_g"])
                elif name == "pq" and args[1] == 0:
                    prev = {"x0": None, "c0": "x0", "x1": "c0"}[args[0]]
                    if prev:
                        sp.wait_ge(mm_done, mm_at["sc", prev, 7])
                    chunks(2)
                    sp.wait_ge(gain_used, gains[0])
                    sp.dma_start(keysT[:, :], A["keysT"][RUNS[args[0]][1]]).then_inc(ld_keys, 16)
                else:
                    chunks(per_stage(name, *args))
                if name == "mod" and args == [0, 3]:
                    sp.dma_start(x[0][:, :, :], A["x"].rearrange("(t p) d -> p t d", p=P)).then_inc(ld_x, 16)

            plan_2 = plan2()
            n2, g2n = [0], [0]

            def slot2_free(c):
                if c >= SLOTS2:
                    sp.wait_ge(mm_done, chunk2_done[c - SLOTS2])
                elif c < SLOTS:
                    last = max(m for m in range(len(plan)) if m % SLOTS == c)
                    sp.wait_ge(mm_done, chunk_done[last])
                else:
                    sp.wait_ge(x2, 2)

            def chunks2(k):
                for _ in range(k):
                    c = n2[0]
                    n2[0] += 1
                    slot2_free(c)
                    name, at_ = plan_2[c]
                    sp.dma_start(W2[c % SLOTS2], A[name][at_]).then_inc(chunk2_in[c % SLOTS2], 16)

            def load_gain2(vec):
                n = g2n[0]
                g2n[0] += 1
                if n >= 2:
                    sp.wait_ge(gain2_used, n - 1)
                else:
                    sp.wait_ge(x2, 2)
                sp.dma_start(gain2[n % 2][:, :], vec.unsqueeze(0).broadcast_to([P, D])).then_inc(gain2_in[n % 2], 16)

            for name, *args in ORDER2:
                if name == "pre":
                    tag = args[0]
                    if tag[0] == "f":
                        load_gain2(A["ffn_pre"][int(tag[1])])
                        load_gain2(A["ffn_post"][int(tag[1])])
                    elif tag == "cv":
                        sp.wait_ge(x2, X2_AT["f0"])
                        load_gain2(A["mix_pre"][0])
                        load_gain2(A["mix_post"][0])
                        sp.dma_start(vec2, A["vec2"]).then_inc(ld_vec2, 16)
                        sp.dma_start(bout_b, A["b_out"].unsqueeze(0).broadcast_to([P, D])).then_inc(ld_vec2, 16)
                    else:
                        load_gain2(A["kv_norm"])
                        load_gain2(A["mix_pre"][1])
                        sp.dma_start(dist, A["dist"]).then_inc(ld_vec2, 16)
                elif name == "gu":
                    chunks2(4)
                    n0 = n2[0]
                    f = plan_2[n0][1][0]
                    done0 = [chunk2_done[n0 + c - SLOTS2] for c in range(4)]
                    assert [chunk2_done[n0 + 4 * i + c - SLOTS2] for i in range(4) for c in range(4)] == [4 * i + done0[c] for i in range(4) for c in range(4)]
                    with sp.Fori(0, FP_ // 2 - 1) as i:
                        for c in range(4):
                            sp.wait_ge(mm_done, 4 * i + done0[c])
                            sp.dma_start(W2[(n0 + c) % SLOTS2], A["wgu"][f, bass.ds(4 * i + (4 + c), 1)].rearrange("a p n -> p (a n)")).then_inc(chunk2_in[(n0 + c) % SLOTS2], 16)
                    n2[0] += 4 * (FP_ // 2 - 1)
                    chunks2(2)
                elif name == "post" and args[0] == "at":
                    load_gain2(A["mix_post"][1])
                elif name == "store":
                    sp.wait_ge(x2, X2_AT["f3"])
                    sp.dma_start(out.rearrange("(t p) d -> p t d", p=P), x[0][:, :, :]).then_inc(out_done, 16)
                    sp.wait_ge(out_done, 16)
                else:
                    chunks2({"dn": FT // 2, "cin": 8, "cout": 4, "qkv": 12, "ao": 4}.get(name, 0))

        @block.gpsimd
        def _(pool):
            copies = [0]

            def gather(run, t):
                G = GATHER_NO[run, t]
                at_mark(pool, "route", run, 2 * t + 1)
                if G:
                    at_mark(pool, "fin", GATHERS[G - 1][0], GATHERS[G - 1][1] + 1)

                def fetch(table, offs, j):
                    pool.sem_inc(slot_ok, 1)
                    pool.indirect_dma_start(out=rows[:, j, :], out_offset=None, in_=table,
                                            in_offset=bass.IndirectOffsetOnAxis(ap=offs[:, j:j + 1], axis=0)).then_inc(row_in[j], 16)

                def down(g, par, first=None):
                    src = idx[t][:, 0:GROUP] if first == 0 else idx[t][:, bass.ds(g * GROUP, GROUP)]
                    pool.tensor_copy(idown[par][:, :], src).then_inc(idx_copied, 1)
                    pool.wait_ge(idx_copied, 2 * g + (2 * GROUPS * G + (1 if first == 0 else 0)))
                    for j in range(GROUP):
                        if first == 1:
                            pool.wait_ge(down_done, P * G + j + 1)
                        elif first is None:
                            pool.wait_ge(upv_done, 8 * g + (P * G - 2 * GROUP + j + 1))
                            pool.wait_ge(upp_done, 8 * g + (P * G - 2 * GROUP + j + 1))
                        fetch(A["peer_down"], idown[par], j)

                def up(g, par, last=False):
                    pool.tensor_copy(iup[par][:, :], idx[t][:, bass.ds(g * GROUP, GROUP)]).then_inc(idx_copied, 1)
                    pool.wait_ge(idx_copied, 2 * g + (2 * GROUPS * G + (2 if last else 3)))
                    for j in range(GROUP):
                        if last:
                            pool.wait_ge(upv_done, 8 * g + (P * G - GROUP + j + 1))
                            pool.wait_ge(upp_done, 8 * g + (P * G - GROUP + j + 1))
                        else:
                            pool.wait_ge(down_done, 8 * g + (P * G + GROUP + j + 1))
                        fetch(A["peer_up"], iup[par], j)

                down(0, 0, 0)
                down(1, 1, 1)
                up(0, 0)
                for m0 in range(2):
                    if m0:
                        at_mark(pool, "route", run, 2 * t + 2)
                    with pool.Fori((1, GROUPS // 4)[m0], (GROUPS // 4, GROUPS // 2)[m0]) as m:
                        down(m * 2, 0)
                        up(m * 2 - 1, 1)
                        down(m * 2 + 1, 1)
                        up(m * 2, 0)
                up(GROUPS - 1, 1, True)

            for run, t in GATHERS:
                gather(run, t)


def tiles(w, k0, nk, c0, nc):
    return w[k0 * P:(k0 + nk) * P, c0:c0 + nc].reshape(nk, P, nc).transpose(1, 0, 2).reshape(P, nk * nc)


def column_chunks(w, nk, nc):
    return np.stack([np.stack([tiles(w, k0, nk, c0, nc) for k0 in range(0, w.shape[0] // P, nk)]) for c0 in range(0, w.shape[1], nc)])


def constants():
    n = np.arange(TOK)
    ang = 2 * np.pi * ((n[:, None] * n[None, :]) % TOK) / TOK
    dft = np.concatenate([np.cos(ang), np.sin(ang), -np.sin(ang)], 1).astype(np.float32) / np.float32(16)
    pool = np.zeros((4, TOK, TOK), np.float32)
    for g, w in enumerate((2, 4, 8, 16)):
        lo, hi = np.clip(n - w // 2, 0, TOK), np.clip(n - w // 2 + w, 0, TOK)
        for t in range(TOK):
            pool[g, lo[t]:hi[t], t] = np.float32(1) / np.float32(hi[t] - lo[t])
            pool[g, t, t] -= 1
    half = ROPE // 2
    inv = (np.float32(10000.0) ** (-np.arange(0, half, 2, dtype=np.float32) / half)).astype(np.float32)
    ar, ac = ((n // 64).astype(np.float32)[:, None] * inv), ((n % 64).astype(np.float32)[:, None] * inv)
    rope = np.concatenate([np.cos(ar), np.cos(ac), np.sin(ar), np.sin(ac)], 1).astype(np.float32)
    sel = np.zeros((P, 2, P), np.float32)
    for qd in range(4):
        for s in range(2):
            sel[32 * qd + s, s] = 1
    return {
        "dft": tiles(dft, 0, 2, 0, 768), "poolm": pool.reshape(4, 2, P, TOK).transpose(2, 1, 0, 3).reshape(P, -1),
        "rope": rope.reshape(TT, P, 32).transpose(1, 0, 2), "sel": sel, "ident": np.eye(P, dtype=np.float32),
        "dist": np.where(n[:, None] >= n[None, :], n[:, None] - n[None, :], 1e33).astype(np.float32).reshape(TT, P, TOK).transpose(1, 0, 2),
        "iota": np.tile(np.arange(TOP, dtype=np.float32), (P, 1)),
    }


def layout(i):
    cols = lambda v: v.reshape(-1, P).T
    bmod = np.zeros((2, P, 3, 512), np.float32)
    for l in range(2):
        for cc in range(12):
            for s in range(2):
                bmod[l, 32 * (cc % 4) + s, cc // 4] = i["b_mod"][l, cc * 512:(cc + 1) * 512]
    wgrp = np.zeros((2, P, 2, P), np.float32)
    for l in range(2):
        for g in range(4):
            po = 64 * (g % 2)
            wgrp[l, po:po + 64, g // 2, po:po + 64] = i["w_grp"][l, g]
    vecs = [np.concatenate([cols(i["kv_norm_g"][l]), cols(i["q_norm_g"][l]), cols(i["pool_scale"][l]), cols(i["b_gate"][l])], 1) for l in range(2)]
    w_in = i["w_in"]
    a = {
        "x": i["x"][0], "ctx": i["ctx"][0],
        "cvec": np.stack([cols(i["c"][0]), cols(i["c_ctx"])], 2),
        "bmod": bmod, "vecs": np.concatenate(vecs, 1), "norm1_g": i["norm1_g"], "norm2_g": i["norm2_g"], "final_g": i["final_g"],
        "wmod": np.stack([column_chunks(i["w_mod"][l], 4, 512).reshape(24, P, SLOT_W) for l in range(2)]),
        "wA": np.stack([column_chunks(w_in[l][:, 0:WA], 4, WA)[0] for l in range(2)]),
        "wZ": np.stack([column_chunks(w_in[l][:, WA:WA + WZ], 4, WZ)[0] for l in range(2)]),
        "wG": np.stack([column_chunks(w_in[l][:, WA + WZ:], 8, 256).reshape(3, 4, P, SLOT_W).transpose(1, 0, 2, 3) for l in range(2)]),
        "wO": np.stack([column_chunks(np.concatenate([i["w_oa"][l], i["w_ob"][l], i["w_oc"][l]], 0), 8, 256)[:, 0] for l in range(2)]),
        "wuq": np.stack([tiles(i["w_uq"][l], 0, 2, 0, 768) for l in range(2)]), "wukv": i["w_ukv"], "wgrp": wgrp.reshape(2, P, 256),
        "wout": np.stack([column_chunks(i["w_out"][l], 4, 512).reshape(4, P, SLOT_W) for l in range(2)]),
        "wpq": np.stack([column_chunks(i["w_pq"][l], 8, 256)[:, 0] for l in range(2)]),
        "keysT": i["peer_keys"].transpose(0, 4, 1, 2, 3).reshape(2, P, HP * KEYS),
        "peer_down": i["peer_down"].reshape(-1, D), "peer_up": i["peer_up"].reshape(-1, D),
    }
    gu = i["ffn_w_gate_up_2"].reshape(4, D, 2, FF)
    v2 = [cols(i[n][0]) for n in ("conv_b_in_2",)] + [i["conv_w_dw_2"][0].reshape(TAPS, 8, P).transpose(2, 0, 1).reshape(P, TAPS * 8)]
    v2 += [cols(i[n][0]) for n in ("conv_b_dw_2", "conv_ln_g_2", "conv_ln_b_2")]
    a.update({
        "wgu": np.stack([np.stack([column_chunks(gu[n, :, g], 8, 256)[:, 0] for g in range(2)], 1).reshape(2 * FP_, P, SLOT_W) for n in range(4)]),
        "wdn": np.stack([np.stack([tiles(w, 2 * c, 2, 0, D) for c in range(FT // 2)]) for w in i["ffn_w_down_2"].reshape(4, FF, D)]),
        "ffn_pre": i["ffn_norm_pre_2"].reshape(4, D), "ffn_post": i["ffn_norm_post_2"].reshape(4, D),
        "mix_pre": i["mix_norm_pre_2"], "mix_post": i["mix_norm_post_2"], "kv_norm": i["kv_norm_2"], "b_out": i["conv_b_out_2"][0],
        "vec2": np.concatenate(v2, 1),
        "cwin": np.stack([column_chunks(i["conv_w_in_2"][0][:, s * D:(s + 1) * D], 8, 256)[:, 0] for s in range(2)], 1).reshape(8, P, SLOT_W),
        "cwout": column_chunks(i["conv_w_out_2"][0], 4, 512).reshape(4, P, SLOT_W),
        "w2k": column_chunks(i["w_kv_2"][:, 0:D], 8, 256)[:, 0], "w2v": column_chunks(i["w_kv_2"][:, D:], 4, 512).reshape(4, P, SLOT_W),
        "w2q": column_chunks(i["attn_w_q_2"][0], 8, 256)[:, 0], "w2o": column_chunks(i["attn_w_o_2"][0], 4, 512).reshape(4, P, SLOT_W),
    })
    a.update(constants())
    return {k: np.ascontiguousarray(v, dtype=np.float32) for k, v in a.items()}


def kernel(**inputs):
    import concourse.bacc as bacc
    from concourse.bass_utils import run_bass_kernel_spmd

    nc = bacc.Bacc("TRN2", target_bir_lowering=False, num_devices=1)
    arrays = {f"in_{name}": a for name, a in layout({k: np.asarray(v) for k, v in inputs.items()}).items()}
    A = {name[3:]: nc.dram_tensor(name, a.shape, mybir.dt.from_np(a.dtype), kind="ExternalInput").ap() for name, a in arrays.items()}
    out = nc.dram_tensor("out_0", (TOK, D), mybir.dt.float32, kind="ExternalOutput").ap()
    build(nc, A, out)
    result = run_bass_kernel_spmd(nc, [arrays], core_ids=[0])
    return result.results[0]["out_0"].reshape(1, TOK, D)
```

```python
from contextlib import ExitStack

import numpy as np

import concourse.bass as bass
from concourse import mybir

P = 128
D = 1024
KT = D // P
TOK = 256
TT = TOK // P
EPS = 1e-6
H = 8
NOPE, ROPE, VH = 64, 32, 64
QK = NOPE + ROPE
QLORA, KVLORA = 256, 128
ATT_SCALE = QK ** -0.5
WA = QLORA + KVLORA + ROPE
WZ = 512
HP = 16
KEYS = 128
TOP = 16
NEG = -3.0e38
GROUP = 8
GROUPS = P // GROUP
SLOTS = 3
SLOT_W = 2048
DIAGS = 4
NEWTON = 3
GELU_C = 0.7978845608028654
GELU_A = 0.044715

RUNS = {"c0": (1, 0), "x0": (0, 0), "x1": (0, 1), "c1": (1, 1)}
GATHERS = [(r, t) for r in ("x0", "c0", "x1") for t in range(TT)]
GATHER_NO = {g: n for n, g in enumerate(GATHERS)}


def keys_stages(r):
    return [("norm", r, 0), ("hT", r, 0), ("zA", r)] + [("kv", r, k) for k in range(4)]


def branches(r):
    return [[("zF", r)], [("four", r, 0), ("q", r, 0)], [("four", r, 1), ("q", r, 1)], [("q", r, 2)], [("q", r, 3)]]


def heads(r):
    return [[("att", r, i)] for i in range(H + 2)]


def mixing(r):
    return [[("gate", r, dp, part)] for dp in range(4) for part in ((0, 1) if r != "x1" else (1,))] + [[("out", r, half)] for half in range(2)] + [[("norm", r, 1)], [("hT", r, 1)]]


def scoring(r):
    if r == "c0":
        ranks = [[("route", r, 0, k)] for k in (0, 1, 2, 3, 8, 4, 5, 6, 7, 9)]
        return [[("pq", r, 0)]] + [x for i in range(1, 5) for x in ([("pq", r, i)], ranks[i - 1])] + ranks[4:]
    ranks = [[], [0, 1], [2, 3, 8], [4, 5]]
    return [[("pq", r, i)] + [("route", r, 0, k) for k in ranks[i]] for i in range(4)]


def ranking(r, t):
    first = [[("route", r, t, 0)], [("route", r, t, 1)], [("route", r, t, 2)], [("route", r, t, 3)], [("route", r, t, 8)]]
    rest = [[("route", r, t, k)] for k in (4, 5, 6, 7, 9)]
    return first + rest if t else [[("pq", r, 4)] + rest[2]] + rest[3:]


HEAVY = ("zF", "zA", "gate", "gpre", "out", "pq")


def during(r, t, pieces, most=2):
    slots, rest = [], list(pieces)
    for n in range(GROUPS):
        a = rest.pop(0) if rest else []
        b = rest.pop(0) if rest and most == 2 and not (rest[0][0][0] in HEAVY and a[0][0] in HEAVY) else []
        slots.append((a, b))
    out, n = [], 0
    while n < GROUPS:
        m = n + 1
        if not slots[n][0] and not slots[n][1]:
            while m < GROUPS and not slots[m][0] and not slots[m][1]:
                m += 1
        out.append(("gather", r, t, n, m, *slots[n]))
        n = m
    return out + [("fin", r, t)], rest


def flat(pieces):
    return [st for p in pieces for st in p]


def interleave(a, b):
    out, k = [], 0
    for n, st in enumerate(a):
        out.append(st)
        while k < (n + 1) * len(b) // len(a):
            out.append(b[k])
            k += 1
    return out


def mods(l, ccs):
    return [("mod", l, cc) for cc in ccs]


def order():
    o = [("start",)] + mods(0, range(4))
    x = branches("x0")
    units = [[st] for st in keys_stages("c0") + keys_stages("x0")] + [x[0], x[1] + x[2]] + x[3:] + heads("x0")
    o += flat(interleave(units, [[st] for st in mods(0, range(4, 12))]))
    o += flat(mixing("x0") + scoring("x0"))
    beside = ranking("x0", 0) + ranking("x0", 1) + [[("hT", "c0", 2)]] + branches("c0") + heads("c0") + mixing("c0") + scoring("c0")
    for t in range(TT):
        part, beside = during("x0", t, beside)
        o += part
    o += flat(beside)
    m = [[st] for st in mods(1, range(12))]
    r = ranking("c0", 1)
    gates_ = [[("gpre", "x1", dp, j) for j in js] for dp in range(3) for js in ((0,), (1, 2))]
    beside = [x + y for x, y in zip(m, r)] + m[len(r):] + [[st] for st in keys_stages("x1")] + branches("x1") + gates_
    for t in range(TT):
        part, beside = during("c0", t, beside, 1)
        o += part
    o += flat(beside)
    k = keys_stages("c1")
    o += k[0:1] + [("gpre", "x1", 3, j) for j in range(3)] + k[1:] + flat(heads("x1") + mixing("x1") + scoring("x1"))
    part, beside = during("x1", 0, ranking("x1", 0) + ranking("x1", 1), 1)
    assert not beside
    o += part + during("x1", 1, [])[0]
    return o + [("final",)]


ORDER = order()
STAGES = [st for e in ORDER for st in (e[5] + e[6] if e[0] == "gather" else [e])]

FF = 2816
FT = FF // P
TURN = 4
TURNS = FT // TURN
TAPS = 31
TAPS_DVE = 4
PAD = TAPS - 1
H2, DH = 8, 128
LN_EPS = 1e-5
BLOCKS = ["f0", "cv", "f1", "f2", "at", "f3"]


def block_stages(tag):
    inner = {"f": [("gu", tag), ("dn", tag)], "c": [("cin",), ("taps",), ("ln",), ("cout",)], "a": [("qkv",), ("moba",), ("ao",)]}[tag[0]]
    return [("pre", tag), ("hT2", tag)] + inner + [("post", tag)]


ORDER2 = [st for tag in BLOCKS for st in block_stages(tag)] + [("store",)]
SS2_AT, X2_AT, H2_AT = {}, {"start": 2}, {}
_s, _x, _h = 0, 2, 0
for _st in ORDER2:
    if _st[0] == "pre":
        _s += 2
        SS2_AT["pre", _st[1]] = _s
        _h += 4 if _st[1] == "at" else 2
        H2_AT[_st[1]] = _h
    elif _st[0] == "post":
        _s += 4
        SS2_AT["post", _st[1]] = _s
        _x += 2
        X2_AT[_st[1]] = _x


def x2_before(tag):
    n = BLOCKS.index(tag)
    return X2_AT[BLOCKS[n - 1]] if n else X2_AT["start"]


def plan2():
    plan = []
    for name, *args in ORDER2:
        if name in ("gu", "dn"):
            n = int(args[0][1])
            plan += [("wgu" if name == "gu" else "wdn", (n, c)) for c in range(FT if name == "gu" else FT // 2)]
        elif name == "cin":
            plan += [("cwin", (c,)) for c in range(8)]
        elif name == "cout":
            plan += [("cwout", (c,)) for c in range(4)]
        elif name == "qkv":
            plan += [("w2k", (c,)) for c in range(4)] + [("w2v", (c,)) for c in range(4)] + [("w2q", (c,)) for c in range(4)]
        elif name == "ao":
            plan += [("w2o", (c,)) for c in range(4)]
    return plan


SLOTS2 = 4
AHEAD = 2

MARKS = {
    "h": (2, ["c0", "x0", "x1", "c1"]),
    "ckn": (2, ["c0", "x0", "x1", "c1"]),
    "krr": (2, ["c0", "x0", "x1", "c1"]),
    "cqn": (2, ["x0", "c0", "x1"]),
    "qr": (2, ["x0", "x1"]),
    "nmax": (16, ["x0", "c0", "x1"]),
    "pn": (16, ["x0", "c0", "x1"]),
    "mixT": (4, ["x0", "c0", "x1"]),
    "resid": (4, ["x0", "c0", "x1"]),
    "topd": (4, ["x0", "c0", "x1"]),
    "route": (4, ["x0", "c0", "x1"]),
    "fin": (2, ["x0", "c0", "x1"]),
    "ss": (4, ["c0", "x0", "x1", "c1"]),
    "kvss": (2, ["c0", "x0", "x1", "c1"]),
    "qss": (2, ["x0", "c0", "x1"]),
    "tope": (4, ["x0", "c0", "x1"]),
}


def mark_base(name, run):
    per, runs = MARKS[name]
    return per * runs.index(run)


def chunk_plan():
    plan = []
    for st in STAGES:
        name = st[0]
        if name == "mod":
            plan += [("wmod", (st[1], 2 * st[2] + n), SLOT_W) for n in range(2)]
            continue
        if name in ("start", "final"):
            continue
        l = RUNS[st[1]][1]
        if name == "zA":
            plan += [("wA", (l, n), 4 * WA) for n in range(2)]
        elif name == "kv":
            plan += [("wukv", (l,), D)] if st[2] == 2 else []
        elif name == "zF":
            plan += [("wZ", (l, n), SLOT_W) for n in range(2)]
        elif name == "four":
            plan += [("wgrp", (l,), 256)] if st[2] else [("dft", (), 2 * 768), ("poolm", (), SLOT_W)]
        elif name == "q":
            plan += [("wuq", (l,), 2 * H * QK)] if st[2] == 2 else []
        elif name == "gate":
            dp = st[2]
            js = () if st[1] == "x1" else (2,) if st[3] else (0, 1)
            plan += [("wG", (l, dp, j), SLOT_W) for j in js] + ([("wO", (l, dp), SLOT_W)] if st[3] else [])
        elif name == "gpre":
            plan += [("wG", (l, *st[2:]), SLOT_W)]
        elif name == "out":
            plan += [("wout", (l, 2 * st[2] + n), SLOT_W) for n in range(2)]
        elif name == "pq":
            plan += [("wpq", (l, 2 * st[2] + n), SLOT_W) for n in range(2)] if st[2] < 4 else []
    return plan


def build(nc, A, out):
    f32, i32, u32, f32r = mybir.dt.float32, mybir.dt.int32, mybir.dt.uint32, mybir.dt.float32r
    ALU, ACT, AX = mybir.AluOpType, mybir.ActivationFunctionType, mybir.AxisListType
    ctx = ExitStack()

    offset = {}

    def sb(name, shape, dt=f32):
        t = ctx.enter_context(nc.sbuf_tensor(name, shape, dt))
        offset[name] = nc.sbuf_base - 4 * int(np.prod(shape[1:]))
        return t

    def part_of(name, inside, at_, *dims):
        t = nc.alloc_sbuf_tensor_at(name, [P, int(np.prod(dims))], f32r, offset=offset[inside] + 4 * at_)[:, :]
        return t if len(dims) == 1 else t.rearrange("p (k n) -> p k n", k=dims[0])

    def sem(name):
        return ctx.enter_context(nc.semaphore(name))

    with ctx:
        x = [sb("x_in", [P, TT, D]), sb("x_ctx", [P, TT, D])]
        h = [sb("h_in", [P, TT, D]), sb("h_ctx", [P, TT, D])]
        hT = sb("hT", [P, KT, TOK])
        mrows = [sb(f"mrows{l}", [P, 3, 512]) for l in range(2)]
        gain = sb("gain", [P, D])
        keysT = sb("keysT", [P, HP * KEYS])
        amul, junk = keysT[:, 0:D], keysT[:, D:2 * D]
        mb = sb("mb", [P, D])
        wring = sb("wring", [P, SLOTS, SLOT_W])
        rows = sb("rows", [P, GROUP, D])
        zA = [sb("zA_in", [P, TT, WA]), sb("zA_ctx", [P, TT, WA])]
        kvmem = sb("kvmem", [P, H * 2 * TOK + 2 * TT * H * VH])
        kT = kvmem[:, 0:H * 2 * TOK].rearrange("p (h n) -> p h n", h=H)
        vv = kvmem[:, H * 2 * TOK:].rearrange("p (k n) -> p k n", n=H * VH)
        YT = sb("YT", [P, 512])
        ypT = sb("ypT", [P, 512])
        ident = sb("ident", [P, P])
        sel = sb("sel", [P, 2, P])
        rope = sb("rope", [P, TT, 32])
        iota = sb("iota", [P, TOP])
        cvec = sb("cvec", [P, KT, 2])
        cth = sb("cth", [P, KT, 2])
        vecs = sb("vecs", [P, 58])
        hbg = sb("hbg", [P, 2, 24])
        ss = sb("ss", [P, 8])
        nwt = sb("nwt", [P, 8])
        nwi = sb("nwi", [P, 8], i32)
        a8 = sb("a8", [P, GROUP])
        g1 = sb("g1", [P, GROUP])
        g2 = sb("g2", [P, GROUP])
        th8 = sb("th8", [P, GROUP])
        act8 = sb("act8", [P, GROUP])
        diag = sb("diag", [P, DIAGS, P])
        accv = sb("accv", [P, 512])
        nmax, rsum, rinv = (sb(n, [P, 4]) for n in ("nmax", "rsum", "rinv"))
        idx = [sb(f"idx{t}", [P, P], u32) for t in range(TT)]
        gates = [sb(f"gates{t}", [P, P]) for t in range(TT)]
        idown = [sb(f"idown{n}", [P, GROUP], u32) for n in range(2)]
        iup = [sb(f"iup{n}", [P, GROUP], u32) for n in range(2)]
        U = sb("shared", [P, 10240])
        at = [0]

        def part(n):
            at[0] += n
            assert at[0] <= 10240, at
            return U[:, at[0] - n:at[0]]

        q = part(2 * 768).rearrange("p (t n) -> p t n", t=TT)
        kfull = part(2 * 768).rearrange("p (t n) -> p t n", t=TT)
        qT = part(H * TOK).rearrange("p (h n) -> p h n", h=H)
        at[0] = 2 * 1536
        sg = part(3 * 512).rearrange("p (j n) -> p j n", j=3)
        mtmp = part(512)
        at[0] = 0
        mixT = part(KT * TOK).rearrange("p (k n) -> p k n", k=KT)
        at[0] = 3072 + 2048
        pr = part(4 * 512).rearrange("p (a t n) -> p a t n", a=2, t=TT)
        pT = part(4 * TOK).rearrange("p (k n) -> p k n", k=4)
        attT = part(4 * TOK).rearrange("p (k n) -> p k n", k=4)
        ckn = part(2 * P).rearrange("p (t n) -> p t n", t=TT)
        ckT = part(TOK)
        rtmp = part(4 * P).rearrange("p (a n) -> p a n", a=4)
        at[0] = 3072 + 2048
        zfp = part(2 * 512).rearrange("p (t n) -> p t n", t=TT)
        T1 = part(2 * 512).rearrange("p (t n) -> p t n", t=TT)
        poolT = part(512)
        cqn = part(2 * QLORA).rearrange("p (t n) -> p t n", t=TT)
        cqT = part(2 * TOK).rearrange("p (k n) -> p k n", k=2)
        at[0] = 0
        s_sb = part(TT * 2048).rearrange("p (t n) -> p t n", t=TT)
        cand = part(512).rearrange("p (a n) -> p a n", a=2)
        eq = part(1024)
        qpT = part(2 * 512).rearrange("p (a n) -> p a n", a=2)
        sv, sif = (part(HP * TOP).rearrange("p (i k) -> p i k", k=TOP) for _ in range(2))
        si = part(HP * TOP).bitcast(u32).rearrange("p (i k) -> p i k", k=TOP)
        ts, te = (part(P).rearrange("p (i k) -> p i k", k=TOP) for _ in range(2))
        fa, fb, ia, ib = (part(P) for _ in range(4))
        pos = part(P).bitcast(u32).rearrange("p (i k) -> p i k", k=TOP)
        pa = part(P).bitcast(u32)
        tsum = part(H)

        def gate_at(run, dp, j):
            if run != "x1":
                return sg[:, j, :]
            if dp == 3:
                return (mb[:, 0:512], mb[:, 512:D], zA[0].rearrange("p t n -> p (t n)")[:, 0:512])[j]
            if j == 0:
                return U[:, dp * 512:(dp + 1) * 512]
            n = 2 * dp + j - 1
            return h[0][:, n // 2, (n % 2) * 512:(n % 2 + 1) * 512] if n < 4 else junk[:, (n - 4) * 512:(n - 3) * 512]

        W2 = [wring[:, n, :] for n in range(SLOTS)] + [rows[:, 0:2, :].rearrange("p a n -> p (a n)")]
        gain2 = [gain, mb]
        at[0] = 0
        at[0] += FT * TOK
        fth = part(4 * TOK).rearrange("p (a n) -> p a n", a=4)
        ft2 = part(4 * TOK).rearrange("p (a n) -> p a n", a=4)
        at[0] = 0
        upad = part(8 * (TOK + PAD)).rearrange("p (c n) -> p c n", c=8)
        uc = part(8 * TOK).rearrange("p (c n) -> p c n", c=8)
        rln, rl2 = part(TOK), part(TOK)
        ctmp = part(2 * TOK).rearrange("p (a n) -> p a n", a=2)
        usq = part(8 * TOK).rearrange("p (c n) -> p c n", c=8)
        uth = part(8 * TOK).rearrange("p (c n) -> p c n", c=8)
        m0 = mrows[0].rearrange("p a n -> p (a n)")
        bout_b, vec2 = m0[:, 0:D], m0[:, D:D + 288]
        rli = rows[:, 2, 0:TOK].bitcast(i32)
        rli2 = rows[:, 2, TOK:2 * TOK].bitcast(i32)
        ones = rows[:, 3, 0:P]
        kT2 = kT[:, :, 0:TOK]
        qT2 = kT[:, :, TOK:2 * TOK]
        v2 = kvmem[:, H * 2 * TOK:].rearrange("p (t n) -> p t n", t=TT)
        at[0] = 0
        at[0] += 2 * KT * TOK
        p2 = part(4 * TOK).rearrange("p (a t n) -> p a t n", a=2, t=TT)
        pT2 = part(2 * TOK).rearrange("p (k n) -> p k n", k=2)

        W2_HI = [part_of("w_hi0", "rows", 4 * D, SLOT_W), part_of("w_hi1", "rows", 6 * D, SLOT_W), part_of("w_hi2", "x_ctx", 0, SLOT_W),
                 part_of("w_hi3", "keysT", 0, SLOT_W)]
        W2_LO = [part_of(f"w_lo{n}", "wring", n * SLOT_W, SLOT_W) for n in range(SLOTS)] + [part_of("w_lo3", "rows", 0, SLOT_W)]
        hT_2 = part_of("hT_hi", "hT", 0, KT, TOK), part_of("hT_lo", "shared", 8192, KT, TOK)
        hid_2 = part_of("hid_hi", "shared", 0, FT, TOK), part_of("hid_lo", "kvmem", 0, FT, TOK)
        conv_2 = part_of("conv_hi", "shared", 8 * (TOK + PAD) + 8 * TOK + 4 * TOK, 8, TOK), part_of("conv_lo", "shared", 8 * (TOK + PAD), 8, TOK)
        hkT_2 = part_of("hkT_hi", "shared", KT * TOK, KT, TOK), part_of("hkT_lo", "shared", 2 * KT * TOK + 6 * TOK, KT, TOK)
        attT_2 = part_of("attT_hi", "shared", 0, KT, TOK), part_of("attT_lo", "shared", 2 * KT * TOK + 6 * TOK, KT, TOK)

        dist = rows[:, 3, 512:1024].rearrange("p (t n) -> p t n", t=TT)

        ps = ctx.enter_context(nc.psum_tensor("ps", [P, 8, 512], f32))
        ROT = [0, 1, 2, 3, 5, 6, 7]
        ROT2, WIDE = [0, 1, 2, 3], [4, 5, 6, 7]
        UPB = 4
        UPV = 512

        mm_done = sem("mm_done")
        bank_free = [sem(f"bank_free{b}") for b in range(8)]
        mark = {n: sem(n) for n in MARKS}
        chunk_in = [sem(f"chunk_in{n}") for n in range(SLOTS)]
        row_in = [sem(f"row_in{n}") for n in range(GROUP)]
        ld_const, ld_x, ld_c, ld_gain, ld_keys, ld_mrow = (sem(n) for n in ("ld_const", "ld_x", "ld_c", "ld_gain", "ld_keys", "ld_mrow"))
        gain_used = sem("gain_used")
        dve_step, act_step = sem("dve_step"), sem("act_step")
        silu_t, silu_c = sem("silu_t"), sem("silu_c")
        down_done, upv_done, upp_done = sem("down_done"), sem("upv_done"), sem("upp_done")
        idx_copied, gelu_step, gelu_in, gelu_th, act_ready, diag_ready = (sem(n) for n in (
            "idx_copied", "gelu_step", "gelu_in", "gelu_th", "act_ready", "diag_ready"))
        slot_ok = sem("slot_ok")
        ss2, x2, h2m, ld_vec2, ones_set = (sem(n) for n in ("ss2", "x2", "h2m", "ld_vec2", "ones_set"))
        gain2_in = [sem(f"gain2_in{n}") for n in range(2)]
        gain2_used = sem("gain2_used")
        chunk2_in = [sem(f"chunk2_in{n}") for n in range(SLOTS2)]
        hi_ready, lo_ready = sem("hi_ready"), sem("lo_ready")
        hT2_hi, att2_hi = sem("hT2_hi"), sem("att2_hi")
        gate_th, gu_step = sem("gate_th"), sem("gu_step")
        hid_ready, tap_ready, conv_h, conv_th, conv_u, conv_y, ln_d, ln_v, ln_z, ln_t, ln_s = (sem(n) for n in (
            "hid_ready", "tap_ready", "conv_h", "conv_th", "conv_u", "conv_y", "ln_d", "ln_v", "ln_z", "ln_t", "ln_s"))
        s2_ready, p2_ready, bout_y = sem("s2_ready"), sem("p2_ready"), sem("bout_y")
        out_done = sem("out_done")

        mm_at, job_bank, job_use = {}, {}, {}
        uses = [0] * 8
        plan = chunk_plan()
        gu_base, gu_use, chunk2_done, plan_2 = {}, {}, [], plan2()
        chunk_done = {}

        def at_mark(eng, name, run, n):
            eng.wait_ge(mark[name], mark_base(name, run) + n)

        def at_mm(eng, key):
            eng.wait_ge(mm_done, mm_at[key])
            return ps[:, job_bank[key], :]

        def at_evac(eng, key):
            eng.wait_ge(bank_free[job_bank[key]], job_use[key])

        def release(ins, key):
            ins.then_inc(bank_free[job_bank[key]], 1)

        def norm_mark(run, k, n):
            firsts = {"c0": 0, "x0": 1, "x1": 4, "c1": 5}
            return (firsts[run] if k == 0 else {"x0": 2, "c0": 3, "x1": 6}[run]) * 2 + n

        def is_group(n, which):
            return isinstance(n, int) and n == which

        def groups(eng, n0, n1, body):
            lo, hi = max(n0, 2), min(n1, GROUPS - 1)
            for n in range(n0, min(n1, 2)):
                body(n)
            if hi - lo > 1:
                with eng.Fori(lo, hi) as n:
                    body(n)
            elif hi - lo == 1:
                body(lo)
            if n1 == GROUPS and n0 < GROUPS:
                body(GROUPS - 1)

        block = ctx.enter_context(nc.Block())

        @block.tensor
        def _(pe):
            count = [0]
            rot = [0]
            chunk_no = [0]

            def job(key):
                b = ROT[rot[0] % len(ROT)]
                rot[0] += 1
                if uses[b]:
                    pe.wait_ge(bank_free[b], uses[b])
                uses[b] += 1
                job_bank[key], job_use[key] = b, uses[b]
                return ps[:, b, :]

            def ended(ins, key):
                count[0] += 1
                ins.then_inc(mm_done, 1)
                mm_at[key] = count[0]

            def chunk():
                n = chunk_no[0]
                chunk_no[0] += 1
                pe.wait_ge(chunk_in[n % SLOTS], 16 * (n // SLOTS + 1))
                return wring[:, n % SLOTS, 0:plan[n][2]]

            def chunk_end(n=1):
                for _ in range(n):
                    chunk_done[len(chunk_done)] = count[0]

            def bcast(key, run, j, half):
                s, l = RUNS[run]
                cc = 2 * j + half
                at_evac(pe, ("mod", l, cc))
                qd, a = 32 * (cc % 4), cc // 4
                ended(pe.matmul(job(key), sel[qd:qd + 2, s, :], mrows[l][qd:qd + 2, a, :], start=True, stop=True,
                                tile_position=(qd, 0)), key)

            def start():
                pe.wait_ge(ld_const, 16 * 6)

            def mod(l, cc):
                if l + cc == 0:
                    pe.wait_ge(silu_c, 1)
                qd = 32 * (cc % 4)
                b = job(("mod", l, cc))
                for half in range(2):
                    w = chunk()
                    for k in range(4):
                        last = pe.matmul(b[qd:qd + 2, :], cvec[:, 4 * half + k, :], w[:, k * 512:(k + 1) * 512],
                                         start=(half + k == 0), stop=(half == 1 and k == 3), tile_position=(0, qd))
                ended(last, ("mod", l, cc))
                chunk_end(2)

            def norm(run, k):
                for half in range(2):
                    bcast(("bs", run, k, half), run, 1 + 3 * k, half)
                for half in range(2):
                    bcast(("bh", run, k, half), run, 3 * k, half)

            hT_now = [None]

            def hT_(run, k):
                s = RUNS[run][0]
                hT_now[0] = (run, k)
                for a in range(2):
                    for t in range(TT):
                        if k < 2 and t == 0:
                            pe.wait_ge(mark["h"], norm_mark(run, k, a + 1))
                        elif k < 2:
                            at_evac(pe, ("bh", run, k, a))
                        b = job(("hT", run, k, t, a))
                        for j in range(4):
                            last = pe.transpose(b[:, j * P:(j + 1) * P], h[s][:, t, (4 * a + j) * P:(4 * a + j + 1) * P], ident[:, :])
                        ended(last, ("hT", run, k, t, a))

            def hT_ready():
                for t in range(TT):
                    for a in range(2):
                        at_evac(pe, ("hT", *hT_now[0], t, a))

            def token_major(keys, lhs, width, halves=2):
                bs = [job(k) for k in keys]
                for c in range(2):
                    w = chunk()
                    for t in range(TT):
                        for k in range(4):
                            last = pe.matmul(bs[t][:, 0:width], lhs[:, 4 * c + k, t * P:(t + 1) * P], w[:, k * width:(k + 1) * width],
                                             start=(c + k == 0), stop=(c == 1 and k == 3))
                        if c == 1:
                            ended(last, keys[t])
                chunk_end(2)

            def zA_(run):
                hT_ready()
                token_major([("zA", run, t) for t in range(TT)], hT, WA)

            def kv(run, step):
                if step == 1:
                    b = job(("ckT", run))
                    for t in range(TT):
                        at_mark(pe, "ckn", run, t + 1)
                        last = pe.transpose(b[:, t * P:(t + 1) * P], ckn[:, t, :], ident[:, :])
                    ended(last, ("ckT", run))
                elif step == 2:
                    w = chunk()
                    at_evac(pe, ("ckT", run))
                    for t in range(TT):
                        for half in range(2):
                            key = ("kv", run, t, half)
                            ended(pe.matmul(job(key), ckT[:, t * P:(t + 1) * P], w[:, half * 512:(half + 1) * 512], start=True, stop=True), key)
                    chunk_end()
                elif step == 3:
                    for t in range(TT):
                        at_mark(pe, "krr", run, t + 1)
                        for hq in range(2):
                            at_evac(pe, ("kv", run, t, hq))
                            b = job(("kT", run, t, hq))
                            for j in range(4):
                                hh = 4 * hq + j
                                last = pe.transpose(b[0:QK, j * P:(j + 1) * P], kfull[:, t, hh * QK:(hh + 1) * QK], ident[:, :])
                            ended(last, ("kT", run, t, hq))

            def zF(run):
                hT_ready()
                token_major([("zF", run, t) for t in range(TT)], hT, WZ)

            dft_now = [None]

            def four(run, step):
                if step == 0:
                    for t in range(TT):
                        at_evac(pe, ("zF", run, t))
                    w = dft_now[0] = chunk().rearrange("p (k n) -> p k n", k=2)
                    for ft in range(2):
                        b = job(("T1", run, ft))
                        for lt in range(TT):
                            last = pe.matmul(b, zfp[:, lt, ft * P:(ft + 1) * P], w[:, lt, 0:512], start=(lt == 0), stop=(lt == 1))
                        ended(last, ("T1", run, ft))
                    wp = chunk().rearrange("p (k g n) -> p k g n", k=2, g=4)
                    b = job(("P", run))
                    for g in range(4):
                        for lt in range(TT):
                            po = 64 * (g % 2)
                            last = pe.matmul(b[po:po + 64, (g // 2) * TOK:(g // 2 + 1) * TOK], zfp[:, lt, TOK + g * 64:TOK + (g + 1) * 64],
                                             wp[:, lt, g, :], start=(lt == 0), stop=(lt == 1), tile_position=(0, po))
                    ended(last, ("P", run))
                    return
                w = dft_now[0]
                b = job(("Y", run))
                for ft in range(2):
                    at_evac(pe, ("T1", run, ft))
                for fo in range(2):
                    for ft in range(2):
                        for part_ in range(2):
                            last = pe.matmul(b[:, fo * TOK:(fo + 1) * TOK], w[:, ft, part_ * 512 + fo * P:part_ * 512 + (fo + 1) * P],
                                             T1[:, ft, part_ * TOK:(part_ + 1) * TOK], start=(ft + part_ == 0), stop=(ft + part_ == 2))
                ended(last, ("Y", run))
                chunk_end(2)
                wg = chunk()
                at_evac(pe, ("P", run))
                b = job(("G", run))
                for pair in range(2):
                    last = pe.matmul(b[:, pair * TOK:(pair + 1) * TOK], wg[:, pair * P:(pair + 1) * P], poolT[:, pair * TOK:(pair + 1) * TOK],
                                     start=True, stop=True)
                ended(last, ("G", run))
                chunk_end()

            def q_(run, step):
                if step == 1:
                    b = job(("cqT", run))
                    for t in range(TT):
                        at_mark(pe, "cqn", run, t + 1)
                        for k in range(2):
                            last = pe.transpose(b[:, k * TOK + t * P:k * TOK + (t + 1) * P], cqn[:, t, k * P:(k + 1) * P], ident[:, :])
                    ended(last, ("cqT", run))
                elif step == 2:
                    w = chunk()
                    at_evac(pe, ("cqT", run))
                    for t in range(TT):
                        for half in range(2):
                            key = ("q", run, t, half)
                            b = job(key)
                            for k in range(2):
                                last = pe.matmul(b[:, 0:384], cqT[:, k, t * P:(t + 1) * P], w[:, k * 768 + half * 384:k * 768 + (half + 1) * 384],
                                                 start=(k == 0), stop=(k == 1))
                            ended(last, key)
                    chunk_end()
                elif step == 3:
                    for t in range(TT):
                        for half in range(2):
                            at_evac(pe, ("q", run, t, half))
                        if RUNS[run][0] == 0:
                            at_mark(pe, "qr", run, t + 1)
                        for hq in range(2):
                            b = job(("qT", run, t, hq))
                            for j in range(4):
                                hh = 4 * hq + j
                                last = pe.transpose(b[0:QK, j * P:(j + 1) * P], q[:, t, hh * QK:(hh + 1) * QK], ident[:, :])
                            ended(last, ("qT", run, t, hq))

            def att(run, i):
                nk = 4 if RUNS[run][0] == 0 else 2
                if i == 0:
                    for r2 in {"x0": ("x0", "c0"), "c0": ("c0",), "x1": ("x1", "c1")}[run]:
                        for t in range(TT):
                            for hq in range(2):
                                at_evac(pe, ("kT", r2, t, hq))
                    for t in range(TT):
                        for hq in range(2):
                            at_evac(pe, ("qT", run, t, hq))
                if i < H:
                    for t in range(TT):
                        key = ("s", run, i, t)
                        ended(pe.matmul(job(key)[:, 0:nk * P], qT[0:QK, i, t * P:(t + 1) * P], kT[0:QK, i, 0:nk * P], start=True, stop=True), key)
                if i >= 2:
                    hh = i - 2
                    for t in range(TT):
                        at_evac(pe, ("pT", run, hh, t))
                    if hh % 2 == 0:
                        job(("pv", run, hh // 2))
                    pv = ps[:, job_bank["pv", run, hh // 2], :]
                    po = 64 * (hh % 2)
                    for k in range(nk):
                        last = pe.matmul(pv[po:po + VH, 0:TOK], vv[:, k, hh * VH:(hh + 1) * VH], pT[:, k, :],
                                         start=(k == 0), stop=(k == nk - 1), tile_position=(0, po))
                    ended(last, ("pvh", run, hh))
                    if hh % 2:
                        mm_at["pv", run, hh // 2] = count[0]
                if 1 <= i <= H:
                    hh = i - 1
                    for t in range(TT):
                        at_mark(pe, "pn", run, 2 * hh + t + 1)
                        b = job(("pT", run, hh, t))
                        for k in range(nk):
                            last = pe.transpose(b[:, k * P:(k + 1) * P], pr[:, hh % 2, t, k * P:(k + 1) * P], ident[:, :])
                        ended(last, ("pT", run, hh, t))

            def gpre(run, dp, j):
                hT_ready()
                w = chunk()
                b = job(("g", run, dp, j))
                for dt in range(2):
                    for k in range(KT):
                        last = pe.matmul(b[:, dt * TOK:(dt + 1) * TOK], w[:, k * 256 + dt * P:k * 256 + (dt + 1) * P], hT[:, k, :],
                                         start=(k == 0), stop=(k == KT - 1))
                ended(last, ("g", run, dp, j))
                chunk_end()

            def gate(run, dp, part_):
                if dp + part_ == 0:
                    hT_ready()
                for j in (() if run == "x1" else (2,) if part_ else (0, 1)):
                    gpre(run, dp, j)
                if not part_:
                    return
                if dp == 0:
                    for n in range(4):
                        at_evac(pe, ("pv", run, n))
                    at_evac(pe, ("Y", run))
                    at_evac(pe, ("G", run))
                w = chunk()
                for j, ks in enumerate(([0, 1, 2, 3], [4, 5], [6, 7])):
                    b = job(("y", run, dp, j))
                    for dt in range(2):
                        for k in ks:
                            rhs = attT[:, k, :] if j == 0 else (YT, ypT)[j - 1][:, (k % 2) * TOK:(k % 2 + 1) * TOK]
                            last = pe.matmul(b[:, dt * TOK:(dt + 1) * TOK], w[:, k * 256 + dt * P:k * 256 + (dt + 1) * P], rhs,
                                             start=(k == ks[0]), stop=(k == ks[-1]))
                    ended(last, ("y", run, dp, j))
                chunk_end()

            def out_(run, half):
                at_mark(pe, "mixT", run, 4)
                bcast(("bm", run, half), run, 2, half)
                token_major([("o", run, half, t) for t in range(TT)], mixT, 512)

            def pq(run, i):
                if i == 0:
                    hT_ready()
                if i == 1:
                    pe.wait_ge(ld_keys, 16 * (["x0", "c0", "x1"].index(run) + 1))

                def queries(c):
                    w = chunk()
                    b = job(("qp", run, c))
                    for hp in range(2):
                        for k in range(KT):
                            last = pe.matmul(b[:, hp * TOK:(hp + 1) * TOK], w[:, k * 256 + hp * P:k * 256 + (hp + 1) * P],
                                             hT[:, k, :], start=(k == 0), stop=(k == KT - 1))
                    ended(last, ("qp", run, c))
                    chunk_end()

                def scores(c):
                    at_evac(pe, ("qp", run, c))
                    b = job(("sc", run, c))
                    for t in range(TT):
                        for hp in range(2):
                            last = pe.matmul(b[:, t * 256 + hp * P:t * 256 + (hp + 1) * P], qpT[:, c % 2, hp * TOK + t * P:hp * TOK + (t + 1) * P],
                                             keysT[:, (2 * c + hp) * P:(2 * c + hp + 1) * P], start=True, stop=True)
                    ended(last, ("sc", run, c))

                for c in (2 * i, 2 * i + 1):
                    if i < 4:
                        queries(c)
                    if i:
                        scores(c - 2)

            def gather(run, t, n0, n1, beside_a, beside_b):
                G = GATHER_NO[run, t]

                def up(g, first=False, last=False):
                    pos_ = 31 if last else 2 * g + 2
                    for j in range(GROUP):
                        pe.wait_ge(row_in[j], 16 * (32 * G + 1) + 16 * pos_)
                        pe.wait_ge(diag_ready, 8 * g + (P * G + j + 1))
                        pe.matmul(ps[:, UPB, :], diag[:, j % DIAGS, :], rows[:, j, UPV:D], start=(first and j == 0), stop=(last and j == GROUP - 1),
                                  skip_group_check=True).then_inc(upp_done, 1)

                run_stages(beside_a)
                if n0 <= 1 < n1 and G:
                    at_mark(pe, "fin", GATHERS[G - 1][0], GATHERS[G - 1][1] + 1)
                groups(pe, n0, n1, lambda n: is_group(n, 0) or up(n - 1, first=is_group(n, 1)))
                run_stages(beside_b)
                if n1 == GROUPS:
                    up(GROUPS - 1, last=True)

            def fin(run, t):
                for half in range(2):
                    bcast(("bf", run, t, half), run, 5, half)

            rots = {"a": 0, "w": 0}
            chunk2_no = [0]

            def job2(key, wide=False):
                banks, r = (WIDE, "w") if wide else (ROT2, "a")
                b = banks[rots[r] % 4]
                rots[r] += 1
                if uses[b]:
                    pe.wait_ge(bank_free[b], uses[b])
                uses[b] += 1
                job_bank[key], job_use[key] = b, uses[b]
                return ps[:, b, :]

            def chunk2():
                n = chunk2_no[0]
                chunk2_no[0] += 1
                pe.wait_ge(lo_ready, n + 1)
                return W2_HI[n % SLOTS2], W2_LO[n % SLOTS2]

            def product(out_, lhs, l_at, rhs, r_at, start, stop):
                (lh, ll), (rh, rl) = lhs, rhs
                pe.matmul(out_, lh[l_at], rh[r_at], start=start, stop=False)
                pe.matmul(out_, ll[l_at], rh[r_at], start=False, stop=False)
                return pe.matmul(out_, lh[l_at], rl[r_at], start=False, stop=stop)

            def chunk2_end(n=1):
                chunk2_done.extend([count[0]] * n)

            def hT2(tag):
                for gi, src in enumerate([h[1], h[0]] if tag == "at" else [h[0]]):
                    for t in range(TT):
                        pe.wait_ge(h2m, H2_AT[tag] - (4 if tag == "at" else 2) + 2 * gi + t + 1)
                        for a in range(2):
                            key = ("hT2", tag, gi, t, a)
                            b = job2(key)
                            for j in range(4):
                                last = pe.transpose(b[:, j * P:(j + 1) * P], src[:, t, (4 * a + j) * P:(4 * a + j + 1) * P], ident[:, :])
                            ended(last, key)

            def hT2_ready(tag, gi=0):
                for t in range(TT):
                    for a in range(2):
                        at_evac(pe, ("hT2", tag, gi, t, a))

            def two_tiles(b, w, act_):
                for j in range(2):
                    for k in range(KT):
                        last = product(b[:, j * TOK:(j + 1) * TOK], w, np.s_[:, k * 256 + j * P:k * 256 + (j + 1) * P], act_, np.s_[:, k, :],
                                       start=(k == 0), stop=(k == KT - 1))
                return last

            def gu(tag):
                hT2_ready(tag)
                n0, m0, use0, r0 = chunk2_no[0], count[0], list(uses), rots["a"]
                gu_base[tag], gu_use[tag] = (m0, r0, n0), use0
                with pe.Fori(0, TURNS) as i:
                    for j in range(TURN):
                        n = n0 + j
                        pe.wait_ge(lo_ready, 4 * i + (n + 1))
                        b = ROT2[(r0 + j) % 4]
                        pe.wait_ge(bank_free[b], i + use0[b])
                        two_tiles(ps[:, b, :], (W2_HI[n % SLOTS2], W2_LO[n % SLOTS2]), hT_2).then_inc(mm_done, 1)
                for b in ROT2:
                    uses[b] += TURNS
                count[0] += TURN * TURNS
                rots["a"] += TURN * TURNS
                chunk2_no[0] += TURN * TURNS
                chunk2_done.extend(m0 + n + 1 for n in range(TURN * TURNS))
                for j in range(FT - TURN * TURNS):
                    key = ("gu", tag, j)
                    w = chunk2()
                    ended(two_tiles(job2(key), w, hT_2), key)
                    chunk2_end()

            def dn(tag):
                keys = [("d", tag, t, half) for t in range(TT) for half in range(2)]
                bs = [job2(key, True) for key in keys]
                for c in range(FT // 2):
                    w = chunk2()
                    if c == 0:
                        pe.wait_ge(hid_ready, FT * int(tag[1]) + TURN * TURNS)
                    if c == TURN * TURNS // 2:
                        pe.wait_ge(hid_ready, FT * (int(tag[1]) + 1))
                    for n, (t, half) in enumerate([(t, half) for t in range(TT) for half in range(2)]):
                        for k in range(2):
                            last = product(bs[n], hid_2, np.s_[:, 2 * c + k, t * P:(t + 1) * P], w,
                                           np.s_[:, k * D + half * 512:k * D + (half + 1) * 512], start=(c + k == 0), stop=(c == FT // 2 - 1 and k == 1))
                        if c == FT // 2 - 1:
                            ended(last, keys[n])
                    if c < FT // 2 - 1:
                        ended(last, ("dn", tag, c))
                    chunk2_end()

            def token_major2(tag, lhs, name="d", wide=True):
                for half in range(2):
                    keys = [(name, tag, t, half) for t in range(TT)]
                    bs = [job2(key, wide) for key in keys]
                    for c in range(2):
                        w = chunk2()
                        for t in range(TT):
                            for k in range(4):
                                last = product(bs[t], lhs, np.s_[:, 4 * c + k, t * P:(t + 1) * P], w, np.s_[:, k * 512:(k + 1) * 512],
                                               start=(c + k == 0), stop=(c == 1 and k == 3))
                            if c == 1:
                                ended(last, keys[t])
                        if c == 0:
                            ended(last, (name, tag, "part", half))
                        chunk2_end()

            def cin():
                hT2_ready("cv")
                for c in range(8):
                    w = chunk2()
                    ended(two_tiles(job2(("cin", c)), w, hT_2), ("cin", c))
                    chunk2_end()

            def taps():
                for n, c in enumerate(range(TAPS_DVE, 8)):
                    pe.wait_ge(conv_u, c + 1)
                    b = job2(("tap", c))
                    for j in range(TAPS):
                        k = n * TAPS + j
                        pe.wait_ge(tap_ready, k + 1)
                        last = pe.matmul(b[:, 0:TOK], diag[:, k % DIAGS, :], upad[:, c, j:j + TOK], start=(j == 0), stop=(j == TAPS - 1))
                        if j < TAPS - 1:
                            ended(last, ("tap", c, j))
                    ended(last, ("tap", c, j))
                    mm_at["tap", c] = count[0]

            def ln():
                pe.wait_ge(ones_set, 1)
                b = job2(("mean",))
                for c in range(8):
                    if c < TAPS_DVE:
                        pe.wait_ge(conv_y, c + 1)
                    else:
                        at_evac(pe, ("tap", c))
                    last = pe.matmul(b[:, 0:TOK], ones, uc[:, c, :], start=(c == 0), stop=(c == 7))
                ended(last, ("mean",))
                b = job2(("var",))
                pe.wait_ge(ln_v, 1)
                for c in range(8):
                    last = pe.matmul(b[:, 0:TOK], ones, usq[:, c, :], start=(c == 0), stop=(c == 7))
                ended(last, ("var",))

            def cout():
                pe.wait_ge(ln_s, 1)
                token_major2("cv", conv_2)

            def qkv():
                for name, gi in (("k2", 0), ("v2", 0), ("q2", 1)):
                    hT2_ready("at", gi)
                    src = (hkT_2, hT_2)[gi]
                    if name == "v2":
                        token_major2("at", src, "v2", False)
                        continue
                    for c in range(4):
                        w = chunk2()
                        ended(two_tiles(job2((name, c)), w, src), (name, c))
                        chunk2_end()

            def moba():
                for c in range(4):
                    at_evac(pe, ("k2", c))
                    at_evac(pe, ("q2", c))
                for t in range(TT):
                    for half in range(2):
                        at_evac(pe, ("v2", "at", t, half))

                def scores(hh):
                    b = job2(("s2", hh))
                    for t in range(TT):
                        last = pe.matmul(b[:, t * TOK:(t + 1) * TOK], qT2[:, hh, t * P:(t + 1) * P], kT2[:, hh, :], start=True, stop=True)
                    ended(last, ("s2", hh))

                scores(0)
                for hh in range(H2):
                    if hh + 1 < H2:
                        scores(hh + 1)
                    b = job2(("pT2", hh))
                    for t in range(TT):
                        pe.wait_ge(p2_ready, 2 * hh + t + 1)
                        for k in range(2):
                            last = pe.transpose(b[:, k * TOK + t * P:k * TOK + (t + 1) * P], p2[:, hh % 2, t, k * P:(k + 1) * P], ident[:, :])
                    ended(last, ("pT2", hh))
                    at_evac(pe, ("pT2", hh))
                    b = job2(("pv2", hh))
                    for k in range(2):
                        last = pe.matmul(b[:, 0:TOK], v2[:, k, hh * DH:(hh + 1) * DH], pT2[:, k, :], start=(k == 0), stop=(k == 1))
                    ended(last, ("pv2", hh))

            def ao():
                for hh in range(H2):
                    at_evac(pe, ("pv2", hh))
                token_major2("at", attT_2)

            program = {"hT2": hT2, "gu": gu, "dn": dn, "cin": cin, "taps": taps, "ln": ln, "cout": cout, "qkv": qkv, "moba": moba, "ao": ao,
                       "start": start, "mod": mod, "norm": norm, "hT": hT_, "zA": zA_, "kv": kv, "zF": zF, "four": four, "q": q_, "att": att,
                       "gate": gate, "gpre": gpre, "out": out_, "pq": pq, "gather": gather, "fin": fin}

            def run_stages(stages):
                for name, *args in stages:
                    if name in program:
                        program[name](*args)

            run_stages(ORDER + ORDER2)
            assert chunk_no[0] == len(plan) == len(chunk_done)
            assert chunk2_no[0] == len(plan_2) == len(chunk2_done)

        @block.scalar
        def _(act):
            def copy(dst, src, key, scale=None):
                release(act.activation(dst, src, ACT.Copy) if scale is None else act.activation(dst, src, ACT.Copy, scale=scale), key)

            def squares(src, n, scratch):
                return act.activation(scratch, src, ACT.Square, accum_out=ss[:, n:n + 1])

            def start():
                act.wait_ge(ld_const, 16 * 6)
                act.activation(cth[:, :, :], cvec[:, :, :], ACT.Tanh, scale=0.5).then_inc(silu_t, 1)

            def norm(run, k):
                s = RUNS[run][0]
                if k:
                    at_mark(act, "resid", run, 4)
                elif RUNS[run][1] == 0:
                    act.wait_ge((ld_x, ld_c)[s], 16)
                else:
                    at_mark(act, "fin", ("x0", "c0")[s], 2)
                for t in range(TT):
                    squares(x[s][:, t, :], t, h[s][:, t, :]).then_inc(mark["ss"], 1)

            def hT_(run, k):
                s = RUNS[run][0]
                for a in range(2):
                    for t in range(TT):
                        key = ("hT", run, k, t, a)
                        b = at_mm(act, key)
                        copy(hT[:, 4 * a:4 * a + 4, t * P:(t + 1) * P], b.rearrange("p (j n) -> p j n", j=4), key)

            def zA_(run):
                s = RUNS[run][0]
                for t in range(TT):
                    key = ("zA", run, t)
                    b = at_mm(act, key)
                    copy(zA[s][:, t, :], b[:, 0:WA], key)

            def kv(run, step):
                s, l = RUNS[run]
                if step == 0:
                    for t in range(TT):
                        at_evac(act, ("zA", run, t))
                        squares(zA[s][:, t, QLORA:QLORA + KVLORA], 2 + t, ckn[:, t, :]).then_inc(mark["kvss"], 1)
                elif step == 1:
                    key = ("ckT", run)
                    b = at_mm(act, key)
                    release(act.activation(ckT[:, :], b[:, 0:TOK], ACT.Copy, scale=vecs[:, 29 * l:29 * l + 1]), key)
                elif step == 2:
                    for t in range(TT):
                        for half in range(2):
                            key = ("kv", run, t, half)
                            b = at_mm(act, key).rearrange("p (h n) -> p h n", h=4)
                            kd = kfull[:, t, half * 4 * QK:(half + 1) * 4 * QK].rearrange("p (h n) -> p h n", h=4)
                            act.activation(kd[:, :, 0:NOPE], b[:, :, 0:NOPE], ACT.Copy)
                            ko = (0 if s else TT) + t
                            copy(vv[:, ko, half * 4 * VH:(half + 1) * 4 * VH].rearrange("p (h n) -> p h n", h=4), b[:, :, NOPE:NOPE + VH], key)
                else:
                    for t in range(TT):
                        for hq in range(2):
                            key = ("kT", run, t, hq)
                            b = at_mm(act, key)[0:QK, :].rearrange("p (h n) -> p h n", h=4)
                            ko = ((0 if s else TT) + t) * P
                            copy(kT[0:QK, 4 * hq:4 * hq + 4, ko:ko + P], b, key)

            def zF(run):
                for t in range(TT):
                    key = ("zF", run, t)
                    copy(zfp[:, t, :], at_mm(act, key), key)

            def four(run, step):
                if step == 0:
                    for ft in range(2):
                        key = ("T1", run, ft)
                        copy(T1[:, ft, :], at_mm(act, key), key)
                    copy(poolT, at_mm(act, ("P", run)), ("P", run))
                    return
                copy(YT[:, :], at_mm(act, ("Y", run)), ("Y", run))
                b = at_mm(act, ("G", run))
                l = RUNS[run][1]
                for pair in range(2):
                    last = act.activation(ypT[:, pair * TOK:(pair + 1) * TOK], b[:, pair * TOK:(pair + 1) * TOK], ACT.Copy,
                                          scale=vecs[:, 29 * l + 3 + pair:29 * l + 4 + pair])
                release(last, ("G", run))

            def q_(run, step):
                s, l = RUNS[run]
                if step == 0:
                    for t in range(TT):
                        squares(zA[s][:, t, 0:QLORA], 4 + t, cqn[:, t, :]).then_inc(mark["qss"], 1)
                elif step == 1:
                    b = at_mm(act, ("cqT", run))
                    for k in range(2):
                        last = act.activation(cqT[:, k, :], b[:, k * TOK:(k + 1) * TOK], ACT.Copy, scale=vecs[:, 29 * l + 1 + k:29 * l + 2 + k])
                    release(last, ("cqT", run))
                elif step == 2:
                    for t in range(TT):
                        for half in range(2):
                            key = ("q", run, t, half)
                            copy(q[:, t, half * 384:(half + 1) * 384], at_mm(act, key)[:, 0:384], key)
                else:
                    for t in range(TT):
                        for hq in range(2):
                            key = ("qT", run, t, hq)
                            b = at_mm(act, key)[0:QK, :].rearrange("p (h n) -> p h n", h=4)
                            copy(qT[0:QK, 4 * hq:4 * hq + 4, t * P:(t + 1) * P], b, key, scale=ATT_SCALE)

            def att(run, i):
                nk = 4 if RUNS[run][0] == 0 else 2
                if i < H:
                    for t in range(TT):
                        key = ("s", run, i, t)
                        at_mark(act, "nmax", run, 2 * i + t + 1)
                        if i >= 2:
                            act.wait_ge(mm_done, mm_at["pT", run, i - 2, t])
                        c = 2 * (i % 2) + t
                        release(act.activation(pr[:, i % 2, t, 0:nk * P], at_mm(act, key)[:, 0:nk * P], ACT.Exp,
                                               bias=nmax[:, c:c + 1], accum_out=rsum[:, c:c + 1]), key)
                if i >= 2 and i % 2:
                    key = ("pv", run, (i - 2) // 2)
                    copy(attT[:, (i - 2) // 2, :], at_mm(act, key)[:, 0:TOK], key)
                if 1 <= i <= H:
                    if i >= 2:
                        act.wait_ge(mm_done, mm_at["pvh", run, i - 2])
                    for t in range(TT):
                        key = ("pT", run, i - 1, t)
                        b = at_mm(act, key)[:, 0:nk * P].rearrange("p (k n) -> p k n", k=nk)
                        copy(pT[:, 0:nk, t * P:(t + 1) * P], b, key)

            def gpre(run, dp, j):
                l = RUNS[run][1]
                key = ("g", run, dp, j)
                b = at_mm(act, key)
                dst = gate_at(run, dp, j)
                for dt in range(2):
                    c = j * 8 + dp * 2 + dt
                    last = act.activation(dst[:, dt * TOK:(dt + 1) * TOK], b[:, dt * TOK:(dt + 1) * TOK], ACT.Tanh,
                                          bias=hbg[:, l, c:c + 1], scale=0.5)
                release(last, key)

            def gate(run, dp, part_):
                if dp and not part_:
                    at_mark(act, "mixT", run, dp)
                for j in (() if run == "x1" else (2,) if part_ else (0, 1)):
                    gpre(run, dp, j)

            def out_(run, half):
                key = ("bm", run, half)
                copy(mb[:, half * 512:(half + 1) * 512], at_mm(act, key), key, scale=0.5)

            def pq(run, i):
                for c in (2 * i, 2 * i + 1):
                    if i:
                        key = ("sc", run, c - 2)
                        b = at_mm(act, key).rearrange("p (t n) -> p t n", t=TT)
                        copy(s_sb[:, :, (c - 2) * 256:(c - 1) * 256], b, key)
                    if i < 4:
                        key = ("qp", run, c)
                        copy(qpT[:, c % 2, :], at_mm(act, key), key)

            def route(run, t, k):
                if k >= 8:
                    hs = slice(4 * (k - 8), 4 * (k - 7))
                    at_mark(act, "topd", run, 2 * t + k - 7)
                    act.activation(te[:, hs, :], te[:, hs, :], ACT.Exp).then_inc(mark["tope"], 1)

            def gather(run, t, n0, n1, beside_a, beside_b):
                G = GATHER_NO[run, t]

                def diags(g):
                    act.wait_ge(act_ready, g + (GROUPS * G + 1))
                    for j in range(GROUP):
                        if not (isinstance(g, int) and g == 0 and j < DIAGS and G == 0):
                            act.wait_ge(upp_done, 8 * g + (P * G - DIAGS + j + 1))
                        act.activation(diag[:, j % DIAGS, :], ident[:, :], ACT.Copy, scale=act8[:, j:j + 1]).then_inc(diag_ready, 1)

                def tanh(g):
                    act.wait_ge(gelu_in, g + (GROUPS * G + 1))
                    act.activation(th8[:, :], g2[:, :], ACT.Tanh, scale=GELU_C).then_inc(gelu_th, 1)

                if beside_a or beside_b:
                    if n0:
                        diags(n0 - 1)
                    run_stages(beside_a)
                    tanh(n0)
                    run_stages(beside_b)
                else:
                    groups(act, n0, n1, lambda n: (is_group(n, 0) or diags(n - 1), tanh(n)))
                if n1 == GROUPS:
                    diags(GROUPS - 1)

            def fin(run, t):
                for half in range(2):
                    key = ("bf", run, t, half)
                    copy(mb[:, half * 512:(half + 1) * 512], at_mm(act, key), key, scale=0.5)

            def final():
                at_mark(act, "fin", "x1", 2)
                for t in range(TT):
                    squares(x[0][:, t, :], t, h[0][:, t, :]).then_inc(mark["ss"], 1)

            def pre(tag):
                for t in range(TT):
                    act.wait_ge(x2, x2_before(tag) - TT + t + 1)
                    squares(x[0][:, t, :], t, h[0][:, t, :]).then_inc(ss2, 1)

            split_no = [0]

            def upper(n=1):
                for _ in range(n):
                    c = split_no[0]
                    if c == len(plan_2):
                        return
                    split_no[0] += 1
                    upper_of(c, 16 * (c // SLOTS2 + 1))

            def upper_of(c, landed):
                act.wait_ge(chunk2_in[c % SLOTS2], landed)
                act.activation(W2_HI[c % SLOTS2], W2[c % SLOTS2], ACT.Copy).then_inc(hi_ready, 1)

            def hT2(tag):
                if tag == "f0":
                    upper(AHEAD)
                for gi, (dst, _) in enumerate([hkT_2, hT_2] if tag == "at" else [hT_2]):
                    for t in range(TT):
                        for a in range(2):
                            b = at_mm(act, ("hT2", tag, gi, t, a)).rearrange("p (j n) -> p j n", j=4)
                            act.activation(dst[:, 4 * a:4 * a + 4, t * P:(t + 1) * P], b, ACT.Copy).then_inc(hT2_hi, 1)

            def gu(tag):
                m0, r0, n0 = gu_base[tag]
                with act.Fori(0, TURNS) as i:
                    for j in range(TURN):
                        c = n0 + j + AHEAD
                        upper_of(c, 16 * i + 16 * (c // SLOTS2 + 1))
                        b = ROT2[(r0 + j) % 4]
                        act.wait_ge(mm_done, 4 * i + (m0 + j + 1))
                        act.activation(fth[:, j, :], ps[:, b, 0:TOK], ACT.Tanh, scale=0.5).then_inc(gate_th, 1)
                split_no[0] += TURN * TURNS
                for j in range(FT - TURN * TURNS):
                    upper()
                    act.activation(fth[:, j, :], at_mm(act, ("gu", tag, j))[:, 0:TOK], ACT.Tanh, scale=0.5).then_inc(gate_th, 1)

            def dn(tag):
                upper(FT // 2)

            def cout():
                upper(4)

            def ao():
                upper(4)

            def post(tag):
                for t in range(TT):
                    for half in range(2):
                        cols = slice(half * 512, (half + 1) * 512)
                        if tag == "cv":
                            act.wait_ge(bout_y, 2 * t + half + 1)
                            src, scratch = h[1][:, t, cols], h[0][:, t, cols]
                        else:
                            src, scratch = at_mm(act, ("d", tag, t, half)), h[0][:, t, cols]
                        squares(src, 2 * t + half, scratch).then_inc(ss2, 1)

            def cin():
                act.wait_ge(conv_h, 1)
                for c in range(8):
                    upper()
                    b = at_mm(act, ("cin", c))
                    if c >= 2:
                        act.wait_ge(conv_u, c - 1)
                    act.activation(ctmp[:, c % 2, :], b[:, TOK:2 * TOK], ACT.Tanh, bias=vec2[:, 8 + c:9 + c], scale=0.5).then_inc(conv_th, 1)

            def taps():
                for n, c in enumerate(range(TAPS_DVE, 8)):
                    for j in range(TAPS):
                        k = n * TAPS + j
                        if k >= DIAGS:
                            act.wait_ge(mm_done, mm_at["tap", TAPS_DVE + (k - DIAGS) // TAPS, (k - DIAGS) % TAPS])
                        w = 16 + j * 8 + c
                        act.activation(diag[:, k % DIAGS, :], ident[:, :], ACT.Copy, scale=vec2[:, w:w + 1]).then_inc(tap_ready, 1)
                    if n:
                        tap_sum(c - 1)
                tap_sum(7)

            def tap_sum(c):
                key = ("tap", c)
                release(act.activation(uc[:, c, :], at_mm(act, key)[:, 0:TOK], ACT.Identity, bias=vec2[:, 264 + c:265 + c]), key)

            def ln():
                act.wait_ge(ln_d, 1)
                act.activation(usq, uc, ACT.Square).then_inc(ln_v, 1)
                act.wait_ge(ln_d, 2)
                for c in range(8):
                    act.activation(usq[:, c, :], uc[:, c, :], ACT.Identity, bias=vec2[:, 280 + c:281 + c], scale=vec2[:, 272 + c:273 + c]).then_inc(ln_z, 1)
                act.wait_ge(ln_z, 8)
                act.activation(uth, usq, ACT.Tanh).then_inc(ln_t, 1)

            def qkv():
                for c in range(4):
                    upper()
                    b = at_mm(act, ("k2", c)).rearrange("p (h n) -> p h n", h=2)
                    copy(kT2[:, 2 * c:2 * c + 2, :], b, ("k2", c))
                for half in range(2):
                    upper(2)
                    for t in range(TT):
                        key = ("v2", "at", t, half)
                        copy(v2[:, t, half * 512:(half + 1) * 512], at_mm(act, key), key)
                for c in range(4):
                    upper()
                    b = at_mm(act, ("q2", c)).rearrange("p (h n) -> p h n", h=2)
                    copy(qT2[:, 2 * c:2 * c + 2, :], b, ("q2", c), scale=DH ** -0.5)

            def moba():
                def exps(hh):
                    for t in range(TT):
                        c = 2 * (hh % 2) + t
                        act.wait_ge(s2_ready, 2 * hh + t + 1)
                        pp = p2[:, hh % 2, t, :]
                        act.activation(pp, pp, ACT.Exp, bias=nmax[:, c:c + 1], accum_out=rsum[:, c:c + 1]).then_inc(act_step, 1)

                exps(0)
                for hh in range(H2):
                    if hh + 1 < H2:
                        exps(hh + 1)
                    copy(pT2.rearrange("p k n -> p (k n)"), at_mm(act, ("pT2", hh)), ("pT2", hh))
                    act.activation(attT_2[0][:, hh, :], at_mm(act, ("pv2", hh))[:, 0:TOK], ACT.Copy).then_inc(att2_hi, 1)

            program = {"pre": pre, "hT2": hT2, "gu": gu, "dn": dn, "cout": cout, "ao": ao, "post": post, "cin": cin, "taps": taps, "ln": ln, "qkv": qkv, "moba": moba,
                       "start": start, "norm": norm, "hT": hT_, "zA": zA_, "kv": kv, "zF": zF, "four": four, "q": q_, "att": att,
                       "gate": gate, "gpre": gpre, "out": out_, "pq": pq, "route": route, "gather": gather, "fin": fin, "final": final}

            def run_stages(stages):
                for name, *args in stages:
                    if name in program:
                        program[name](*args)

            run_stages(ORDER + ORDER2)

        @block.vector
        def _(dve):
            own = [0]

            def v(ins):
                own[0] += 1
                ins.then_inc(dve_step, 1)
                dve.wait_ge(dve_step, own[0])

            def rsqrt(dst, src, n, width):
                var, t, y = nwt[:, 0:n], nwt[:, 2:2 + n], nwi[:, 2:2 + n].bitcast(f32)
                v(dve.tensor_scalar(var, src, 1.0 / width, EPS, ALU.mult, ALU.add))
                v(dve.tensor_single_scalar(nwi[:, 0:n], var.bitcast(i32), 1, ALU.logical_shift_right))
                v(dve.tensor_scalar(nwi[:, 2:2 + n], nwi[:, 0:n], -1.0, 1597463007.0, ALU.mult, ALU.add))
                for i in range(NEWTON):
                    v(dve.scalar_tensor_tensor(t, y, -0.5, y, ALU.mult, ALU.mult))
                    v(dve.tensor_tensor(t, t, var, ALU.mult))
                    v(dve.scalar_tensor_tensor(dst if i == NEWTON - 1 else y, t, 1.5, y, ALU.add, ALU.mult))

            def start():
                dve.wait_ge(ld_const, 16 * 6)
                v(dve.tensor_scalar(hbg[:, :, :], vecs[:, :].rearrange("p (l n) -> p l n", l=2)[:, :, 5:29], 0.5, None, ALU.mult))
                dve.wait_ge(silu_t, 1)
                v(dve.scalar_tensor_tensor(cth[:, :, :], cth[:, :, :], 1.0, cvec[:, :, :], ALU.add, ALU.mult))
                dve.tensor_scalar(cvec[:, :, :], cth[:, :, :], 0.5, None, ALU.mult).then_inc(silu_c, 1)

            def mod(l, cc):
                if cc == 0:
                    dve.wait_ge(ld_mrow, 16 * (l + 1))
                key = ("mod", l, cc)
                b = at_mm(dve, key)
                qd, a = 32 * (cc % 4), cc // 4
                m = mrows[l][qd:qd + 2, a, :]
                release(dve.tensor_tensor(m, m, b[qd:qd + 2, :], ALU.add), key)

            gains = [0]

            def norm(run, k):
                s = RUNS[run][0]
                dve.wait_ge(mark["ss"], norm_mark(run, k, 2))
                rsqrt(ss[:, 6:8], ss[:, 0:2], 2, D)
                gains[0] += 1
                dve.wait_ge(ld_gain, 16 * gains[0])
                for half in range(2):
                    cols = slice(half * 512, (half + 1) * 512)
                    key = ("bs", run, k, half)
                    b = at_mm(dve, key)
                    release(dve.scalar_tensor_tensor(amul[:, cols], b, 1.0, gain[:, cols], ALU.add, ALU.mult), key)
                for half in range(2):
                    at_evac(dve, ("bs", run, k, half))
                for t in range(TT):
                    ins = dve.scalar_tensor_tensor(h[s][:, t, :], x[s][:, t, :], ss[:, 6 + t:7 + t], amul[:, :], ALU.mult, ALU.mult)
                    if t == TT - 1:
                        ins.then_inc(gain_used, 1)
                        dve.wait_ge(gain_used, gains[0])
                    else:
                        v(ins)
                for half in range(2):
                    cols = slice(half * 512, (half + 1) * 512)
                    key = ("bh", run, k, half)
                    b = at_mm(dve, key)
                    dve.tensor_tensor(h[s][:, 0, cols], h[s][:, 0, cols], b, ALU.add).then_inc(mark["h"], 1)
                    release(dve.tensor_tensor(h[s][:, 1, cols], h[s][:, 1, cols], b, ALU.add), key)

            def rotate(src, dst, t, heads, signal):
                cs = rope[:, t, 0:16].rearrange("p (r e) -> p r e", r=2).unsqueeze(1).broadcast_to([P, heads, 2, 8])
                sn = rope[:, t, 16:32].rearrange("p (r e) -> p r e", r=2).unsqueeze(1).broadcast_to([P, heads, 2, 8])
                s5 = src.rearrange("p h (r two e) -> p h r two e", r=2, two=2)
                d5 = dst.rearrange("p h (r two e) -> p h r two e", r=2, two=2)
                t4 = [rtmp[:, n, 0:heads * 16].rearrange("p (h r e) -> p h r e", h=heads, r=2) for n in range(4)]
                dve.tensor_tensor(t4[0], s5[:, :, :, 0, :], cs, ALU.mult)
                dve.tensor_tensor(t4[1], s5[:, :, :, 1, :], sn, ALU.mult)
                dve.tensor_tensor(t4[2], s5[:, :, :, 0, :], sn, ALU.mult)
                v(dve.tensor_tensor(t4[3], s5[:, :, :, 1, :], cs, ALU.mult))
                dve.tensor_tensor(d5[:, :, :, 0, :], t4[0], t4[1], ALU.subtract)
                signal(dve.tensor_tensor(d5[:, :, :, 1, :], t4[2], t4[3], ALU.add))

            def kv(run, step):
                if step:
                    return
                s = RUNS[run][0]
                at_mark(dve, "kvss", run, 2)
                rsqrt(ss[:, 6:8], ss[:, 2:4], 2, KVLORA)
                for t in range(TT):
                    dve.tensor_scalar(ckn[:, t, :], zA[s][:, t, QLORA:QLORA + KVLORA], ss[:, 6 + t:7 + t], None, ALU.mult).then_inc(mark["ckn"], 1)
                for t in range(TT):
                    kr = zA[s][:, t, QLORA + KVLORA:WA].unsqueeze(1)
                    if s == 0:
                        rotate(kr, kr, t, 1, v)
                    kd = kfull[:, t, :].rearrange("p (h n) -> p h n", h=H)
                    dve.tensor_copy(kd[:, :, NOPE:QK], kr.broadcast_to([P, H, ROPE])).then_inc(mark["krr"], 1)

            def q_(run, step):
                s = RUNS[run][0]
                if step == 0:
                    at_mark(dve, "qss", run, 2)
                    rsqrt(ss[:, 6:8], ss[:, 4:6], 2, QLORA)
                    for t in range(TT):
                        dve.tensor_scalar(cqn[:, t, :], zA[s][:, t, 0:QLORA], ss[:, 6 + t:7 + t], None, ALU.mult).then_inc(mark["cqn"], 1)
                elif step == 2 and s == 0:
                    for t in range(TT):
                        for half in range(2):
                            at_evac(dve, ("q", run, t, half))
                        qv = q[:, t, :].rearrange("p (h n) -> p h n", h=H)[:, :, NOPE:QK]
                        rotate(qv, qv, t, H, lambda ins: ins.then_inc(mark["qr"], 1))
                        at_mark(dve, "qr", run, t + 1)

            def att(run, i):
                nk = 4 if RUNS[run][0] == 0 else 2
                if i >= H:
                    return
                for t in range(TT):
                    key = ("s", run, i, t)
                    c = 2 * (i % 2) + t
                    dve.tensor_reduce(nmax[:, c:c + 1], at_mm(dve, key)[:, 0:nk * P], axis=AX.X, op=ALU.max, negate=True).then_inc(mark["nmax"], 1)
                for t in range(TT):
                    at_evac(dve, ("s", run, i, t))
                    c = 2 * (i % 2) + t
                    v(dve.reciprocal(rinv[:, c:c + 1], rsum[:, c:c + 1]))
                    pp = pr[:, i % 2, t, 0:nk * P]
                    dve.tensor_scalar(pp, pp, rinv[:, c:c + 1], None, ALU.mult).then_inc(mark["pn"], 1)

            def gate(run, dp, part_):
                if not part_:
                    return
                for j in range(3):
                    key = ("y", run, dp, j)
                    at_evac(dve, ("g", run, dp, j))
                    b = at_mm(dve, key)
                    m = mixT[:, 2 * dp:2 * dp + 2, :].rearrange("p k n -> p (k n)")
                    release(dve.scalar_tensor_tensor(mtmp if j else m, gate_at(run, dp, j), 1.0, b, ALU.add, ALU.mult), key)
                    at_evac(dve, key)
                    if j == 1:
                        v(dve.tensor_tensor(m, m, mtmp, ALU.add))
                    elif j == 2:
                        dve.tensor_tensor(m, m, mtmp, ALU.add).then_inc(mark["mixT"], 1)

            def out_(run, half):
                s = RUNS[run][0]
                cols = slice(half * 512, (half + 1) * 512)
                at_evac(dve, ("bm", run, half))
                for t in range(TT):
                    key = ("o", run, half, t)
                    b = at_mm(dve, key)
                    release(dve.tensor_tensor(amul[:, t * 512:(t + 1) * 512], b, mb[:, cols], ALU.mult), key)
                    at_evac(dve, key)
                    dve.tensor_tensor(x[s][:, t, cols], x[s][:, t, cols], amul[:, t * 512:(t + 1) * 512], ALU.add).then_inc(mark["resid"], 1)

            def top16(val, ind, src):
                v(dve.max(val[:, 0:8], src))
                dve.max_index(ind[:, 0:8], val[:, 0:8], src)
                v(dve.match_replace(src, val[:, 0:8], src, NEG))
                v(dve.max(val[:, 8:16], src))
                v(dve.max_index(ind[:, 8:16], val[:, 8:16], src))

            def route(run, t, k):
                l = RUNS[run][1]
                if k < 8:
                    at_evac(dve, ("sc", run, k))
                    for i in (2 * k, 2 * k + 1):
                        top16(sv[:, i, :], si[:, i, :], s_sb[:, t, i * KEYS:(i + 1) * KEYS])
                    v(dve.tensor_copy(sif[:, 2 * k:2 * k + 2, :], si[:, 2 * k:2 * k + 2, :]))
                    v(dve.tensor_tensor(cand[:, k % 2, :].rearrange("p (a b) -> p a b", a=TOP), sv[:, 2 * k, :].unsqueeze(2).broadcast_to([P, TOP, TOP]),
                                        sv[:, 2 * k + 1, :].unsqueeze(1).broadcast_to([P, TOP, TOP]), ALU.add))
                    top16(ts[:, k, :], pos[:, k, :], cand[:, k % 2, :])
                    return
                half = k - 8
                hs, cols = slice(4 * half, 4 * half + 4), slice(64 * half, 64 * half + 64)
                v(dve.tensor_tensor(te[:, hs, :], ts[:, hs, :], ts[:, hs, 0:1].broadcast_to([P, 4, TOP]), ALU.subtract))
                posf = pos.rearrange("p h k -> p (h k)")[:, cols]
                v(dve.tensor_single_scalar(pa[:, cols], posf, 4, ALU.logical_shift_right))
                v(dve.tensor_copy(fa[:, cols], pa[:, cols]))
                v(dve.tensor_single_scalar(pa[:, cols], posf, TOP - 1, ALU.bitwise_and))
                dve.tensor_copy(fb[:, cols], pa[:, cols]).then_inc(mark["topd"], 1)
                at_mark(dve, "topd", run, 2 * t + half + 1)
                e3 = eq.rearrange("p (n k) -> p n k", k=TOP)
                e4 = eq.rearrange("p (h n k) -> p h n k", h=4, k=TOP)
                sf4 = sif.rearrange("p (h two) k -> p h two k", two=2)
                for which, f, i_ in ((0, fa, ia), (1, fb, ib)):
                    v(dve.tensor_tensor(e3, f[:, cols].unsqueeze(2).broadcast_to([P, 64, TOP]), iota[:, :].unsqueeze(1).broadcast_to([P, 64, TOP]), ALU.is_equal))
                    v(dve.tensor_tensor(e4, e4, sf4[:, hs, which, :].unsqueeze(2).broadcast_to([P, 4, TOP, TOP]), ALU.mult))
                    v(dve.tensor_reduce(i_[:, cols], e3, axis=AX.X, op=ALU.add))
                v(dve.scalar_tensor_tensor(ia[:, cols], ia[:, cols], float(KEYS), ib[:, cols], ALU.mult, ALU.add))
                v(dve.tensor_scalar(idx[t][:, cols], ia[:, cols], float(l * KEYS * KEYS), None, ALU.add))
                at_mark(dve, "tope", run, 2 * t + half + 1)
                v(dve.tensor_reduce(tsum[:, hs], te[:, hs, :], axis=AX.X, op=ALU.add))
                v(dve.reciprocal(tsum[:, hs], tsum[:, hs]))
                dve.tensor_tensor(gates[t][:, cols].rearrange("p (h k) -> p h k", k=TOP), te[:, hs, :],
                                  tsum[:, hs].unsqueeze(2).broadcast_to([P, 4, TOP]), ALU.mult).then_inc(mark["route"], 1)
                at_mark(dve, "route", run, 2 * t + half + 1)

            def gather(run, t, n0, n1, beside_a, beside_b):
                s = RUNS[run][0]
                G = GATHER_NO[run, t]
                if n0 == 0:
                    v(dve.memset(accv[:, :], 0.0))

                def down(g, first=False):
                    for j in range(GROUP):
                        dve.wait_ge(row_in[j], (16 * (32 * G + 1)) if first else 32 * g + 16 * (32 * G))
                        dve.tensor_tensor_reduce(out=rows[:, j, :], in0=rows[:, j, :], in1=h[s][:, t, :], scale=1.0, scalar=0.0,
                                                 op0=ALU.mult, op1=ALU.add, accum_out=a8[:, j:j + 1]).then_inc(down_done, 1)
                    base = 3 * GROUPS * G
                    dve.wait_ge(down_done, 8 * g + (P * G + GROUP))
                    dve.tensor_tensor(g1[:, :], a8[:, :], a8[:, :], ALU.mult).then_inc(gelu_step, 1)
                    dve.wait_ge(gelu_step, 3 * g + (base + 1))
                    dve.tensor_scalar(g1[:, :], g1[:, :], GELU_A, 1.0, ALU.mult, ALU.add).then_inc(gelu_step, 1)
                    dve.wait_ge(gelu_step, 3 * g + (base + 2))
                    dve.tensor_tensor(g2[:, :], g1[:, :], a8[:, :], ALU.mult).then_inc(gelu_in, 1)

                def up(g, last=False):
                    for j in range(GROUP):
                        dve.wait_ge(row_in[j], (16 * (32 * G + 32)) if last else 32 * g + (16 * (32 * G + 3)))
                        if isinstance(g, int) and g == 0 and j == 0:
                            dve.wait_ge(act_ready, GROUPS * G + 1)
                        else:
                            dve.wait_ge(upv_done, 8 * g + (P * G + j))
                        dve.scalar_tensor_tensor(accv[:, :], rows[:, j, 0:UPV], act8[:, j:j + 1], accv[:, :], ALU.mult, ALU.add).then_inc(upv_done, 1)

                def act_of(g, first=False):
                    base = 3 * GROUPS * G
                    dve.wait_ge(gelu_th, g + (GROUPS * G + 1))
                    dve.scalar_tensor_tensor(g1[:, :], th8[:, :], 1.0, a8[:, :], ALU.add, ALU.mult).then_inc(gelu_step, 1)
                    dve.wait_ge(gelu_step, 3 * g + (base + 3))
                    if not first:
                        dve.wait_ge(diag_ready, 8 * g + P * G)
                        dve.wait_ge(upv_done, 8 * g + P * G)
                    gt = gates[t][:, 0:GROUP] if first else gates[t][:, bass.ds(g * GROUP, GROUP)]
                    dve.tensor_tensor(act8[:, :], g1[:, :], gt, ALU.mult).then_inc(act_ready, 1)
                    dve.wait_ge(act_ready, g + (GROUPS * G + 1))

                def group(n, stages_a=(), stages_b=()):
                    first = is_group(n, 0)
                    down(n, first)
                    run_stages(stages_a)
                    if not first:
                        up(n - 1)
                    act_of(n, first)
                    run_stages(stages_b)

                if beside_a or beside_b:
                    group(n0, beside_a, beside_b)
                else:
                    groups(dve, n0, n1, group)
                if n1 == GROUPS:
                    up(GROUPS - 1, True)

            def fin(run, t):
                s = RUNS[run][0]
                G = GATHER_NO[run, t]
                for half in range(2):
                    at_evac(dve, ("bf", run, t, half))
                dve.wait_ge(upv_done, P * (G + 1))
                v(dve.tensor_tensor(accv[:, :], accv[:, :], mb[:, 0:UPV], ALU.mult))
                dve.wait_ge(upp_done, P * (G + 1))
                v(dve.tensor_tensor(mb[:, UPV:D], ps[:, UPB, :], mb[:, UPV:D], ALU.mult))
                v(dve.tensor_tensor(x[s][:, t, 0:UPV], x[s][:, t, 0:UPV], accv[:, :], ALU.add))
                dve.tensor_tensor(x[s][:, t, UPV:D], x[s][:, t, UPV:D], mb[:, UPV:D], ALU.add).then_inc(mark["fin"], 1)
                at_mark(dve, "fin", run, t + 1)

            def final():
                dve.wait_ge(mark["ss"], 2 * 8)
                rsqrt(ss[:, 6:8], ss[:, 0:2], 2, D)
                gains[0] += 1
                dve.wait_ge(ld_gain, 16 * gains[0])
                for t in range(TT):
                    dve.scalar_tensor_tensor(x[0][:, t, :], x[0][:, t, :], ss[:, 6 + t:7 + t], gain[:, :], ALU.mult, ALU.mult).then_inc(x2, 1)

            g2n = [0]

            def next_gain():
                n = g2n[0]
                g2n[0] += 1
                dve.wait_ge(gain2_in[n % 2], 16 * (n // 2 + 1))
                return gain2[n % 2]

            def pre(tag):
                dve.wait_ge(ss2, SS2_AT["pre", tag])
                rsqrt(ss[:, 6:8], ss[:, 0:2], 2, D)
                for dst in ([h[1], h[0]] if tag == "at" else [h[0]]):
                    g = next_gain()
                    for t in range(TT):
                        dve.scalar_tensor_tensor(dst[:, t, :], x[0][:, t, :], ss[:, 6 + t:7 + t], g[:, :], ALU.mult, ALU.mult).then_inc(h2m, 1)
                    dve.wait_ge(h2m, H2_AT[tag] - (2 if dst is h[1] else 0))
                    dve.sem_inc(gain2_used, 1)

            split_no, hT2_no = [0], [0]

            def lower(n=1):
                for _ in range(n):
                    c = split_no[0]
                    if c == len(plan_2):
                        return
                    split_no[0] += 1
                    lower_of(c, c + 1)

            def lower_of(c, upper_at):
                dve.wait_ge(hi_ready, upper_at)
                w = W2[c % SLOTS2]
                dve.tensor_tensor(W2_LO[c % SLOTS2], w, W2_HI[c % SLOTS2].bitcast(f32), ALU.subtract).then_inc(lo_ready, 1)

            def hT2(tag):
                if tag == "f0":
                    lower(AHEAD)
                for gi, (hi, lo) in enumerate([hkT_2, hT_2] if tag == "at" else [hT_2]):
                    for t in range(TT):
                        for a in range(2):
                            hT2_no[0] += 1
                            key = ("hT2", tag, gi, t, a)
                            dve.wait_ge(hT2_hi, hT2_no[0])
                            at_ = np.s_[:, 4 * a:4 * a + 4, t * P:(t + 1) * P]
                            b = at_mm(dve, key).rearrange("p (j n) -> p j n", j=4)
                            release(dve.tensor_tensor(lo[at_], b, hi[at_].bitcast(f32), ALU.subtract), key)

            def gu(tag):
                m0, r0, n0 = gu_base[tag]
                done = FT * int(tag[1])

                def tile(b, j, kt, no):
                    fixed = isinstance(kt, int)
                    g, u = ps[:, b, 0:TOK], ps[:, b, TOK:2 * TOK]
                    dst = [m[:, kt, :] if fixed else m[:, bass.ds(kt, 1), :].rearrange("p a n -> p (a n)") for m in hid_2]
                    dve.wait_ge(gate_th, no + 1)
                    dve.scalar_tensor_tensor(ft2[:, j, :], fth[:, j, :], 1.0, g, ALU.add, ALU.mult).then_inc(gu_step, 1)
                    dve.wait_ge(gu_step, 2 * no + 1)
                    dve.tensor_tensor(ft2[:, j, :], ft2[:, j, :], u, ALU.mult).then_inc(bank_free[b], 1)
                    return dst

                def parts(dst, j, no):
                    dve.tensor_copy(dst[0], ft2[:, j, :]).then_inc(gu_step, 1)
                    dve.wait_ge(gu_step, 2 * no + 2)
                    dve.tensor_tensor(dst[1], ft2[:, j, :], dst[0].bitcast(f32), ALU.subtract).then_inc(hid_ready, 1)

                with dve.Fori(0, TURNS) as i:
                    for j in range(TURN):
                        c = n0 + j + AHEAD
                        lower_of(c, 4 * i + (c + 1))
                        b = ROT2[(r0 + j) % 4]
                        dst = tile(b, j, 4 * i + j, 4 * i + (done + j))
                        dve.wait_ge(bank_free[b], i + (gu_use[tag][b] + 1))
                        parts(dst, j, 4 * i + (done + j))
                split_no[0] += TURN * TURNS
                for j in range(FT - TURN * TURNS):
                    lower()
                    key = ("gu", tag, j)
                    kt = TURN * TURNS + j
                    dst = tile(job_bank[key], j, kt, done + kt)
                    at_evac(dve, key)
                    parts(dst, j, done + kt)

            def dn(tag):
                lower(FT // 2)

            def cout():
                lower(4)

            def ao():
                lower(4)

            def qkv():
                lower(12)

            def post(tag):
                ffn = tag[0] == "f"
                if tag == "cv":
                    for t in range(TT):
                        for half in range(2):
                            cols = slice(half * 512, (half + 1) * 512)
                            key = ("d", tag, t, half)
                            dve.tensor_tensor(h[1][:, t, cols], at_mm(dve, key), bout_b[:, cols], ALU.add).then_inc(bout_y, 1)
                            dve.wait_ge(bout_y, 2 * t + half + 1)
                            dve.sem_inc(bank_free[job_bank[key]], 1)
                g = next_gain()
                for t in range(TT):
                    for half in range(2):
                        dve.wait_ge(ss2, SS2_AT["post", tag] - 3 + 2 * t + half)
                        cols = slice(half * 512, (half + 1) * 512)
                        key = ("d", tag, t, half)
                        if tag == "cv":
                            v(dve.tensor_tensor(h[1][:, t, cols], h[1][:, t, cols], g[:, cols], ALU.mult))
                        else:
                            release(dve.tensor_tensor(h[1][:, t, cols], at_mm(dve, key), g[:, cols], ALU.mult), key)
                s4 = ss[:, 0:4].rearrange("p (t a) -> p t a", t=TT)
                v(dve.tensor_tensor(nwt[:, 4:6], s4[:, :, 0], s4[:, :, 1], ALU.add))
                rsqrt(ss[:, 6:8], nwt[:, 4:6], 2, (4 if ffn else 1) * D)
                if ffn:
                    v(dve.tensor_scalar(ss[:, 6:8], ss[:, 6:8], 0.25, None, ALU.mult))
                dve.sem_inc(gain2_used, 1)
                if tag != "cv":
                    for t in range(TT):
                        for half in range(2):
                            at_evac(dve, ("d", tag, t, half))
                for t in range(TT):
                    dve.scalar_tensor_tensor(x[0][:, t, :], h[1][:, t, :], ss[:, 6 + t:7 + t], x[0][:, t, :], ALU.mult, ALU.add).then_inc(x2, 1)
                dve.wait_ge(x2, X2_AT[tag])

            def cin():
                dve.wait_ge(ld_vec2, 16 * 2)
                v(dve.memset(upad[:, :, 0:PAD], 0.0))
                dve.memset(ones, 1.0 / D).then_inc(ones_set, 1)
                v(dve.tensor_scalar(vec2[:, 8:16], vec2[:, 8:16], 0.5, None, ALU.mult))
                dve.tensor_scalar(vec2[:, 272:288], vec2[:, 272:288], 0.5, None, ALU.mult).then_inc(conv_h, 1)
                for c in range(8):
                    lower()
                    key = ("cin", c)
                    b = at_mm(dve, key)
                    tmp = rows[:, 2, 512:512 + TOK]
                    dve.wait_ge(conv_th, c + 1)
                    v(dve.tensor_scalar(tmp, b[:, 0:TOK], vec2[:, c:c + 1], 0.5, ALU.add, ALU.mult))
                    dve.scalar_tensor_tensor(upad[:, c, PAD:PAD + TOK], ctmp[:, c % 2, :], 1.0, tmp, ALU.add, ALU.mult).then_inc(conv_u, 1)
                    dve.wait_ge(conv_u, c + 1)
                    dve.sem_inc(bank_free[job_bank[key]], 1)

            def taps():
                at_ = {}
                for j in range(TAPS):
                    for c in range(TAPS_DVE):
                        w = vec2[:, 16 + j * 8 + c:17 + j * 8 + c]
                        if j:
                            dve.wait_ge(dve_step, at_[c])
                            ins = dve.scalar_tensor_tensor(uc[:, c, :], upad[:, c, j:j + TOK], w, uc[:, c, :], ALU.mult, ALU.add)
                        else:
                            ins = dve.tensor_scalar(uc[:, c, :], upad[:, c, 0:TOK], w, vec2[:, 264 + c:265 + c], ALU.mult, ALU.add)
                        if j < TAPS - 1:
                            own[0] += 1
                            at_[c] = own[0]
                            ins.then_inc(dve_step, 1)
                        else:
                            ins.then_inc(conv_y, 1)

            def ln():
                b = at_mm(dve, ("mean",))
                bc = b[:, 0:TOK].unsqueeze(1).broadcast_to([P, 8, TOK])
                dve.tensor_tensor(uc, uc, bc, ALU.subtract).then_inc(ln_d, 1)
                dve.wait_ge(ln_d, 1)
                dve.sem_inc(bank_free[job_bank["mean",]], 1)
                b = at_mm(dve, ("var",))
                v(dve.tensor_scalar(rl2, b[:, 0:TOK], LN_EPS, None, ALU.add))
                dve.sem_inc(bank_free[job_bank["var",]], 1)
                y = rli.bitcast(f32)
                v(dve.tensor_single_scalar(rli2, rl2.bitcast(i32), 1, ALU.logical_shift_right))
                v(dve.tensor_scalar(rli, rli2, -1.0, 1597463007.0, ALU.mult, ALU.add))
                for i in range(NEWTON):
                    v(dve.scalar_tensor_tensor(rln, y, -0.5, y, ALU.mult, ALU.mult))
                    v(dve.tensor_tensor(rln, rln, rl2, ALU.mult))
                    v(dve.scalar_tensor_tensor(y, rln, 1.5, y, ALU.add, ALU.mult))
                dve.wait_ge(ln_v, 1)
                dve.tensor_tensor(uc, uc, y.unsqueeze(1).broadcast_to([P, 8, TOK]), ALU.mult).then_inc(ln_d, 1)
                dve.wait_ge(ln_t, 1)
                v(dve.scalar_tensor_tensor(uth, uth, 1.0, usq, ALU.add, ALU.mult))
                v(dve.tensor_copy(conv_2[0], uth))
                dve.tensor_tensor(conv_2[1], uth, conv_2[0].bitcast(f32), ALU.subtract).then_inc(ln_s, 1)

            def moba():
                dve.wait_ge(ld_vec2, 16 * 3)

                def biased(hh):
                    for t in range(TT):
                        c = 2 * (hh % 2) + t
                        b = at_mm(dve, ("s2", hh))
                        if hh >= 2:
                            dve.wait_ge(mm_done, mm_at["pT2", hh - 2])
                        pp = p2[:, hh % 2, t, :]
                        v(dve.scalar_tensor_tensor(pp, dist[:, t, :], -(2.0 ** -(hh + 1)), b[:, t * TOK:(t + 1) * TOK], ALU.mult, ALU.add))
                        if t:
                            dve.sem_inc(bank_free[job_bank["s2", hh]], 1)
                        dve.tensor_reduce(nmax[:, c:c + 1], pp, axis=AX.X, op=ALU.max, negate=True).then_inc(s2_ready, 1)

                def lower_out(hh):
                    key = ("pv2", hh)
                    dve.wait_ge(att2_hi, hh + 1)
                    release(dve.tensor_tensor(attT_2[1][:, hh, :], at_mm(dve, key)[:, 0:TOK], attT_2[0][:, hh, :].bitcast(f32), ALU.subtract), key)

                biased(0)
                for hh in range(H2):
                    if hh + 1 < H2:
                        biased(hh + 1)
                    for t in range(TT):
                        c = 2 * (hh % 2) + t
                        dve.wait_ge(act_step, 2 * hh + t + 1)
                        v(dve.reciprocal(rinv[:, c:c + 1], rsum[:, c:c + 1]))
                        pp = p2[:, hh % 2, t, :]
                        dve.tensor_scalar(pp, pp, rinv[:, c:c + 1], None, ALU.mult).then_inc(p2_ready, 1)
                    if hh:
                        lower_out(hh - 1)
                lower_out(H2 - 1)

            program = {"pre": pre, "hT2": hT2, "gu": gu, "dn": dn, "cout": cout, "qkv": qkv, "ao": ao, "post": post, "cin": cin, "taps": taps, "ln": ln, "moba": moba,
                       "start": start, "mod": mod, "norm": norm, "kv": kv, "q": q_, "att": att, "gate": gate, "out": out_, "route": route,
                       "gather": gather, "fin": fin, "final": final}

            def run_stages(stages):
                for name, *args in stages:
                    if name in program:
                        program[name](*args)

            run_stages(ORDER + ORDER2)

        @block.sync
        def _(sp):
            for dst, src in ((cvec[:, :, :], A["cvec"]), (ident[:, :], A["ident"]), (sel[:, :, :], A["sel"]), (rope[:, :, :], A["rope"]),
                             (iota[:, :], A["iota"]), (vecs[:, :], A["vecs"])):
                sp.dma_start(dst, src).then_inc(ld_const, 16)
            sp.dma_start(x[1][:, :, :], A["ctx"].rearrange("(t p) d -> p t d", p=P)).then_inc(ld_c, 16)
            sp.dma_start(mrows[0][:, :, :], A["bmod"][0]).then_inc(ld_mrow, 16)
            gains, n = [0], [0]

            def chunks(k):
                for _ in range(k):
                    c = n[0]
                    n[0] += 1
                    if c >= SLOTS:
                        sp.wait_ge(mm_done, chunk_done[c - SLOTS])
                    name, at_, width = plan[c]
                    sp.dma_start(wring[:, c % SLOTS, 0:width], A[name][at_] if at_ else A[name]).then_inc(chunk_in[c % SLOTS], 16)

            def load_gain(vec):
                if gains[0]:
                    sp.wait_ge(gain_used, gains[0])
                gains[0] += 1
                sp.dma_start(gain[:, :], vec.unsqueeze(0).broadcast_to([P, D])).then_inc(ld_gain, 16)

            def per_stage(name, *args):
                if name == "gate":
                    return 1 if args[0] == "x1" else 2
                if name in ("kv", "q"):
                    return int(args[1] == 2)
                if name == "four":
                    return 2 - args[1]
                if name == "pq":
                    return 2 if args[1] < 4 else 0
                return {"mod": 2, "zA": 2, "zF": 2, "gpre": 1, "out": 2}.get(name, 0)

            for name, *args in STAGES:
                if name == "mod" and args == [1, 0]:
                    sp.dma_start(mrows[1][:, :, :], A["bmod"][1]).then_inc(ld_mrow, 16)
                if name == "norm":
                    load_gain(A["norm2_g" if args[1] else "norm1_g"][RUNS[args[0]][1]])
                elif name == "final":
                    load_gain(A["final_g"])
                elif name == "pq" and args[1] == 0:
                    if args[0] != "x0":
                        sp.wait_ge(mm_done, mm_at["sc", {"c0": "x0", "x1": "c0"}[args[0]], 7])
                    chunks(2)
                    sp.wait_ge(gain_used, gains[0])
                    sp.dma_start(keysT[:, :], A["keysT"][RUNS[args[0]][1]]).then_inc(ld_keys, 16)
                else:
                    chunks(per_stage(name, *args))
                if name == "mod" and args == [0, 3]:
                    sp.dma_start(x[0][:, :, :], A["x"].rearrange("(t p) d -> p t d", p=P)).then_inc(ld_x, 16)

            n2, g2n, stage_at = [0], [0], 0

            def slot2_free(c):
                if c >= SLOTS2:
                    sp.wait_ge(mm_done, chunk2_done[c - SLOTS2])
                elif c < SLOTS:
                    last = max(m for m in range(len(plan)) if m % SLOTS == c)
                    sp.wait_ge(mm_done, chunk_done[last])
                else:
                    sp.wait_ge(x2, 2)

            def chunks2_to(target):
                while n2[0] < min(target, len(plan_2)):
                    c = n2[0]
                    n2[0] += 1
                    slot2_free(c)
                    name, at_ = plan_2[c]
                    sp.dma_start(W2[c % SLOTS2], A[name][at_]).then_inc(chunk2_in[c % SLOTS2], 16)

            def load_gain2(vec):
                n = g2n[0]
                g2n[0] += 1
                if n >= 2:
                    sp.wait_ge(gain2_used, n - 1)
                else:
                    sp.wait_ge(x2, 2)
                sp.dma_start(gain2[n % 2][:, :], vec.unsqueeze(0).broadcast_to([P, D])).then_inc(gain2_in[n % 2], 16)

            for name, *args in ORDER2:
                if name == "pre":
                    tag = args[0]
                    if tag[0] == "f":
                        load_gain2(A["ffn_pre"][int(tag[1])])
                        load_gain2(A["ffn_post"][int(tag[1])])
                    elif tag == "cv":
                        sp.wait_ge(x2, X2_AT["f0"])
                        load_gain2(A["mix_pre"][0])
                        load_gain2(A["mix_post"][0])
                        sp.dma_start(vec2, A["vec2"]).then_inc(ld_vec2, 16)
                        sp.dma_start(bout_b, A["b_out"].unsqueeze(0).broadcast_to([P, D])).then_inc(ld_vec2, 16)
                    else:
                        load_gain2(A["kv_norm"])
                        load_gain2(A["mix_pre"][1])
                        sp.dma_start(dist, A["dist"]).then_inc(ld_vec2, 16)
                elif name == "gu":
                    chunks2_to(stage_at + TURN)
                    n0 = n2[0]
                    f = plan_2[n0][1][0]
                    done0 = [chunk2_done[n0 + c - SLOTS2] for c in range(4)]
                    with sp.Fori(0, TURNS - 1) as i:
                        for c in range(4):
                            sp.wait_ge(mm_done, 4 * i + done0[c])
                            sp.dma_start(W2[(n0 + c) % SLOTS2], A["wgu"][f, bass.ds(4 * i + (4 + c), 1)].rearrange("a p n -> p (a n)")).then_inc(chunk2_in[(n0 + c) % SLOTS2], 16)
                    n2[0] += 4 * (TURNS - 1)
                    stage_at += FT
                    chunks2_to(stage_at + AHEAD)
                elif name == "post" and args[0] == "at":
                    load_gain2(A["mix_post"][1])
                elif name == "store":
                    sp.wait_ge(x2, X2_AT["f3"])
                    sp.dma_start(out.rearrange("(t p) d -> p t d", p=P), x[0][:, :, :]).then_inc(out_done, 16)
                    sp.wait_ge(out_done, 16)
                else:
                    stage_at += {"dn": FT // 2, "cin": 8, "cout": 4, "qkv": 12, "ao": 4}.get(name, 0)
                    chunks2_to(stage_at + AHEAD)

        @block.gpsimd
        def _(pool):
            copies = [0]

            def gather(run, t):
                G = GATHER_NO[run, t]
                at_mark(pool, "route", run, 2 * t + 1)
                def fetch(table, offs, j):
                    pool.sem_inc(slot_ok, 1)
                    pool.indirect_dma_start(out=rows[:, j, :], out_offset=None, in_=table,
                                            in_offset=bass.IndirectOffsetOnAxis(ap=offs[:, j:j + 1], axis=0)).then_inc(row_in[j], 16)

                def down(g, par, first=None):
                    src = idx[t][:, 0:GROUP] if first == 0 else idx[t][:, bass.ds(g * GROUP, GROUP)]
                    pool.tensor_copy(idown[par][:, :], src).then_inc(idx_copied, 1)
                    pool.wait_ge(idx_copied, 2 * g + (2 * GROUPS * G + (1 if first == 0 else 0)))
                    for j in range(GROUP):
                        if first == 0 and G:
                            pool.wait_ge(upv_done, P * G - GROUP + j + 1)
                            pool.wait_ge(upp_done, P * G - GROUP + j + 1)
                        elif first == 1:
                            pool.wait_ge(down_done, P * G + j + 1)
                        elif first is None:
                            pool.wait_ge(upv_done, 8 * g + (P * G - 2 * GROUP + j + 1))
                            pool.wait_ge(upp_done, 8 * g + (P * G - 2 * GROUP + j + 1))
                        fetch(A["peer_down"], idown[par], j)

                def up(g, par, last=False):
                    pool.tensor_copy(iup[par][:, :], idx[t][:, bass.ds(g * GROUP, GROUP)]).then_inc(idx_copied, 1)
                    pool.wait_ge(idx_copied, 2 * g + (2 * GROUPS * G + (2 if last else 3)))
                    for j in range(GROUP):
                        if last:
                            pool.wait_ge(upv_done, 8 * g + (P * G - GROUP + j + 1))
                            pool.wait_ge(upp_done, 8 * g + (P * G - GROUP + j + 1))
                        else:
                            pool.wait_ge(down_done, 8 * g + (P * G + GROUP + j + 1))
                        fetch(A["peer_up"], iup[par], j)

                down(0, 0, 0)
                down(1, 1, 1)
                up(0, 0)
                for m0 in range(2):
                    if m0:
                        at_mark(pool, "route", run, 2 * t + 2)
                    with pool.Fori((1, GROUPS // 4)[m0], (GROUPS // 4, GROUPS // 2)[m0]) as m:
                        down(m * 2, 0)
                        up(m * 2 - 1, 1)
                        down(m * 2 + 1, 1)
                        up(m * 2, 0)
                up(GROUPS - 1, 1, True)

            for run, t in GATHERS:
                gather(run, t)


def tiles(w, k0, nk, c0, nc):
    return w[k0 * P:(k0 + nk) * P, c0:c0 + nc].reshape(nk, P, nc).transpose(1, 0, 2).reshape(P, nk * nc)


def column_chunks(w, nk, nc):
    return np.stack([np.stack([tiles(w, k0, nk, c0, nc) for k0 in range(0, w.shape[0] // P, nk)]) for c0 in range(0, w.shape[1], nc)])


def beside(w):
    n = w.shape[1] // (2 * P)
    return w.reshape(KT, P, 2, n, P).transpose(3, 1, 0, 2, 4).reshape(n, P, SLOT_W)


def constants():
    n = np.arange(TOK)
    ang = 2 * np.pi * ((n[:, None] * n[None, :]) % TOK) / TOK
    dft = np.concatenate([np.cos(ang), np.sin(ang), -np.sin(ang)], 1).astype(np.float32) / np.float32(16)
    pool = np.zeros((4, TOK, TOK), np.float32)
    for g, w in enumerate((2, 4, 8, 16)):
        lo, hi = np.clip(n - w // 2, 0, TOK), np.clip(n - w // 2 + w, 0, TOK)
        for t in range(TOK):
            pool[g, lo[t]:hi[t], t] = np.float32(1) / np.float32(hi[t] - lo[t])
            pool[g, t, t] -= 1
    half = ROPE // 2
    inv = (np.float32(10000.0) ** (-np.arange(0, half, 2, dtype=np.float32) / half)).astype(np.float32)
    ar, ac = ((n // 64).astype(np.float32)[:, None] * inv), ((n % 64).astype(np.float32)[:, None] * inv)
    rope = np.concatenate([np.cos(ar), np.cos(ac), np.sin(ar), np.sin(ac)], 1).astype(np.float32)
    sel = np.zeros((P, 2, P), np.float32)
    for qd in range(4):
        for s in range(2):
            sel[32 * qd + s, s] = 1
    return {
        "dft": tiles(dft, 0, 2, 0, 768), "poolm": pool.reshape(4, 2, P, TOK).transpose(2, 1, 0, 3).reshape(P, -1),
        "rope": rope.reshape(TT, P, 32).transpose(1, 0, 2), "sel": sel, "ident": np.eye(P, dtype=np.float32),
        "dist": np.where(n[:, None] >= n[None, :], n[:, None] - n[None, :], 1e33).astype(np.float32).reshape(TT, P, TOK).transpose(1, 0, 2),
        "iota": np.tile(np.arange(TOP, dtype=np.float32), (P, 1)),
    }


def layout(i):
    cols = lambda v: v.reshape(-1, P).T
    bmod = np.zeros((2, P, 3, 512), np.float32)
    for l in range(2):
        for cc in range(12):
            for s in range(2):
                bmod[l, 32 * (cc % 4) + s, cc // 4] = i["b_mod"][l, cc * 512:(cc + 1) * 512]
    wgrp = np.zeros((2, P, 2, P), np.float32)
    for l in range(2):
        for g in range(4):
            po = 64 * (g % 2)
            wgrp[l, po:po + 64, g // 2, po:po + 64] = i["w_grp"][l, g]
    vecs = [np.concatenate([cols(i["kv_norm_g"][l]), cols(i["q_norm_g"][l]), cols(i["pool_scale"][l]), cols(i["b_gate"][l])], 1) for l in range(2)]
    w_in = i["w_in"]
    a = {
        "x": i["x"][0], "ctx": i["ctx"][0],
        "cvec": np.stack([cols(i["c"][0]), cols(i["c_ctx"])], 2),
        "bmod": bmod, "vecs": np.concatenate(vecs, 1), "norm1_g": i["norm1_g"], "norm2_g": i["norm2_g"], "final_g": i["final_g"],
        "wmod": np.stack([column_chunks(i["w_mod"][l], 4, 512).reshape(24, P, SLOT_W) for l in range(2)]),
        "wA": np.stack([column_chunks(w_in[l][:, 0:WA], 4, WA)[0] for l in range(2)]),
        "wZ": np.stack([column_chunks(w_in[l][:, WA:WA + WZ], 4, WZ)[0] for l in range(2)]),
        "wG": np.stack([column_chunks(w_in[l][:, WA + WZ:], 8, 256).reshape(3, 4, P, SLOT_W).transpose(1, 0, 2, 3) for l in range(2)]),
        "wO": np.stack([column_chunks(np.concatenate([i["w_oa"][l], i["w_ob"][l], i["w_oc"][l]], 0), 8, 256)[:, 0] for l in range(2)]),
        "wuq": np.stack([tiles(i["w_uq"][l], 0, 2, 0, 768) for l in range(2)]), "wukv": i["w_ukv"], "wgrp": wgrp.reshape(2, P, 256),
        "wout": np.stack([column_chunks(i["w_out"][l], 4, 512).reshape(4, P, SLOT_W) for l in range(2)]),
        "wpq": np.stack([column_chunks(i["w_pq"][l], 8, 256)[:, 0] for l in range(2)]),
        "keysT": i["peer_keys"].transpose(0, 4, 1, 2, 3).reshape(2, P, HP * KEYS),
        "peer_down": i["peer_down"].reshape(-1, D), "peer_up": i["peer_up"].reshape(-1, D),
    }
    v2 = [cols(i[n][0]) for n in ("conv_b_in_2",)] + [i["conv_w_dw_2"][0].reshape(TAPS, 8, P).transpose(2, 0, 1).reshape(P, TAPS * 8)]
    v2 += [cols(i[n][0]) for n in ("conv_b_dw_2", "conv_ln_g_2", "conv_ln_b_2")]
    a.update({
        "wgu": np.stack([beside(w) for w in i["ffn_w_gate_up_2"].reshape(4, D, 2 * FF)]),
        "wdn": np.stack([np.stack([tiles(w, 2 * c, 2, 0, D) for c in range(FT // 2)]) for w in i["ffn_w_down_2"].reshape(4, FF, D)]),
        "ffn_pre": i["ffn_norm_pre_2"].reshape(4, D), "ffn_post": i["ffn_norm_post_2"].reshape(4, D),
        "mix_pre": i["mix_norm_pre_2"], "mix_post": i["mix_norm_post_2"], "kv_norm": i["kv_norm_2"], "b_out": i["conv_b_out_2"][0],
        "vec2": np.concatenate(v2, 1),
        "cwin": beside(i["conv_w_in_2"][0]),
        "cwout": column_chunks(i["conv_w_out_2"][0], 4, 512).reshape(4, P, SLOT_W),
        "w2k": column_chunks(i["w_kv_2"][:, 0:D], 8, 256)[:, 0], "w2v": column_chunks(i["w_kv_2"][:, D:], 4, 512).reshape(4, P, SLOT_W),
        "w2q": column_chunks(i["attn_w_q_2"][0], 8, 256)[:, 0], "w2o": column_chunks(i["attn_w_o_2"][0], 4, 512).reshape(4, P, SLOT_W),
    })
    a.update(constants())
    return {k: np.ascontiguousarray(v, dtype=np.float32) for k, v in a.items()}


def kernel(**inputs):
    import concourse.bacc as bacc
    from concourse.bass_utils import run_bass_kernel_spmd

    nc = bacc.Bacc("TRN2", target_bir_lowering=False, num_devices=1)
    arrays = {f"in_{name}": a for name, a in layout({k: np.asarray(v) for k, v in inputs.items()}).items()}
    A = {name[3:]: nc.dram_tensor(name, a.shape, mybir.dt.from_np(a.dtype), kind="ExternalInput").ap() for name, a in arrays.items()}
    out = nc.dram_tensor("out_0", (TOK, D), mybir.dt.float32, kind="ExternalOutput").ap()
    build(nc, A, out)
    result = run_bass_kernel_spmd(nc, [arrays], core_ids=[0])
    return result.results[0]["out_0"].reshape(1, TOK, D)
```
